# Optimizing a Trainium2 kernel written in Bass

```python
import jax, jax.numpy as jnp
from jax import lax
import numpy as np

D_MODEL = 1024
BATCH = 1
SEQ = 256
DEPTH = 2

N_EVEN = (DEPTH + 1) // 2
N_ODD = DEPTH // 2
EPS = 1e-6
CHUNK = 128
A_WIDTH = D_MODEL // 2
A_HEADS = 8
A_HEAD_DIM = A_WIDTH // A_HEADS
B_WIDTH = D_MODEL // 2
POOL_WINDOWS = (2, 4, 8, 16)
B_GROUPS = len(POOL_WINDOWS)
B_GROUP_DIM = B_WIDTH // B_GROUPS
IN_E = 2 * A_WIDTH + B_WIDTH
MIX_E = A_WIDTH + B_WIDTH
C_WIDTH = D_MODEL
CONV_K = 31
D_FF_DENSE = 2816
N_EXPERTS = 8
TOP_K = 2
D_FF_EXPERT = 3584

kernel_name = "hybrid_gmlp_pool_conformer_moe_trunk"

def rmsnorm(x, g):
    xf = x.astype(jnp.float32)
    y = xf * lax.rsqrt(jnp.mean(xf * xf, axis=-1, keepdims=True) + EPS)
    return (y * g.astype(jnp.float32)).astype(x.dtype)

def layernorm(x, g, b):
    xf = x.astype(jnp.float32)
    mu = jnp.mean(xf, axis=-1, keepdims=True)
    xc = xf - mu
    var = jnp.mean(xc * xc, axis=-1, keepdims=True)
    y = xc * lax.rsqrt(var + EPS) * g.astype(jnp.float32) + b.astype(jnp.float32)
    return y.astype(x.dtype)

def swiglu(h, w_gate, w_up, w_down):
    return (jax.nn.silu(h @ w_gate) * (h @ w_up)) @ w_down

def chunked_sgu(u, v, g_v, w_s, b_s):
    bsz, s, _ = v.shape
    v = rmsnorm(v, g_v)
    vc = v.reshape(bsz, s // CHUNK, CHUNK, A_HEADS, A_HEAD_DIM)
    w = jnp.tril(w_s)
    mixed = jnp.einsum('hts,bnshd->bnthd', w, vc) + b_s.T[None, None, :, :, None]
    return u * mixed.reshape(bsz, s, A_WIDTH)

def pool_mixer(z, w_pool, scale):
    bsz, s, _ = z.shape
    zg = z.astype(jnp.float32).reshape(bsz, s, B_GROUPS, B_GROUP_DIM)
    cs = jnp.cumsum(zg, axis=1)
    pos = jnp.arange(1, s + 1, dtype=jnp.float32)
    means = []
    for g, win in enumerate(POOL_WINDOWS):
        csg = cs[:, :, g]
        lag = jnp.pad(csg, ((0, 0), (win, 0), (0, 0)))[:, :s]
        cnt = jnp.minimum(pos, jnp.float32(win))
        means.append((csg - lag) / cnt[None, :, None])
    mixed = (jnp.stack(means, axis=2) - zg).astype(z.dtype)
    y = jnp.einsum('bsgc,gcd->bsgd', mixed, w_pool).reshape(bsz, s, B_WIDTH)
    return y * scale

def conformer_conv(h, w_pw1, b_pw1, w_dw, b_dw, ln_g, ln_b, w_pw2, b_pw2):
    a = h @ w_pw1 + b_pw1
    val, gate = jnp.split(a, 2, axis=-1)
    x = val * jax.nn.sigmoid(gate)
    x = lax.conv_general_dilated(
        x, w_dw[:, None, :].astype(x.dtype), window_strides=(1,),
        padding=[(CONV_K - 1, 0)], dimension_numbers=('NWC', 'WIO', 'NWC'),
        feature_group_count=C_WIDTH) + b_dw
    x = jax.nn.silu(layernorm(x, ln_g, ln_b))
    return x @ w_pw2 + b_pw2

def moe_swiglu(h, w_router, w_gate, w_up, w_down):
    bsz, s, d = h.shape
    hf = h.reshape(bsz * s, d)
    logits = (hf @ w_router).astype(jnp.float32)
    top_v, top_i = lax.top_k(logits, TOP_K)
    gates = jax.nn.softmax(top_v, axis=-1)
    comb = jnp.sum(jax.nn.one_hot(top_i, N_EXPERTS, dtype=jnp.float32) * gates[..., None], axis=1)
    comb = comb.astype(h.dtype)
    y = jnp.zeros_like(hf)
    for e in range(N_EXPERTS):
        y = y + comb[:, e:e + 1] * swiglu(hf, w_gate[e], w_up[e], w_down[e])
    return y.reshape(bsz, s, d)

def setup_inputs(seed: int = 0) -> dict:
    key = jax.random.key(seed)
    ks = iter(jax.random.split(key, 40))
    f32 = jnp.float32

    def nrm(shape, fan_in):
        return jax.random.normal(next(ks), shape, f32) * (fan_in ** -0.5)

    def gain(shape):
        return 1.0 + 0.05 * jax.random.normal(next(ks), shape, f32)

    def bias(shape):
        return 0.02 * jax.random.normal(next(ks), shape, f32)

    tri = jnp.tril(jnp.ones((CHUNK, CHUNK), f32))
    return {
        "x": jax.random.normal(next(ks), (BATCH, SEQ, D_MODEL), f32),
        "norm_mix_e": gain((N_EVEN, D_MODEL)),
        "w_in_e": nrm((N_EVEN, D_MODEL, IN_E), D_MODEL),
        "sgu_norm": gain((N_EVEN, A_WIDTH)),
        "w_spatial": nrm((N_EVEN, A_HEADS, CHUNK, CHUNK), CHUNK) * tri,
        "b_spatial": gain((N_EVEN, A_HEADS, CHUNK)),
        "w_pool": nrm((N_EVEN, B_GROUPS, B_GROUP_DIM, B_GROUP_DIM), B_GROUP_DIM),
        "pool_scale": gain((N_EVEN, B_WIDTH)),
        "w_out_e": nrm((N_EVEN, MIX_E, D_MODEL), MIX_E),
        "norm_ffn_e": gain((N_EVEN, D_MODEL)),
        "w_gate_d": nrm((N_EVEN, D_MODEL, D_FF_DENSE), D_MODEL),
        "w_up_d": nrm((N_EVEN, D_MODEL, D_FF_DENSE), D_MODEL),
        "w_down_d": nrm((N_EVEN, D_FF_DENSE, D_MODEL), D_FF_DENSE),
        "norm_mix_o": gain((N_ODD, D_MODEL)),
        "w_pw1": nrm((N_ODD, D_MODEL, 2 * C_WIDTH), D_MODEL),
        "b_pw1": bias((N_ODD, 2 * C_WIDTH)),
        "w_dw": nrm((N_ODD, CONV_K, C_WIDTH), CONV_K),
        "b_dw": bias((N_ODD, C_WIDTH)),
        "ln_g": gain((N_ODD, C_WIDTH)),
        "ln_b": bias((N_ODD, C_WIDTH)),
        "w_pw2": nrm((N_ODD, C_WIDTH, D_MODEL), C_WIDTH),
        "b_pw2": bias((N_ODD, D_MODEL)),
        "norm_ffn_o": gain((N_ODD, D_MODEL)),
        "w_router": nrm((N_ODD, D_MODEL, N_EXPERTS), D_MODEL),
        "w_gate_x": nrm((N_ODD, N_EXPERTS, D_MODEL, D_FF_EXPERT), D_MODEL),
        "w_up_x": nrm((N_ODD, N_EXPERTS, D_MODEL, D_FF_EXPERT), D_MODEL),
        "w_down_x": nrm((N_ODD, N_EXPERTS, D_FF_EXPERT, D_MODEL), D_FF_EXPERT),
        "norm_final": gain((D_MODEL,)),
    }

def reference(x, norm_mix_e, w_in_e, sgu_norm, w_spatial, b_spatial, w_pool, pool_scale,
              w_out_e, norm_ffn_e, w_gate_d, w_up_d, w_down_d,
              norm_mix_o, w_pw1, b_pw1, w_dw, b_dw, ln_g, ln_b, w_pw2, b_pw2,
              norm_ffn_o, w_router, w_gate_x, w_up_x, w_down_x, norm_final):
    h = x
    for layer in range(DEPTH):
        i = layer // 2
        if layer % 2 == 0:
            hn = rmsnorm(h, norm_mix_e[i])
            proj = hn @ w_in_e[i]
            uv = jax.nn.gelu(proj[..., :2 * A_WIDTH])
            u, v = uv[..., :A_WIDTH], uv[..., A_WIDTH:]
            z = proj[..., 2 * A_WIDTH:]
            a_out = chunked_sgu(u, v, sgu_norm[i], w_spatial[i], b_spatial[i])
            b_out = pool_mixer(z, w_pool[i], pool_scale[i])
            h = h + jnp.concatenate([a_out, b_out], axis=-1) @ w_out_e[i]
            h = h + swiglu(rmsnorm(h, norm_ffn_e[i]), w_gate_d[i], w_up_d[i], w_down_d[i])
        else:
            hn = rmsnorm(h, norm_mix_o[i])
            h = h + conformer_conv(hn, w_pw1[i], b_pw1[i], w_dw[i], b_dw[i],
                                   ln_g[i], ln_b[i], w_pw2[i], b_pw2[i])
            h = h + moe_swiglu(rmsnorm(h, norm_ffn_o[i]), w_router[i],
                               w_gate_x[i], w_up_x[i], w_down_x[i])
    return rmsnorm(h, norm_final)


_drawn_inputs = setup_inputs


def setup_inputs(seed=0):
    import zlib

    import numpy as np

    out = dict(_drawn_inputs(seed))
    spreads = {}
    factors = {'sgu_norm': 2.767, 'ln_b': 4.752, 'b_pw2': 4.061}
    for name, (base, spread) in spreads.items():
        noise = np.random.default_rng([zlib.crc32(name.encode()), seed]).standard_normal(out[name].shape)
        drawn = base * np.exp(spread * noise) if base else spread * noise
        out[name] = __import__('jax').numpy.asarray(drawn.astype(out[name].dtype))
    for name, factor in factors.items():
        out[name] = (out[name] * factor).astype(out[name].dtype)
    return out
```

```python
from contextlib import ExitStack

import numpy as np

import concourse.bass as bass
from concourse import mybir

ALU = mybir.AluOpType
ACT = mybir.ActivationFunctionType
AX = mybir.AxisListType
F32 = mybir.dt.float32
F32R = mybir.dt.float32r
I32 = mybir.dt.int32

P = 128
SEQ = 256
D = 1024
TT = SEQ // P
KT = D // P
HEADS = 8
HEAD_DIM = 64
WINDOWS = (2, 4, 8, 16)
GROUPS = len(WINDOWS)
CONV_K = 31
F_DENSE = 2816
F_EXPERT = 3584
EXPERTS = 8
EPS = 1e-6

UNIT = 2048
BLK = 512
RING = 6
RAW_EARLY = 3

U_IN = 0
U_OUT = U_IN + 6
U_FFN = U_OUT + 4
FFN_BLOCKS = 6
U_PW1 = U_FFN + 33
U_PW2 = U_PW1 + 8
TRUNK_UNITS = U_PW2 + 4
STEPS = F_EXPERT // BLK
ITEM_UNITS = 6 * STEPS
MAX_ITEMS = 12

C_NORM_MIX_E, C_NORM_FFN_E, C_NORM_MIX_O = 0, 8, 16
C_POOL_SCALE, C_B_DW, C_LN_G, C_LN_B = 24, 28, 36, 44
C_B_PW1, C_B_SPATIAL, C_W_DW, C_ROUTER = 52, 68, 76, 76 + 8 * CONV_K
C_ALL = C_ROUTER + KT * EXPERTS
K_IDENT, K_BEFORE, K_IOTA, K_TIE, K_EXPERT = 0, 128, 256, 384, 448
K_ALL = 456


def build(nc, x, trunk, experts, channel, consts, bands, w_spatial, w_pool, sgu_norm, b_pw2,
          norm_ffn_o, norm_final, out):
    ctx = ExitStack()
    with ctx:
        def sb(name, shape, dt=F32):
            return ctx.enter_context(nc.sbuf_tensor(name, shape, dt))

        def sem(name):
            return ctx.enter_context(nc.semaphore(name))

        raw = sb("raw", [P, RING * UNIT + 256])
        w_hi = sb("w_hi", [P, RING, UNIT], F32R)
        w_lo = sb("w_lo", [P, RING, UNIT], F32R)
        xT_hi = sb("xT_hi", [P, KT * SEQ], F32R)
        xT_lo = sb("xT_lo", [P, KT * SEQ], F32R)
        hT_hi = sb("hT_hi", [P, TT, BLK], F32R)
        hT_lo = sb("hT_lo", [P, TT, BLK], F32R)
        xn_hi = sb("xn_hi", [P, TT, D], F32R)
        xn_lo = sb("xn_lo", [P, TT, D], F32R)
        pick = sb("pick", [P, TT, P], F32R)
        pickT = sb("pickT", [P, SEQ], F32R)
        gate_parts = sb("gate_parts", [P, MAX_ITEMS, TT, 2], F32R)
        router_hi = sb("router_hi", [P, KT * EXPERTS], F32R)
        router_lo = sb("router_lo", [P, KT * EXPERTS], F32R)
        h = sb("h", [P, TT, D])
        gated = sb("gated", [P, TT, BLK])
        act_tmp = sb("act_tmp", [P, TT, BLK])
        par = sb("par", [P, C_ALL])
        con = sb("con", [P, K_ALL])
        ones = sb("ones", [P, P])
        sums = sb("sums", [P, 8, TT])
        pos_item = sb("pos_item", [P, MAX_ITEMS, TT])
        gate_col = sb("gate_col", [P, 1])
        item_tab = sb("item_tab", [1, MAX_ITEMS + 4], I32)

        bank = [ctx.enter_context(nc.psum_tensor(f"bank{i}", [P, BLK], F32)) for i in range(8)]

        arena = raw[:, RAW_EARLY * UNIT:]
        scaled = arena[:, 0:TT * D].rearrange("p (t d) -> p t d", t=TT)
        u_sb = arena[:, 0:1024].rearrange("p (t d) -> p t d", t=TT)
        v_sb = arena[:, 1024:2048].rearrange("p (t d) -> p t d", t=TT)
        z_sb = arena[:, 2048:3072].rearrange("p (t d) -> p t d", t=TT)
        band_sb = arena[:, 3072:4608].rearrange("p (g s) -> p g s", g=GROUPS)
        wsp_sb = arena[:, 4608:5632].rearrange("p (h s) -> p h s", h=HEADS)
        wpool_sb = arena[:, 5632:6144].rearrange("p (g s) -> p g s", g=GROUPS)
        sig = arena[:, 0:1024].rearrange("p (c s) -> p c s", c=4)
        squares = arena[:, 0:2048].rearrange("p (c s) -> p c s", c=KT)
        xc = arena[:, 2048:2048 + KT * (SEQ + CONV_K - 1)].rearrange("p (c s) -> p c s", c=KT)
        yc = arena[:, 4336:4336 + KT * SEQ].rearrange("p (c s) -> p c s", c=KT)
        mean_sb = arena[:, 2048:2048 + SEQ]
        rstd_sb = arena[:, 2304:2304 + SEQ]
        mixedT = gated[:, :, :].rearrange("p t s -> p (t s)").rearrange("p (g s) -> p g s", g=GROUPS)
        act_flat = act_tmp[:, :, :].rearrange("p t s -> p (t s)")
        gv_sb = act_tmp[:, 0, :]
        route = act_tmp[:, 1, 0:128].rearrange("p (q t e) -> p q t e", q=8, t=TT)
        logits = act_tmp[:, 1, 128:144].rearrange("p (t e) -> p t e", t=TT)
        item_f = act_tmp[:, 1, 144:144 + MAX_ITEMS + 4]
        gate_item = act_tmp[:, 1, 160:160 + MAX_ITEMS * TT].rearrange("p (i t) -> p i t", t=TT)
        ident = con[:, K_IDENT:K_IDENT + P]
        before = con[:, K_BEFORE:K_BEFORE + P]
        iota = con[:, K_IOTA:K_IOTA + P]
        tie = con[:, K_TIE:K_TIE + 64].rearrange("p (e j) -> p e j", e=EXPERTS)
        expert_no = con[:, K_EXPERT:K_EXPERT + EXPERTS]
        xT_hi_k = xT_hi[:, :].rearrange("p (k s) -> p k s", k=KT)
        xT_lo_k = xT_lo[:, :].rearrange("p (k s) -> p k s", k=KT)
        xg_hi = xT_hi[:, 0:KT * P].rearrange("p (k s) -> p k s", k=KT)
        xg_lo = xT_lo[:, 0:KT * P].rearrange("p (k s) -> p k s", k=KT)
        y_hi = xT_hi[:, KT * P:]
        y_lo = xT_lo[:, KT * P:]

        x_in, par_in, con_in = sem("x_in"), sem("par_in"), sem("con_in")
        band_in, wsp_in, wpool_in, gv_in = sem("band_in"), sem("wsp_in"), sem("wpool_in"), sem("gv_in")
        b_pw2_in, g_ffn_in, g_final_in = sem("b_pw2_in"), sem("g_ffn_in"), sem("g_final_in")
        out_written = sem("out_written")
        landed = [sem(f"landed{s}") for s in range(RING)]
        hi_split, lo_split, w_used = sem("hi_split"), sem("lo_split"), sem("w_used")
        ones_set, masked = sem("ones_set"), sem("masked")
        norm_sq = [sem(f"norm_sq{s}") for s in range(5)]
        norm_ms = [sem(f"norm_ms{s}") for s in range(5)]
        norm_root = [sem(f"norm_root{s}") for s in range(5)]
        norm_scaled = [sem(f"norm_scaled{s}") for s in range(4)]
        turned = [sem(f"turned{s}") for s in range(4)]
        xT_hi_set = [sem(f"xT_hi_set{s}") for s in range(4)]
        xT_lo_set = [sem(f"xT_lo_set{s}") for s in range(4)]
        dve_step = sem("dve_step")
        gelu_done, v_sq, v_ms, v_root, v_normed = (sem(n) for n in ("gelu_done", "v_sq", "v_ms", "v_root", "v_normed"))
        z_copied, pooled, pool_copied, pool_mapped = (sem(n) for n in ("z_copied", "pooled", "pool_copied", "pool_mapped"))
        mixed, a_gated, a_turned = sem("mixed"), sem("a_gated"), sem("a_turned")
        cat_hi, cat_lo, h_mixed = sem("cat_hi"), sem("cat_lo"), sem("h_mixed")
        ffn_first = sem("ffn_first")
        ffn_silu = [sem("ffn_silu0"), sem("ffn_silu1")]
        ffn_gated = [sem("ffn_gated0"), sem("ffn_gated1")]
        ffn_turned = [sem("ffn_turned0"), sem("ffn_turned1")]
        ffn_hi = [sem("ffn_hi0"), sem("ffn_hi1")]
        ffn_lo = [sem("ffn_lo0"), sem("ffn_lo1")]
        h_ffn = sem("h_ffn")
        val_copied, gatec_copied, vg_turned = sem("val_copied"), sem("gatec_copied"), sem("vg_turned")
        sig_done, glu_done, conv_step = sem("sig_done"), sem("glu_done"), sem("conv_step")
        sum_done, centred, sq_done, var_set, var_root = (sem(n) for n in ("sum_done", "centred", "sq_done", "var_set", "var_root"))
        ln_scaled, swish_done, cv_hi, cv_lo, h_conv = (sem(n) for n in ("ln_scaled", "swish_done", "cv_hi", "cv_lo", "h_conv"))
        xn_hi_set, xn_lo_set, router_hi_set, router_lo_set = (sem(n) for n in ("xn_hi_set", "xn_lo_set", "router_hi_set", "router_lo_set"))
        logits_done, centred_logits, exp_done, chosen, counted = (sem(n) for n in ("logits_done", "centred_logits", "exp_done", "chosen", "counted"))
        gates_f, gates_hi, tab_ready = sem("gates_f"), sem("gates_hi"), sem("tab_ready")
        pick_ready, gathered, xg_hi_set, xg_lo_set = (sem(n) for n in ("pick_ready", "gathered", "xg_hi_set", "xg_lo_set"))
        silu_done, gated_done, ht_turned, ht_hi, ht_lo = (sem(n) for n in ("silu_done", "gated_done", "ht_turned", "ht_hi", "ht_lo"))
        slots_turned, pickT_set, gate_col_set = sem("slots_turned"), sem("pickT_set"), sem("gate_col_set")
        y_hi_set, y_lo_set, scattered, h_added = (sem(n) for n in ("y_hi_set", "y_lo_set", "scattered", "h_added"))
        out_ready = sem("out_ready")

        raw_slot = {u: u % RAW_EARLY for u in range(TRUNK_UNITS)}
        trunk_in_slot = [sum(1 for u in raw_slot if raw_slot[u] == s) for s in range(RING)]
        last_trunk_in_slot = [max(u for u in raw_slot if raw_slot[u] == s) for s in range(RAW_EARLY)]

        def raw_at(s):
            return raw[:, s * UNIT:(s + 1) * UNIT]

        def ring_slot(u):
            return u % RING

        def item_base(i):
            return i * ITEM_UNITS + TRUNK_UNITS

        def step_unit(n):
            return 4 + 6 * (n - 1)

        def wait(e, s, value):
            if not isinstance(value, int) or value > 0:
                e.wait_ge(s, value)

        block = ctx.enter_context(nc.Block())

        @block.sync
        def _(sp):
            sp.dma_start(h[:, :, :], x.rearrange("(t p) d -> p t d", p=P)).then_inc(x_in, 16)
            sp.dma_start(con[:, :], consts).then_inc(con_in, 16)
            sp.dma_start(par[:, :], channel).then_inc(par_in, 16)
            for u in range(TRUNK_UNITS):
                wait(sp, lo_split, u - RAW_EARLY + 1)
                sp.dma_start(raw_at(raw_slot[u]), trunk[u, :, :]).then_inc(landed[raw_slot[u]], 16)
            for j in range(RING):
                if j < RAW_EARLY:
                    sp.wait_ge(lo_split, last_trunk_in_slot[j] + 1)
                if j == RAW_EARLY:
                    sp.wait_ge(turned[3], 4)
                    sp.wait_ge(xn_lo_set, 2)
                sp.dma_start(raw_at(j), experts[j, :, :]).then_inc(landed[j], 16)
            with sp.Fori(1, STEPS) as r:
                for j in range(RING):
                    sp.wait_ge(lo_split, r * RING + (TRUNK_UNITS + j - RING + 1))
                    sp.dma_start(raw_at(j), experts[r * RING + j, :, :]).then_inc(landed[j], 16)
            sp.wait_ge(tab_ready, 1)
            n_items = sp.value_load(item_tab[0:1, MAX_ITEMS:MAX_ITEMS + 1], min_val=EXPERTS, max_val=MAX_ITEMS - 1)
            with sp.Fori(1, n_items) as i:
                e = sp.value_load(item_tab[0:1, bass.ds(i, 1)], min_val=0, max_val=EXPERTS - 1)
                with sp.Fori(0, STEPS) as r:
                    for j in range(RING):
                        sp.wait_ge(lo_split, item_base(i) + r * RING + (j - RING + 1))
                        sp.dma_start(raw_at(j), experts[e * ITEM_UNITS + r * RING + j, :, :]).then_inc(landed[j], 16)
            sp.wait_ge(lo_split, item_base(n_items))
            sp.dma_start(raw_at(0)[:, 0:D], norm_final.partition_broadcast(P)).then_inc(g_final_in, 16)
            for t in range(TT):
                sp.wait_ge(out_ready, t + 1)
                sp.dma_start(out[t * P:(t + 1) * P, :], raw_at(1 + t)[:, 0:D]).then_inc(out_written, 16)
            sp.wait_ge(out_written, 16 * TT)

        @block.gpsimd
        def _(pool):
            pool.memset(ones[:, :], 1.0).then_inc(ones_set, 1)
            pool.wait_ge(wsp_in, 16)
            pool.affine_select(out=wsp_sb, in_=wsp_sb, compare_op=ALU.is_ge, fill=0.0, base=0,
                               pattern=[[0, HEADS], [1, P]], channel_multiplier=-1).then_inc(masked, 1)

        @block.scalar
        def _(act):
            act.dma_start(wsp_sb, w_spatial).then_inc(wsp_in, 16)
            act.dma_start(band_sb, bands).then_inc(band_in, 16)
            act.dma_start(wpool_sb, w_pool).then_inc(wpool_in, 16)
            act.dma_start(gv_sb, sgu_norm.partition_broadcast(P)).then_inc(gv_in, 16)
            done = [0]

            def split_unit(u):
                act.wait_ge(landed[raw_slot[u]], 16 * (u // RAW_EARLY + 1))
                wait(act, w_used, u - RING + 1)
                act.activation(w_hi[:, ring_slot(u), :], raw_at(raw_slot[u]), ACT.Copy).then_inc(hi_split, 1)

            def split_item(i, units):
                for m in units:
                    act.wait_ge(landed[m % RING], i * (16 * STEPS) + 16 * (trunk_in_slot[m % RING] + m // RING + 1))
                    act.wait_ge(w_used, item_base(i) + (m - RING + 1))
                    act.activation(w_hi[:, ring_slot(TRUNK_UNITS + m), :], raw_at(m % RING), ACT.Copy).then_inc(hi_split, 1)

            def splits(until):
                for u in range(done[0], until):
                    if u < TRUNK_UNITS:
                        split_unit(u)
                    else:
                        split_item(0, [u - TRUNK_UNITS])
                done[0] = max(done[0], until)

            def norm_front(s):
                for t in range(TT):
                    act.activation(scaled[:, t, :], h[:, t, :], ACT.Square, accum_out=sums[:, 0, t:t + 1]).then_inc(norm_sq[s], 1)
                act.wait_ge(norm_ms[s], 1)
                act.activation(sums[:, 2, :], sums[:, 1, :], ACT.Sqrt).then_inc(norm_root[s], 1)

            def norm_back(s, col):
                for b in range(4):
                    act.wait_ge(turned[s], b + 1)
                    for k in (2 * b, 2 * b + 1):
                        last = act.activation(xT_hi_k[:, k, :], bank[b][:, (k % 2) * SEQ:(k % 2 + 1) * SEQ], ACT.Copy,
                                              scale=par[:, col + k:col + k + 1])
                    last.then_inc(xT_hi_set[s], 1)

            act.wait_ge(x_in, 16)
            norm_front(0)
            splits(2)
            act.wait_ge(par_in, 16)
            norm_back(0, C_NORM_MIX_E)
            splits(6)
            act.wait_ge(w_used, 2)
            for t in range(TT):
                act.activation(u_sb[:, t, :], bank[4 + t][:, :], ACT.Gelu_apprx_tanh).then_inc(gelu_done, 1)
            splits(8)
            act.wait_ge(w_used, 4)
            for t in range(TT):
                act.activation(v_sb[:, t, :], bank[6 + t][:, :], ACT.Gelu_apprx_tanh).then_inc(gelu_done, 1)
            for t in range(TT):
                act.wait_ge(gelu_done, 3 + t)
                act.activation(gated[:, t, :], v_sb[:, t, :], ACT.Square, accum_out=sums[:, 3, t:t + 1]).then_inc(v_sq, 1)
            act.wait_ge(v_ms, 1)
            act.activation(sums[:, 5, :], sums[:, 4, :], ACT.Sqrt).then_inc(v_root, 1)
            splits(10)
            act.wait_ge(w_used, 6)
            for t in range(TT):
                act.activation(z_sb[:, t, :], bank[t][:, :], ACT.Copy).then_inc(z_copied, 1)
            act.wait_ge(v_sq, 2)
            for b in range(2):
                act.wait_ge(pooled, b + 1)
                act.activation(mixedT[:, 2 * b:2 * b + 2, :], bank[4 + b][:, :].rearrange("p (g s) -> p g s", g=2),
                               ACT.Copy).then_inc(pool_copied, 1)
            for b in range(2):
                act.wait_ge(pool_mapped, b + 1)
                for g in (2 * b, 2 * b + 1):
                    last = act.activation(xT_hi_k[:, 4 + g, :], bank[6 + b][:, (g % 2) * SEQ:(g % 2 + 1) * SEQ], ACT.Copy,
                                          scale=par[:, C_POOL_SCALE + g:C_POOL_SCALE + g + 1])
                last.then_inc(cat_hi, 1)
            for b in range(2):
                act.wait_ge(a_turned, b + 1)
                act.activation(xT_hi[:, b * BLK:(b + 1) * BLK], bank[b][:, :], ACT.Copy).then_inc(cat_hi, 1)
            splits(12)
            splits(14)
            act.wait_ge(h_mixed, 4)
            norm_front(1)
            splits(16)
            norm_back(1, C_NORM_FFN_E)
            for n in range(FFN_BLOCKS + 1):
                nf = BLK if n < FFN_BLOCKS - 1 else BLK // 2
                base = U_FFN + 6 * n
                if n < FFN_BLOCKS:
                    act.wait_ge(ffn_first, 2 * n + 1)
                    wait(act, ffn_gated[0], n)
                    act.activation(act_tmp[:, 0, 0:nf], bank[0][:, 0:nf], ACT.Silu).then_inc(ffn_silu[0], 1)
                if n >= 1:
                    pf = BLK if n - 1 < FFN_BLOCKS - 1 else BLK // 2
                    act.wait_ge(ffn_turned[1], n)
                    act.activation(hT_hi[:, 1, 0:pf], bank[1][:, 0:pf], ACT.Copy).then_inc(ffn_hi[1], 1)
                if n == FFN_BLOCKS:
                    break
                small = n == FFN_BLOCKS - 1
                splits(base + RING)
                g_end = base + (1 if small else 2)
                act.wait_ge(w_used, g_end)
                wait(act, ffn_gated[1], n)
                act.activation(act_tmp[:, 1, 0:nf], bank[1][:, 0:nf], ACT.Silu).then_inc(ffn_silu[1], 1)
                act.wait_ge(ffn_turned[0], n + 1)
                act.activation(hT_hi[:, 0, 0:nf], bank[0][:, 0:nf], ACT.Copy).then_inc(ffn_hi[0], 1)
                splits(g_end + RING)
                splits(base + (2 if small else 4) + RING)
            act.wait_ge(h_ffn, 4)
            norm_front(2)
            splits(U_PW1 + RING)
            norm_back(2, C_NORM_MIX_O)
            for j in range(2):
                u0 = U_PW1 + 4 * j
                act.wait_ge(w_used, u0 + 4)
                wait(act, vg_turned, 4 * j)
                for t in range(TT):
                    act.activation(act_tmp[:, t, :], bank[6 + t][:, :], ACT.Copy).then_inc(gatec_copied, 1)
                for c in range(4 * j, 4 * j + 4):
                    act.wait_ge(vg_turned, c + 1)
                    wait(act, glu_done, c - 3)
                    act.activation(sig[:, c % 4, :], bank[c % 4][:, SEQ:2 * SEQ], ACT.Sigmoid,
                                   bias=par[:, C_B_PW1 + 8 + c:C_B_PW1 + 9 + c]).then_inc(sig_done, 1)
                splits(u0 + 4 + RING)
            act.dma_start(act_tmp[0:1, :, :].rearrange("p t s -> p (t s)"), b_pw2).then_inc(b_pw2_in, 16)
            for q in range(2):
                act.wait_ge(centred, 1)
                act.activation(squares[:, 4 * q:4 * q + 4, :], yc[:, 4 * q:4 * q + 4, :], ACT.Square).then_inc(sq_done, 1)
            act.wait_ge(var_set, 1)
            act.activation(rstd_sb, rstd_sb, ACT.Sqrt).then_inc(var_root, 1)
            for c in range(KT):
                act.wait_ge(ln_scaled, c // 4 + 1)
                act.activation(yc[:, c, :], yc[:, c, :], ACT.Silu, bias=par[:, C_LN_B + c:C_LN_B + c + 1],
                               scale=par[:, C_LN_G + c:C_LN_G + c + 1]).then_inc(swish_done, 1)
            for c in range(0, KT, 2):
                act.wait_ge(swish_done, c + 2)
                act.activation(xT_hi_k[:, c:c + 2, :], yc[:, c:c + 2, :], ACT.Copy).then_inc(cv_hi, 1)
            splits(TRUNK_UNITS + 2)
            act.wait_ge(w_used, TRUNK_UNITS)
            act.dma_start(act_flat, norm_ffn_o.partition_broadcast(P)).then_inc(g_ffn_in, 16)
            act.activation(router_hi[:, :], par[:, C_ROUTER:C_ROUTER + KT * EXPERTS], ACT.Copy).then_inc(router_hi_set, 1)
            act.wait_ge(h_conv, 4)
            norm_front(3)
            for t in range(TT):
                act.wait_ge(norm_scaled[3], t + 1)
                act.activation(xn_hi[:, t, :], scaled[:, t, :], ACT.Copy).then_inc(xn_hi_set, 1)
            for b in range(4):
                act.wait_ge(turned[3], b + 1)
                act.activation(xT_hi[:, b * BLK:(b + 1) * BLK], bank[b][:, :], ACT.Copy).then_inc(xT_hi_set[3], 1)
            splits(TRUNK_UNITS + 3)
            act.wait_ge(centred_logits, 1)
            act.activation(route[:, 2, :, :], route[:, 1, :, :], ACT.Exp).then_inc(exp_done, 1)
            act.wait_ge(gates_f, 1)
            act.activation(gate_parts[:, :, :, 0], gate_item[:, :, :], ACT.Copy).then_inc(gates_hi, 1)
            splits(TRUNK_UNITS + RING)

            def turned_hi(i, n):
                act.wait_ge(ht_turned, i * STEPS + (n + 1))
                act.activation(hT_hi[:, 0, :], bank[2][:, :], ACT.Copy).then_inc(ht_hi, 1)

            def silu(i, n, unit_end):
                act.wait_ge(w_used, item_base(i) + unit_end)
                wait(act, gated_done, i * STEPS + n)
                act.activation(act_tmp[:, 0, :], bank[0][:, :], ACT.Silu).then_inc(silu_done, 1)

            def tail(i):
                turned_hi(i, STEPS - 1)
                act.wait_ge(w_used, item_base(i + 1))
                act.wait_ge(gate_col_set, i + 1)
                for c in range(2):
                    act.activation(y_hi[:, c * BLK:(c + 1) * BLK], bank[3 + c][:, :], ACT.Copy,
                                   scale=gate_col[:, 0:1]).then_inc(y_hi_set, 1)

            def item(i, first):
                if not first:
                    split_item(i, range(0, 4))
                for b in range(2):
                    act.wait_ge(gathered, 2 * i + (b + 1))
                    act.activation(xT_hi[:, b * BLK:(b + 1) * BLK], bank[5 + b][:, :], ACT.Copy).then_inc(xg_hi_set, 1)
                if not first:
                    tail(i - 1)
                    split_item(i, range(4, 6))
                silu(i, 0, 2)
                split_item(i, range(6, 10))
                silu(i, 1, step_unit(1) + 2)
                turned_hi(i, 0)
                split_item(i, range(10, 16))
                act.wait_ge(slots_turned, i + 1)
                act.activation(pickT[:, :], bank[5][:, P:P + SEQ], ACT.Copy).then_inc(pickT_set, 1)
                with act.Fori(2, STEPS - 1) as n:
                    act.wait_ge(w_used, item_base(i) + n * 6)
                    act.wait_ge(gated_done, i * STEPS + n)
                    act.activation(act_tmp[:, 0, :], bank[0][:, :], ACT.Silu).then_inc(silu_done, 1)
                    act.wait_ge(ht_turned, i * STEPS + n)
                    act.activation(hT_hi[:, 0, :], bank[2][:, :], ACT.Copy).then_inc(ht_hi, 1)
                    for j in range(RING):
                        m = 10 - 6 + j
                        s = m % RING
                        act.wait_ge(landed[s], i * (16 * STEPS) + n * 16 + 16 * (trunk_in_slot[s] + m // RING + 1))
                        act.wait_ge(w_used, item_base(i) + n * 6 + (m - RING + 1))
                        act.activation(w_hi[:, ring_slot(TRUNK_UNITS + m), :], raw_at(s), ACT.Copy).then_inc(hi_split, 1)
                silu(i, STEPS - 1, step_unit(STEPS - 1) + 2)
                turned_hi(i, STEPS - 2)
                split_item(i, range(ITEM_UNITS - 2, ITEM_UNITS))

            act.wait_ge(tab_ready, 1)
            n_items = act.value_load(item_tab[0:1, MAX_ITEMS:MAX_ITEMS + 1], min_val=EXPERTS, max_val=MAX_ITEMS - 1)
            last_item = act.value_load(item_tab[0:1, MAX_ITEMS + 1:MAX_ITEMS + 2], min_val=EXPERTS - 1, max_val=MAX_ITEMS - 2)
            item(0, True)
            with act.Fori(1, n_items) as i:
                item(i, False)
            tail(last_item)
            act.wait_ge(h_added, n_items * 4)
            for t in range(TT):
                act.activation(raw_at(1 + t)[:, 0:D], h[:, t, :], ACT.Square, accum_out=sums[:, 0, t:t + 1]).then_inc(norm_sq[4], 1)
            act.wait_ge(norm_ms[4], 1)
            act.activation(sums[:, 2, :], sums[:, 1, :], ACT.Sqrt).then_inc(norm_root[4], 1)

        @block.vector
        def _(dve):
            done = [0]
            steps = [0]

            def link(ins):
                steps[0] += 1
                ins.then_inc(dve_step, 1)
                dve.wait_ge(dve_step, steps[0])

            def split_unit(u):
                dve.wait_ge(hi_split, u + 1)
                s = ring_slot(u)
                dve.tensor_tensor(w_lo[:, s, :], raw_at(raw_slot[u]), w_hi[:, s, :].bitcast(F32), ALU.subtract).then_inc(lo_split, 1)

            def split_item(i, units):
                for m in units:
                    s = ring_slot(TRUNK_UNITS + m)
                    dve.wait_ge(hi_split, item_base(i) + (m + 1))
                    dve.tensor_tensor(w_lo[:, s, :], raw_at(m % RING), w_hi[:, s, :].bitcast(F32), ALU.subtract).then_inc(lo_split, 1)

            def splits(until):
                for u in range(done[0], until):
                    if u < TRUNK_UNITS:
                        split_unit(u)
                    else:
                        split_item(0, [u - TRUNK_UNITS])
                done[0] = max(done[0], until)

            def norm_rstd(s):
                dve.wait_ge(norm_sq[s], TT)
                dve.tensor_scalar(sums[:, 1, :], sums[:, 0, :], 1.0 / D, EPS, ALU.mult, ALU.add).then_inc(norm_ms[s], 1)
                dve.wait_ge(norm_root[s], 1)
                link(dve.reciprocal(sums[:, 6, :], sums[:, 2, :]))

            def norm_front(s):
                norm_rstd(s)
                for t in range(TT):
                    dve.tensor_scalar(scaled[:, t, :], h[:, t, :], sums[:, 6, t:t + 1], None, ALU.mult).then_inc(norm_scaled[s], 1)

            def norm_back(s, col):
                for b in range(4):
                    dve.wait_ge(xT_hi_set[s], b + 1)
                    for k in (2 * b, 2 * b + 1):
                        last = dve.scalar_tensor_tensor(out=xT_lo_k[:, k, :], in0=bank[b][:, (k % 2) * SEQ:(k % 2 + 1) * SEQ],
                                                        scalar=par[:, col + k:col + k + 1], in1=xT_hi_k[:, k, :].bitcast(F32),
                                                        op0=ALU.mult, op1=ALU.subtract)
                    last.then_inc(xT_lo_set[s], 1)

            dve.wait_ge(x_in, 16)
            norm_front(0)
            splits(2)
            dve.wait_ge(par_in, 16)
            norm_back(0, C_NORM_MIX_E)
            splits(6)
            splits(8)
            dve.wait_ge(v_sq, TT)
            dve.tensor_scalar(sums[:, 4, :], sums[:, 3, :], 1.0 / BLK, EPS, ALU.mult, ALU.add).then_inc(v_ms, 1)
            dve.wait_ge(v_root, 1)
            link(dve.reciprocal(sums[:, 7, :], sums[:, 5, :]))
            dve.wait_ge(gv_in, 16)
            for t in range(TT):
                dve.scalar_tensor_tensor(out=v_sb[:, t, :], in0=v_sb[:, t, :], scalar=sums[:, 7, t:t + 1], in1=gv_sb,
                                         op0=ALU.mult, op1=ALU.mult).then_inc(v_normed, 1)
            splits(10)
            for t in range(TT):
                dve.wait_ge(mixed, t + 1)
                for hd in range(HEADS):
                    cols = slice(hd * HEAD_DIM, (hd + 1) * HEAD_DIM)
                    last = dve.scalar_tensor_tensor(out=u_sb[:, t, cols], in0=bank[2 + t][:, cols],
                                                    scalar=par[:, C_B_SPATIAL + hd:C_B_SPATIAL + hd + 1], in1=u_sb[:, t, cols],
                                                    op0=ALU.add, op1=ALU.mult)
                last.then_inc(a_gated, 1)
            for b in range(2):
                dve.wait_ge(cat_hi, b + 1)
                for g in (2 * b, 2 * b + 1):
                    last = dve.scalar_tensor_tensor(out=xT_lo_k[:, 4 + g, :], in0=bank[6 + b][:, (g % 2) * SEQ:(g % 2 + 1) * SEQ],
                                                    scalar=par[:, C_POOL_SCALE + g:C_POOL_SCALE + g + 1],
                                                    in1=xT_hi_k[:, 4 + g, :].bitcast(F32), op0=ALU.mult, op1=ALU.subtract)
                last.then_inc(cat_lo, 1)
            for b in range(2):
                dve.wait_ge(cat_hi, 2 + b + 1)
                dve.tensor_tensor(xT_lo[:, b * BLK:(b + 1) * BLK], bank[b][:, :], xT_hi[:, b * BLK:(b + 1) * BLK].bitcast(F32),
                                  ALU.subtract).then_inc(cat_lo, 1)
            splits(12)

            def add_to_h(c, t, b, s):
                dve.tensor_tensor(h[:, t, c * BLK:(c + 1) * BLK], bank[b][:, :], h[:, t, c * BLK:(c + 1) * BLK],
                                  ALU.add).then_inc(s, 1)

            for c in range(2):
                dve.wait_ge(w_used, U_OUT + 2 * c + 2)
                for t in range(TT):
                    add_to_h(c, t, 2 + 2 * c + t, h_mixed)
                if c == 0:
                    splits(14)
            dve.wait_ge(h_mixed, 4)
            norm_front(1)
            splits(16)
            norm_back(1, C_NORM_FFN_E)
            for n in range(FFN_BLOCKS + 1):
                nf = BLK if n < FFN_BLOCKS - 1 else BLK // 2
                base = U_FFN + 6 * n
                if n >= 1:
                    pf = BLK if n - 1 < FFN_BLOCKS - 1 else BLK // 2
                    dve.wait_ge(ffn_hi[1], n)
                    dve.tensor_tensor(hT_lo[:, 1, 0:pf], bank[1][:, 0:pf], hT_hi[:, 1, 0:pf].bitcast(F32), ALU.subtract).then_inc(ffn_lo[1], 1)
                if n == FFN_BLOCKS:
                    break
                small = n == FFN_BLOCKS - 1
                dve.wait_ge(ffn_first, 2 * n + 2)
                dve.wait_ge(ffn_silu[0], n + 1)
                dve.tensor_tensor(gated[:, 0, 0:nf], bank[2][:, 0:nf], act_tmp[:, 0, 0:nf], ALU.mult).then_inc(ffn_gated[0], 1)
                splits(base + RING)
                dve.wait_ge(ffn_hi[0], n + 1)
                dve.tensor_tensor(hT_lo[:, 0, 0:nf], bank[0][:, 0:nf], hT_hi[:, 0, 0:nf].bitcast(F32), ALU.subtract).then_inc(ffn_lo[0], 1)
                splits(base + (1 if small else 2) + RING)
                u_end = base + (2 if small else 4)
                dve.wait_ge(w_used, u_end)
                dve.wait_ge(ffn_silu[1], n + 1)
                dve.tensor_tensor(gated[:, 1, 0:nf], bank[3][:, 0:nf], act_tmp[:, 1, 0:nf], ALU.mult).then_inc(ffn_gated[1], 1)
                splits(u_end + RING)
            dve.wait_ge(w_used, U_PW1)
            dve.wait_ge(h_mixed, 4)
            for t in range(TT):
                for c in range(2):
                    add_to_h(c, t, 4 + 2 * t + c, h_ffn)
            dve.wait_ge(h_ffn, 4)
            norm_front(2)
            dve.memset(xc[:, :, 0:CONV_K - 1], 0.0).then_inc(dve_step, 1)
            steps[0] += 1
            splits(U_PW1 + RING)
            norm_back(2, C_NORM_MIX_O)
            taps = [0]

            def conv(c0):
                for k in range(CONV_K):
                    for c in range(c0, c0 + 4):
                        w = par[:, C_W_DW + c * CONV_K + k:C_W_DW + c * CONV_K + k + 1]
                        if k == 0:
                            ins = dve.tensor_scalar(yc[:, c, :], xc[:, c, 0:SEQ], w, par[:, C_B_DW + c:C_B_DW + c + 1],
                                                    ALU.mult, ALU.add)
                        else:
                            dve.wait_ge(conv_step, taps[0] - 3)
                            ins = dve.scalar_tensor_tensor(out=yc[:, c, :], in0=xc[:, c, k:k + SEQ], scalar=w,
                                                           in1=yc[:, c, :], op0=ALU.mult, op1=ALU.add)
                        ins.then_inc(conv_step, 1)
                        taps[0] += 1

            for j in range(2):
                u0 = U_PW1 + 4 * j
                dve.wait_ge(w_used, u0 + 2)
                wait(dve, vg_turned, 4 * j)
                for t in range(TT):
                    dve.tensor_copy(gated[:, t, :], bank[4 + t][:, :]).then_inc(val_copied, 1)
                for c in range(4 * j, 4 * j + 4):
                    dve.wait_ge(sig_done, c + 1)
                    dve.scalar_tensor_tensor(out=xc[:, c, CONV_K - 1:CONV_K - 1 + SEQ], in0=bank[c % 4][:, 0:SEQ],
                                             scalar=par[:, C_B_PW1 + c:C_B_PW1 + c + 1], in1=sig[:, c % 4, :],
                                             op0=ALU.add, op1=ALU.mult).then_inc(glu_done, 1)
                splits(u0 + 4 + RING)
                dve.wait_ge(glu_done, 4 * j + 4)
                conv(4 * j)
            dve.wait_ge(sum_done, 1)
            link(dve.tensor_scalar(mean_sb, bank[4][:, 0:SEQ], 1.0 / D, None, ALU.mult))
            dve.wait_ge(conv_step, 2 * 4 * CONV_K)
            dve.tensor_tensor(yc, yc, mean_sb.unsqueeze(1).broadcast_to([P, KT, SEQ]), ALU.subtract).then_inc(centred, 1)
            dve.wait_ge(sum_done, 2)
            dve.tensor_scalar(rstd_sb, bank[5][:, 0:SEQ], 1.0 / D, EPS, ALU.mult, ALU.add).then_inc(var_set, 1)
            dve.wait_ge(var_root, 1)
            link(dve.reciprocal(mean_sb, rstd_sb))
            dve.wait_ge(centred, 1)
            for q in range(2):
                dve.tensor_tensor(yc[:, 4 * q:4 * q + 4, :], yc[:, 4 * q:4 * q + 4, :],
                                  mean_sb.unsqueeze(1).broadcast_to([P, 4, SEQ]), ALU.mult).then_inc(ln_scaled, 1)
            for c in range(0, KT, 2):
                dve.wait_ge(cv_hi, c // 2 + 1)
                dve.tensor_tensor(xT_lo_k[:, c:c + 2, :], yc[:, c:c + 2, :], xT_hi_k[:, c:c + 2, :].bitcast(F32),
                                  ALU.subtract).then_inc(cv_lo, 1)
            splits(TRUNK_UNITS + 2)
            dve.wait_ge(router_hi_set, 1)
            dve.tensor_tensor(router_lo[:, :], par[:, C_ROUTER:C_ROUTER + KT * EXPERTS], router_hi[:, :].bitcast(F32),
                              ALU.subtract).then_inc(router_lo_set, 1)
            dve.wait_ge(h_ffn, 4)
            for c in range(2):
                dve.wait_ge(w_used, U_PW2 + 2 * c + 2)
                for t in range(TT):
                    add_to_h(c, t, 4 + 2 * c + t, h_conv)
            dve.wait_ge(h_conv, 4)
            norm_rstd(3)
            dve.wait_ge(g_ffn_in, 16)
            for t in range(TT):
                dve.scalar_tensor_tensor(out=scaled[:, t, :], in0=h[:, t, :], scalar=sums[:, 6, t:t + 1], in1=act_flat,
                                         op0=ALU.mult, op1=ALU.mult).then_inc(norm_scaled[3], 1)
            for b in range(4):
                dve.wait_ge(xT_hi_set[3], b + 1)
                dve.tensor_tensor(xT_lo[:, b * BLK:(b + 1) * BLK], bank[b][:, :], xT_hi[:, b * BLK:(b + 1) * BLK].bitcast(F32),
                                  ALU.subtract).then_inc(xT_lo_set[3], 1)
            for t in range(TT):
                dve.wait_ge(xn_hi_set, t + 1)
                dve.tensor_tensor(xn_lo[:, t, :], scaled[:, t, :], xn_hi[:, t, :].bitcast(F32), ALU.subtract).then_inc(xn_lo_set, 1)
            splits(TRUNK_UNITS + 3)
            dve.wait_ge(logits_done, 1)
            dve.wait_ge(con_in, 16)
            link(dve.tensor_copy(logits[:, :, :], bank[4][:, 0:TT * EXPERTS].rearrange("p (t e) -> p t e", t=TT)))
            scratch = act_flat[:, 0:256].rearrange("p (q t e j) -> p q t e j", q=2, t=TT, e=EXPERTS)
            for t in range(TT):
                other = logits[:, t, :].unsqueeze(1).broadcast_to([P, EXPERTS, EXPERTS])
                own = logits[:, t, :].unsqueeze(2).broadcast_to([P, EXPERTS, EXPERTS])
                dve.tensor_tensor(scratch[:, 0, t, :, :], other, own, ALU.is_gt)
                link(dve.tensor_tensor(scratch[:, 1, t, :, :], other, own, ALU.is_equal))
                link(dve.tensor_tensor(scratch[:, 1, t, :, :], scratch[:, 1, t, :, :], tie, ALU.mult))
                link(dve.tensor_tensor(scratch[:, 0, t, :, :], scratch[:, 0, t, :, :], scratch[:, 1, t, :, :], ALU.add))
            link(dve.tensor_reduce(route[:, 0, :, :], scratch[:, 0, :, :, :], AX.X, ALU.add))
            link(dve.tensor_reduce(sums[:, 3, :], logits[:, :, :], AX.X, ALU.max))
            dve.tensor_tensor(route[:, 1, :, :], logits[:, :, :], sums[:, 3, :].unsqueeze(2).broadcast_to([P, TT, EXPERTS]),
                              ALU.subtract).then_inc(centred_logits, 1)
            sel = route[:, 3, :, :]
            dve.tensor_scalar(sel, route[:, 0, :, :], 2.0, None, ALU.is_lt).then_inc(chosen, 1)
            dve.wait_ge(exp_done, 1)
            dve.wait_ge(chosen, 1)
            link(dve.tensor_tensor(route[:, 4, :, :], route[:, 2, :, :], sel, ALU.mult))
            link(dve.tensor_reduce(sums[:, 4, :], route[:, 4, :, :], AX.X, ALU.add))
            link(dve.reciprocal(sums[:, 5, :], sums[:, 4, :]))
            gates = route[:, 5, :, :]
            link(dve.tensor_tensor(gates, route[:, 4, :, :], sums[:, 5, :].unsqueeze(2).broadcast_to([P, TT, EXPERTS]), ALU.mult))
            dve.wait_ge(counted, 1)
            place = route[:, 6, :, :]
            link(dve.scalar_tensor_tensor(out=place, in0=bank[5][:, 0:TT * EXPERTS].rearrange("p (t e) -> p t e", t=TT),
                                          scalar=1000.0, in1=sel, op0=ALU.add, op1=ALU.mult))
            link(dve.tensor_scalar(place, place, -1000.0, None, ALU.add))
            over, before_over, chosen_one = route[:, 7, 0, :], route[:, 7, 1, :], route[:, 0, 0, :]
            dve.wait_ge(ones_set, 1)
            link(dve.tensor_scalar(over, bank[5][:, TT * EXPERTS:(TT + 1) * EXPERTS], float(P), None, ALU.is_gt))
            link(dve.tensor_tensor_scan(route[:, 0, 1, :], ones[:, 0:EXPERTS], over, 0.0, ALU.mult, ALU.add))
            link(dve.tensor_tensor(before_over, route[:, 0, 1, :], over, ALU.subtract))
            dve.memset(pos_item[:, :, :], -1000.0)
            dve.memset(gate_item[:, :, :], 0.0)
            link(dve.memset(item_f[:, :], 0.0))
            dve.tensor_copy(pos_item[:, 0:EXPERTS, :].rearrange("p e t -> p t e"), place)
            dve.tensor_copy(gate_item[:, 0:EXPERTS, :].rearrange("p e t -> p t e"), gates)
            dve.tensor_copy(item_f[:, 0:EXPERTS], expert_no)
            for q in range(2):
                last = dve.tensor_scalar(item_f[:, MAX_ITEMS + q:MAX_ITEMS + q + 1], route[:, 0, 1, EXPERTS - 1:EXPERTS],
                                         float(EXPERTS - q), None, ALU.add)
            link(last)
            for j in range(3):
                link(dve.scalar_tensor_tensor(out=chosen_one, in0=before_over, scalar=float(j), in1=over, op0=ALU.is_equal, op1=ALU.mult))
                q = EXPERTS + j
                dve.tensor_tensor(route[:, 1, 0, :], chosen_one, expert_no, ALU.mult)
                for t in range(TT):
                    dve.tensor_tensor(route[:, 2, t, :], chosen_one, place[:, t, :], ALU.mult)
                    last = dve.tensor_tensor(route[:, 4, t, :], chosen_one, gates[:, t, :], ALU.mult)
                link(last)
                dve.tensor_reduce(item_f[:, q:q + 1], route[:, 1, 0, :], AX.X, ALU.add)
                dve.tensor_reduce(pos_item[:, q, :], route[:, 2, :, :], AX.X, ALU.add)
                link(dve.tensor_reduce(gate_item[:, q, :], route[:, 4, :, :], AX.X, ALU.add))
            link(dve.tensor_scalar(pos_item[:, EXPERTS:, :], pos_item[:, EXPERTS:, :], -float(P), None, ALU.add))
            dve.tensor_copy(item_tab[:, :], item_f[0:1, :]).then_inc(tab_ready, 1)

            def build_pick(i, where):
                for t in range(TT):
                    last = dve.tensor_scalar(pick[:, t, :], iota, where[:, t:t + 1], None, ALU.is_equal)
                last.then_inc(pick_ready, 1)

            build_pick(0, pos_item[:, 0, :])
            dve.tensor_copy(gate_item[:, :, :], gate_item[:, :, :]).then_inc(gates_f, 1)
            dve.wait_ge(gates_hi, 1)
            link(dve.tensor_tensor(gate_parts[:, :, :, 1], gate_item[:, :, :], gate_parts[:, :, :, 0].bitcast(F32), ALU.subtract))
            splits(TRUNK_UNITS + RING)

            def turned_lo(i, n):
                dve.wait_ge(ht_hi, i * STEPS + (n + 1))
                dve.tensor_tensor(hT_lo[:, 0, :], bank[2][:, :], hT_hi[:, 0, :].bitcast(F32), ALU.subtract).then_inc(ht_lo, 1)

            def gate_up(i, n, unit_end):
                dve.wait_ge(w_used, item_base(i) + unit_end)
                dve.wait_ge(silu_done, i * STEPS + (n + 1))
                dve.tensor_tensor(gated[:, 0, :], bank[1][:, :], act_tmp[:, 0, :], ALU.mult).then_inc(gated_done, 1)

            def tail(i):
                turned_lo(i, STEPS - 1)
                for c in range(2):
                    dve.wait_ge(y_hi_set, 2 * i + (c + 1))
                    dve.scalar_tensor_tensor(out=y_lo[:, c * BLK:(c + 1) * BLK], in0=bank[3 + c][:, :], scalar=gate_col[:, 0:1],
                                             in1=y_hi[:, c * BLK:(c + 1) * BLK].bitcast(F32), op0=ALU.mult, op1=ALU.subtract).then_inc(y_lo_set, 1)

            def add_item(i):
                wait(dve, h_added, 4 * i)
                for q in range(4):
                    dve.wait_ge(scattered, 4 * i + (q + 1))
                    add_to_h(q % 2, q // 2, (5, 6, 7, 2)[q], h_added)

            def item(i, first):
                if not first:
                    split_item(i, range(0, 4))
                for b in range(2):
                    dve.wait_ge(xg_hi_set, 2 * i + (b + 1))
                    dve.tensor_tensor(xT_lo[:, b * BLK:(b + 1) * BLK], bank[5 + b][:, :], xT_hi[:, b * BLK:(b + 1) * BLK].bitcast(F32),
                                      ALU.subtract).then_inc(xg_lo_set, 1)
                if not first:
                    tail(i - 1)
                    split_item(i, range(4, 6))
                split_item(i, range(6, 8))
                if not first:
                    add_item(i - 1)
                gate_up(i, 0, 4)
                split_item(i, range(8, 10))
                turned_lo(i, 0)
                split_item(i, range(10, 12))
                gate_up(i, 1, step_unit(1) + 4)
                split_item(i, range(12, 16))
                dve.wait_ge(pickT_set, i + 1)
                dve.tensor_reduce(gate_col[:, :], bank[5][:, 0:2], AX.X, ALU.add).then_inc(gate_col_set, 1)
                build_pick(i + 1, pos_item[:, 1, :] if first else pos_item[:, bass.ds(i + 1, 1), :].rearrange("p o t -> p (o t)"))
                with dve.Fori(2, STEPS - 1) as n:
                    dve.wait_ge(ht_hi, i * STEPS + n)
                    dve.tensor_tensor(hT_lo[:, 0, :], bank[2][:, :], hT_hi[:, 0, :].bitcast(F32), ALU.subtract).then_inc(ht_lo, 1)
                    for j in range(RING):
                        if j == 2:
                            dve.wait_ge(w_used, item_base(i) + n * 6 + 2)
                            dve.wait_ge(silu_done, i * STEPS + n + 1)
                            dve.tensor_tensor(gated[:, 0, :], bank[1][:, :], act_tmp[:, 0, :], ALU.mult).then_inc(gated_done, 1)
                        m = 10 - 6 + j
                        s = ring_slot(TRUNK_UNITS + m)
                        dve.wait_ge(hi_split, item_base(i) + n * 6 + (m + 1))
                        dve.tensor_tensor(w_lo[:, s, :], raw_at(m % RING), w_hi[:, s, :].bitcast(F32), ALU.subtract).then_inc(lo_split, 1)
                turned_lo(i, STEPS - 2)
                split_item(i, range(ITEM_UNITS - 2, ITEM_UNITS))
                gate_up(i, STEPS - 1, step_unit(STEPS - 1) + 4)

            dve.wait_ge(tab_ready, 1)
            n_items = dve.value_load(item_tab[0:1, MAX_ITEMS:MAX_ITEMS + 1], min_val=EXPERTS, max_val=MAX_ITEMS - 1)
            last_item = dve.value_load(item_tab[0:1, MAX_ITEMS + 1:MAX_ITEMS + 2], min_val=EXPERTS - 1, max_val=MAX_ITEMS - 2)
            item(0, True)
            with dve.Fori(1, n_items) as i:
                item(i, False)
            tail(last_item)
            add_item(last_item)
            dve.wait_ge(norm_sq[4], TT)
            dve.tensor_scalar(sums[:, 1, :], sums[:, 0, :], 1.0 / D, EPS, ALU.mult, ALU.add).then_inc(norm_ms[4], 1)
            dve.wait_ge(norm_root[4], 1)
            link(dve.reciprocal(sums[:, 6, :], sums[:, 2, :]))
            dve.wait_ge(g_final_in, 16)
            for t in range(TT):
                dve.scalar_tensor_tensor(out=raw_at(1 + t)[:, 0:D], in0=h[:, t, :], scalar=sums[:, 6, t:t + 1], in1=raw_at(0)[:, 0:D],
                                         op0=ALU.mult, op1=ALU.mult).then_inc(out_ready, 1)

        @block.tensor
        def _(pe):
            def product(dst, a_hi, a_lo, b_hi, b_lo, first, last):
                pe.matmul(dst, a_hi, b_hi, start=first, stop=False)
                pe.matmul(dst, a_hi, b_lo, start=False, stop=False)
                return pe.matmul(dst, a_lo, b_hi, start=False, stop=last)

            def weights(slot, kts, cols):
                return (w_hi[:, slot, :].rearrange("p (k c) -> p k c", k=kts)[:, :, 0:cols],
                        w_lo[:, slot, :].rearrange("p (k c) -> p k c", k=kts)[:, :, 0:cols])

            def columns(units, t, dst, nf=BLK, more=False, tile=None):
                per = KT // len(units)
                for q, u in enumerate(units):
                    pe.wait_ge(lo_split, u + 1)
                    b_hi, b_lo = weights(ring_slot(u), per, nf)
                    for k in range(per):
                        kt = q * per + k
                        toks = slice(t * P, (t + 1) * P)
                        last = product(dst[:, 0:nf], xT_hi_k[:, kt, toks], xT_lo_k[:, kt, toks], b_hi[:, k, :], b_lo[:, k, :],
                                       kt == 0 and not more, kt == KT - 1)
                    if t == TT - 1:
                        last.then_inc(w_used, 1)
                return last

            def pair(units, dsts, nf=BLK):
                per = KT // len(units)
                for q, u in enumerate(units):
                    pe.wait_ge(lo_split, u + 1)
                    b_hi, b_lo = weights(ring_slot(u), per, nf)
                    for t in range(TT):
                        toks = slice(t * P, (t + 1) * P)
                        for k in range(per):
                            kt = q * per + k
                            last = product(dsts[t][:, 0:nf], xT_hi_k[:, kt, toks], xT_lo_k[:, kt, toks], b_hi[:, k, :],
                                           b_lo[:, k, :], kt == 0, kt == KT - 1)
                    last.then_inc(w_used, 1)

            def turn_scaled(s):
                for k in range(KT):
                    for t in range(TT):
                        if k == 0:
                            pe.wait_ge(norm_scaled[s], t + 1)
                        last = pe.transpose(bank[k // 2][:, (k % 2) * SEQ + t * P:(k % 2) * SEQ + (t + 1) * P],
                                            scaled[:, t, k * P:(k + 1) * P], ident)
                    if k % 2 == 1:
                        last.then_inc(turned[s], 1)

            pe.wait_ge(con_in, 16)
            turn_scaled(0)
            pe.wait_ge(xT_lo_set[0], 4)
            pair([0, 1], bank[4:6])
            pair([2, 3], bank[6:8])
            pair([4, 5], bank[0:2])
            pe.wait_ge(z_copied, 2)
            pe.wait_ge(gelu_done, 4)
            pe.wait_ge(band_in, 16)
            for g in range(GROUPS):
                chans = slice(g * P, (g + 1) * P)
                o = bank[4 + g // 2][:, (g % 2) * SEQ:(g % 2 + 1) * SEQ]
                pe.matmul(o[:, 0:P], z_sb[:, 0, chans], band_sb[:, g, 0:P], start=True, stop=True)
                pe.matmul(o[:, P:SEQ], z_sb[:, 0, chans], band_sb[:, g, P:2 * P], start=True, stop=False)
                last = pe.matmul(o[:, P:SEQ], z_sb[:, 1, chans], band_sb[:, g, 2 * P:3 * P], start=False, stop=True)
                if g % 2 == 1:
                    last.then_inc(pooled, 1)
            pe.wait_ge(masked, 1)
            for t in range(TT):
                pe.wait_ge(v_normed, t + 1)
                for hd in range(HEADS):
                    cols = slice(hd * HEAD_DIM, (hd + 1) * HEAD_DIM)
                    last = pe.matmul(bank[2 + t][:, cols], wsp_sb[:, hd, :], v_sb[:, t, cols], start=True, stop=True)
                last.then_inc(mixed, 1)
            pe.wait_ge(wpool_in, 16)
            for g in range(GROUPS):
                pe.wait_ge(pool_copied, g // 2 + 1)
                last = pe.matmul(bank[6 + g // 2][:, (g % 2) * SEQ:(g % 2 + 1) * SEQ], wpool_sb[:, g, :], mixedT[:, g, :],
                                 start=True, stop=True)
                if g % 2 == 1:
                    last.then_inc(pool_mapped, 1)
            pe.wait_ge(a_gated, 2)
            for b in range(4):
                for t in range(TT):
                    last = pe.transpose(bank[b // 2][:, (b % 2) * SEQ + t * P:(b % 2) * SEQ + (t + 1) * P],
                                        u_sb[:, t, b * P:(b + 1) * P], ident)
                if b % 2 == 1:
                    last.then_inc(a_turned, 1)
            pe.wait_ge(cat_lo, 4)
            pair([6, 7], bank[2:4])
            pair([8, 9], bank[4:6])
            turn_scaled(1)
            pe.wait_ge(xT_lo_set[1], 4)

            def turn_hidden(n, t, nf):
                pe.wait_ge(ffn_gated[t], n + 1)
                for f in range(nf // P):
                    last = pe.transpose(bank[t][:, f * P:(f + 1) * P], gated[:, t, f * P:(f + 1) * P], ident)
                last.then_inc(ffn_turned[t], 1)

            def down(n, t, units):
                pe.wait_ge(ffn_lo[t], n + 1)
                for q, u in enumerate(units):
                    pe.wait_ge(lo_split, u + 1)
                    b_hi, b_lo = weights(ring_slot(u), 2, D)
                    for f in range(2):
                        ft = slice((2 * q + f) * P, (2 * q + f + 1) * P)
                        for c in range(2):
                            cols = slice(c * BLK, (c + 1) * BLK)
                            last = product(bank[4 + 2 * t + c][:, :], hT_hi[:, t, ft], hT_lo[:, t, ft], b_hi[:, f, cols], b_lo[:, f, cols],
                                           n == 0 and q == 0 and f == 0, n == FFN_BLOCKS - 1 and f == 1)
                    if t == TT - 1:
                        last.then_inc(w_used, 1)

            def ffn_units(n):
                base = U_FFN + 6 * n
                if n < FFN_BLOCKS - 1:
                    return BLK, [base, base + 1], [base + 2, base + 3], [base + 4, base + 5]
                return BLK // 2, [base], [base + 1], [base + 2]

            for n in range(FFN_BLOCKS):
                nf, gate_u, up_u, down_u = ffn_units(n)
                columns(gate_u, 0, bank[0], nf).then_inc(ffn_first, 1)
                if n >= 1:
                    pf, _, _, last_down = ffn_units(n - 1)
                    turn_hidden(n - 1, 1, pf)
                columns(up_u, 0, bank[2], nf).then_inc(ffn_first, 1)
                if n >= 1:
                    down(n - 1, 1, last_down)
                columns(gate_u, 1, bank[1], nf)
                turn_hidden(n, 0, nf)
                columns(up_u, 1, bank[3], nf)
                down(n, 0, down_u)
            nf, _, _, down_u = ffn_units(FFN_BLOCKS - 1)
            turn_hidden(FFN_BLOCKS - 1, 1, nf)
            down(FFN_BLOCKS - 1, 1, down_u)
            turn_scaled(2)
            pe.wait_ge(xT_lo_set[2], 4)
            for j in range(2):
                u0 = U_PW1 + 4 * j
                wait(pe, val_copied, 2 * j)
                pair([u0, u0 + 1], bank[4:6])
                wait(pe, gatec_copied, 2 * j)
                pair([u0 + 2, u0 + 3], bank[6:8])
                pe.wait_ge(val_copied, 2 * j + 2)
                pe.wait_ge(gatec_copied, 2 * j + 2)
                for c in range(4 * j, 4 * j + 4):
                    wait(pe, glu_done, c - 3)
                    for t in range(TT):
                        pe.transpose(bank[c % 4][:, t * P:(t + 1) * P], gated[:, t, (c % 4) * P:(c % 4 + 1) * P], ident)
                        last = pe.transpose(bank[c % 4][:, SEQ + t * P:SEQ + (t + 1) * P], act_tmp[:, t, (c % 4) * P:(c % 4 + 1) * P], ident)
                    last.then_inc(vg_turned, 1)
            pe.wait_ge(ones_set, 1)
            for c in range(KT):
                pe.wait_ge(conv_step, (c // 4) * 4 * CONV_K + 4 * (CONV_K - 1) + c % 4 + 1)
                last = pe.matmul(bank[4][:, 0:SEQ], ones[:, :], yc[:, c, :], start=c == 0, stop=c == KT - 1)
            last.then_inc(sum_done, 1)
            for c in range(KT):
                pe.wait_ge(sq_done, c // 4 + 1)
                last = pe.matmul(bank[5][:, 0:SEQ], ones[:, :], squares[:, c, :], start=c == 0, stop=c == KT - 1)
            last.then_inc(sum_done, 1)
            pe.wait_ge(cv_lo, 4)
            pe.wait_ge(b_pw2_in, 16)
            for c in range(2):
                us = [U_PW2 + 2 * c, U_PW2 + 2 * c + 1]
                for t in range(TT):
                    pe.matmul(bank[4 + 2 * c + t][:, :], ones[0:1, :], act_flat[0:1, c * BLK:(c + 1) * BLK], start=True, stop=False)
                for q, u in enumerate(us):
                    pe.wait_ge(lo_split, u + 1)
                    b_hi, b_lo = weights(ring_slot(u), 4, BLK)
                    for t in range(TT):
                        toks = slice(t * P, (t + 1) * P)
                        for k in range(4):
                            kt = q * 4 + k
                            last = product(bank[4 + 2 * c + t][:, :], xT_hi_k[:, kt, toks], xT_lo_k[:, kt, toks], b_hi[:, k, :],
                                           b_lo[:, k, :], False, kt == KT - 1)
                    last.then_inc(w_used, 1)
            turn_scaled(3)
            pe.wait_ge(xT_lo_set[3], 4)
            pe.wait_ge(router_lo_set, 1)
            for t in range(TT):
                toks = slice(t * P, (t + 1) * P)
                o = bank[4][:, t * EXPERTS:(t + 1) * EXPERTS]
                for k in range(KT):
                    r = slice(k * EXPERTS, (k + 1) * EXPERTS)
                    product(o, xT_hi_k[:, k, toks], xT_lo_k[:, k, toks], router_hi[:, r], router_lo[:, r], k == 0, False)
                    last = pe.matmul(o, xT_lo_k[:, k, toks], router_lo[:, r], start=False, stop=k == KT - 1)
            last.then_inc(logits_done, 1)
            pe.wait_ge(chosen, 1)
            sel = route[:, 3, :, :]
            places = bank[5]
            pe.matmul(places[:, 0:EXPERTS], before, sel[:, 0, :], start=True, stop=True)
            pe.matmul(places[:, EXPERTS:2 * EXPERTS], ones[:, :], sel[:, 0, :], start=True, stop=False)
            pe.matmul(places[:, EXPERTS:2 * EXPERTS], before, sel[:, 1, :], start=False, stop=True)
            pe.matmul(places[:, 2 * EXPERTS:3 * EXPERTS], ones[:, :], sel[:, 0, :], start=True, stop=False)
            pe.matmul(places[:, 2 * EXPERTS:3 * EXPERTS], ones[:, :], sel[:, 1, :], start=False, stop=True).then_inc(counted, 1)

            def item_columns(i, m0, dst):
                for q in range(2):
                    pe.wait_ge(lo_split, item_base(i) + (m0 + q + 1))
                    b_hi, b_lo = weights(ring_slot(TRUNK_UNITS + m0 + q), 4, BLK)
                    for k in range(4):
                        kt = q * 4 + k
                        last = product(dst[:, :], xg_hi[:, kt, :], xg_lo[:, kt, :], b_hi[:, k, :], b_lo[:, k, :], kt == 0, kt == KT - 1)
                    last.then_inc(w_used, 1)

            def item_down(i, m0, first, last_step):
                for q in range(2):
                    pe.wait_ge(lo_split, item_base(i) + (m0 + q + 1))
                    b_hi, b_lo = weights(ring_slot(TRUNK_UNITS + m0 + q), 2, D)
                    for f in range(2):
                        ft = slice((2 * q + f) * P, (2 * q + f + 1) * P)
                        for c in range(2):
                            cols = slice(c * BLK, (c + 1) * BLK)
                            last = product(bank[3 + c][:, :], hT_hi[:, 0, ft], hT_lo[:, 0, ft], b_hi[:, f, cols], b_lo[:, f, cols],
                                           first and q == 0 and f == 0, last_step and q == 1 and f == 1)
                    last.then_inc(w_used, 1)

            def item_turn():
                for f in range(BLK // P):
                    last = pe.transpose(bank[2][:, f * P:(f + 1) * P], gated[:, 0, f * P:(f + 1) * P], ident)
                last.then_inc(ht_turned, 1)

            def tail(i):
                pe.wait_ge(gated_done, (i + 1) * STEPS)
                item_turn()
                pe.wait_ge(ht_lo, (i + 1) * STEPS)
                item_down(i, ITEM_UNITS - 2, False, True)

            def scatter(i):
                pe.wait_ge(y_lo_set, 2 * i + 2)
                pe.wait_ge(pickT_set, i + 1)
                for q in range(4):
                    t, c = q // 2, q % 2
                    dst = bank[(5, 6, 7, 2)[q]][:, :]
                    cols = slice(c * BLK, (c + 1) * BLK)
                    pe.matmul(dst, pickT[:, t * P:(t + 1) * P], y_hi[:, cols], start=True, stop=False)
                    pe.matmul(dst, pickT[:, t * P:(t + 1) * P], y_lo[:, cols], start=False, stop=True).then_inc(scattered, 1)

            def item(i, first):
                pe.wait_ge(pick_ready, i + 1)
                wait(pe, gate_col_set, i)
                for b in range(2):
                    for k in range(4):
                        o = bank[5 + b][:, k * P:(k + 1) * P]
                        chans = slice((4 * b + k) * P, (4 * b + k + 1) * P)
                        for t in range(TT):
                            pe.matmul(o, xn_hi[:, t, chans], pick[:, t, :], start=t == 0, stop=False)
                            last = pe.matmul(o, xn_lo[:, t, chans], pick[:, t, :], start=False, stop=t == TT - 1)
                    last.then_inc(gathered, 1)
                if not first:
                    tail(i - 1)
                pe.wait_ge(xg_lo_set, 2 * i + 2)
                wait(pe, silu_done, i * STEPS)
                item_columns(i, 0, bank[0])
                if not first:
                    scatter(i - 1)
                wait(pe, gated_done, i * STEPS)
                item_columns(i, 2, bank[1])
                pe.wait_ge(silu_done, i * STEPS + 1)
                item_columns(i, 4, bank[0])
                pe.wait_ge(gated_done, i * STEPS + 1)
                wait(pe, h_added, 4 * i)
                item_turn()
                item_columns(i, 6, bank[1])
                pe.wait_ge(ht_lo, i * STEPS + 1)
                item_down(i, 8, True, False)
                pe.wait_ge(gates_hi, 1)
                for t in range(TT):
                    parts = gate_parts[:, 0, t, :] if first else gate_parts[:, bass.ds(i, 1), t, :].rearrange("p o w -> p (o w)")
                    pe.matmul(bank[5][:, 0:2], pick[:, t, :], parts, start=t == 0, stop=t == TT - 1)
                for t in range(TT):
                    last = pe.transpose(bank[5][:, P + t * P:P + (t + 1) * P], pick[:, t, :].bitcast(F32), ident)
                last.then_inc(slots_turned, 1)
                with pe.Fori(2, STEPS) as n:
                    pe.wait_ge(silu_done, i * STEPS + n)
                    b = item_base(i) + n * 6
                    for q in range(2):
                        pe.wait_ge(lo_split, b + (q - 1))
                        b_hi, b_lo = weights(ring_slot(TRUNK_UNITS + 4 + q), 4, BLK)
                        for k in range(4):
                            kt = q * 4 + k
                            last = product(bank[0][:, :], xg_hi[:, kt, :], xg_lo[:, kt, :], b_hi[:, k, :], b_lo[:, k, :], kt == 0, kt == KT - 1)
                        last.then_inc(w_used, 1)
                    pe.wait_ge(gated_done, i * STEPS + n)
                    item_turn()
                    for q in range(2):
                        pe.wait_ge(lo_split, b + (q + 1))
                        b_hi, b_lo = weights(ring_slot(TRUNK_UNITS + 6 + q), 4, BLK)
                        for k in range(4):
                            kt = q * 4 + k
                            last = product(bank[1][:, :], xg_hi[:, kt, :], xg_lo[:, kt, :], b_hi[:, k, :], b_lo[:, k, :], kt == 0, kt == KT - 1)
                        last.then_inc(w_used, 1)
                    pe.wait_ge(ht_lo, i * STEPS + n)
                    for q in range(2):
                        pe.wait_ge(lo_split, b + (q + 3))
                        b_hi, b_lo = weights(ring_slot(TRUNK_UNITS + 8 + q), 2, D)
                        for f in range(2):
                            ft = slice((2 * q + f) * P, (2 * q + f + 1) * P)
                            for c in range(2):
                                cols = slice(c * BLK, (c + 1) * BLK)
                                last = product(bank[3 + c][:, :], hT_hi[:, 0, ft], hT_lo[:, 0, ft], b_hi[:, f, cols], b_lo[:, f, cols], False, False)
                        last.then_inc(w_used, 1)

            pe.wait_ge(tab_ready, 1)
            n_items = pe.value_load(item_tab[0:1, MAX_ITEMS:MAX_ITEMS + 1], min_val=EXPERTS, max_val=MAX_ITEMS - 1)
            last_item = pe.value_load(item_tab[0:1, MAX_ITEMS + 1:MAX_ITEMS + 2], min_val=EXPERTS - 1, max_val=MAX_ITEMS - 2)
            item(0, True)
            with pe.Fori(1, n_items) as i:
                item(i, False)
            tail(last_item)
            scatter(last_item)


def col_units(w, nf, halves):
    f = w.shape[1]
    per = KT // halves
    return (w.reshape(halves, per, P, f // nf, nf).transpose(3, 0, 2, 1, 4).reshape(f // nf, halves, P, UNIT))


def row_units(w):
    return w.reshape(-1, 2, P, D).transpose(0, 2, 1, 3).reshape(-1, P, UNIT)


def constants():
    con = np.zeros((P, K_ALL), np.float32)
    con[:, K_IDENT:K_IDENT + P] = np.eye(P)
    s = np.arange(P)
    con[:, K_BEFORE:K_BEFORE + P] = s[:, None] < s[None, :]
    con[:, K_IOTA:K_IOTA + P] = s[None, :]
    e = np.arange(EXPERTS)
    con[:, K_TIE:K_TIE + 64] = (e[None, :] < e[:, None]).reshape(1, 64)
    con[:, K_EXPERT:K_EXPERT + EXPERTS] = e[None, :]
    band = np.zeros((P, GROUPS, 3 * P), np.float32)
    t = np.arange(SEQ)
    for g, win in enumerate(WINDOWS):
        lag = t[None, :] - t[:, None]
        b = np.where((lag >= 0) & (lag < win), np.float32(1) / np.minimum(t + 1, win).astype(np.float32)[None, :], np.float32(0))
        b = b - np.eye(SEQ, dtype=np.float32)
        band[:, g, 0:SEQ] = b[0:P, :]
        band[:, g, SEQ:] = b[P:, P:]
    return con, band


def kernel(**inputs):
    import concourse.bacc as _bacc
    from concourse.bass_utils import run_bass_kernel_spmd as _run

    a = {k: np.asarray(v) for k, v in inputs.items()}
    f32 = np.float32

    trunk = np.empty((TRUNK_UNITS, P, UNIT), f32)
    trunk[U_IN:U_OUT] = col_units(a["w_in_e"][0], BLK, 2).reshape(-1, P, UNIT)
    trunk[U_OUT:U_FFN] = col_units(a["w_out_e"][0], BLK, 2).reshape(-1, P, UNIT)
    whole = (FFN_BLOCKS - 1) * BLK
    ffn = trunk[U_FFN:U_FFN + 30].reshape(FFN_BLOCKS - 1, 3, 2, P, UNIT)
    ffn[:, 0] = col_units(a["w_gate_d"][0][:, :whole], BLK, 2)
    ffn[:, 1] = col_units(a["w_up_d"][0][:, :whole], BLK, 2)
    ffn[:, 2] = row_units(a["w_down_d"][0][:whole]).reshape(-1, 2, P, UNIT)
    trunk[U_FFN + 30] = col_units(a["w_gate_d"][0][:, whole:], BLK // 2, 1)[0, 0]
    trunk[U_FFN + 31] = col_units(a["w_up_d"][0][:, whole:], BLK // 2, 1)[0, 0]
    trunk[U_FFN + 32] = row_units(a["w_down_d"][0][whole:])[0]
    pw1 = col_units(a["w_pw1"][0], BLK, 2)
    trunk[U_PW1:U_PW2] = pw1[[0, 2, 1, 3]].reshape(-1, P, UNIT)
    trunk[U_PW2:] = col_units(a["w_pw2"][0], BLK, 2).reshape(-1, P, UNIT)

    experts = np.empty((EXPERTS, ITEM_UNITS, P, UNIT), f32)
    for e in range(EXPERTS):
        g = col_units(a["w_gate_x"][0, e], BLK, 2)
        u = col_units(a["w_up_x"][0, e], BLK, 2)
        d = row_units(a["w_down_x"][0, e]).reshape(STEPS, 2, P, UNIT)
        experts[e, 0:2], experts[e, 2:4] = g[0], u[0]
        for n in range(1, STEPS):
            m = 4 + 6 * (n - 1)
            experts[e, m:m + 2], experts[e, m + 2:m + 4], experts[e, m + 4:m + 6] = g[n], u[n], d[n - 1]
        experts[e, ITEM_UNITS - 2:] = d[STEPS - 1]

    def by_channel(v):
        return v.reshape(-1, P).T

    w_dw = a["w_dw"][0].reshape(CONV_K, KT, P).transpose(2, 1, 0).reshape(P, -1)
    router = a["w_router"][0].reshape(KT, P, EXPERTS).transpose(1, 0, 2).reshape(P, -1)
    channel = np.concatenate([by_channel(a["norm_mix_e"][0]), by_channel(a["norm_ffn_e"][0]), by_channel(a["norm_mix_o"][0]),
                              by_channel(a["pool_scale"][0]), by_channel(a["b_dw"][0]), by_channel(a["ln_g"][0]),
                              by_channel(a["ln_b"][0]), by_channel(a["b_pw1"][0]), a["b_spatial"][0].T, w_dw, router], axis=1)
    con, band = constants()
    arrays = {
        "x_in_dram": a["x"][0], "trunk_dram": trunk, "experts_dram": experts.reshape(-1, P, UNIT),
        "channel_dram": channel, "consts_dram": con, "bands_dram": band,
        "w_spatial_dram": a["w_spatial"][0].transpose(2, 0, 1), "w_pool_dram": a["w_pool"][0].transpose(1, 0, 2),
        "sgu_norm_dram": a["sgu_norm"][0], "b_pw2_dram": a["b_pw2"], "norm_ffn_o_dram": a["norm_ffn_o"][0],
        "norm_final_dram": a["norm_final"],
    }
    arrays = {k: np.ascontiguousarray(v) for k, v in arrays.items()}
    nc = _bacc.Bacc("TRN2", target_bir_lowering=False, num_devices=1)
    args = [nc.dram_tensor(k, v.shape, F32, kind="ExternalInput").ap() for k, v in arrays.items()]
    args.append(nc.dram_tensor("out_dram", (SEQ, D), F32, kind="ExternalOutput").ap())
    build(nc, *args)
    r = _run(nc, [arrays], core_ids=[0])
    return r.results[0]["out_dram"].reshape(1, SEQ, D)
```

```python
from contextlib import ExitStack

import numpy as np

import concourse.bass as bass
from concourse import mybir

ALU = mybir.AluOpType
ACT = mybir.ActivationFunctionType
AX = mybir.AxisListType
F32 = mybir.dt.float32
F32R = mybir.dt.float32r
I32 = mybir.dt.int32

P = 128
SEQ = 256
D = 1024
TT = SEQ // P
KT = D // P
HEADS = 8
HEAD_DIM = 64
WINDOWS = (2, 4, 8, 16)
GROUPS = len(WINDOWS)
CONV_K = 31
F_DENSE = 2816
F_EXPERT = 3584
EXPERTS = 8
EPS = 1e-6

UNIT = 2048
BLK = 512
RING = 6
RAW_EARLY = 3

U_IN = 0
U_OUT = U_IN + 6
U_FFN = U_OUT + 4
FFN_BLOCKS = 6
U_PW1 = U_FFN + 33
U_PW2 = U_PW1 + 8
TRUNK_UNITS = U_PW2 + 4
STEPS = F_EXPERT // BLK
ITEM_UNITS = 6 * STEPS
OVERFLOWS = 3
SLOT_BASE = 1000
MAX_ITEMS = 12

PE_TAPS = 13
DIAGS = 8

C_NORM_MIX_E, C_NORM_FFN_E, C_NORM_MIX_O = 0, 8, 16
C_POOL_SCALE, C_B_DW, C_LN_G, C_LN_B = 24, 28, 36, 44
C_B_PW1, C_B_SPATIAL, C_W_DW, C_ROUTER = 52, 68, 76, 76 + 8 * CONV_K
C_ALL = C_ROUTER + KT * EXPERTS
C_NORM_FFN_O = C_ALL
C_ALL += 8
K_IDENT, K_BEFORE, K_SLOTS, K_TIE, K_EXPERT = 0, 128, 256, 384, 448
K_ALL = 456


def build(nc, x, trunk, experts, channel, consts, bands, w_spatial, w_pool, sgu_norm, b_pw2,
          norm_final, out):
    ctx = ExitStack()
    with ctx:
        def sb(name, shape, dt=F32):
            return ctx.enter_context(nc.sbuf_tensor(name, shape, dt))

        def sem(name):
            return ctx.enter_context(nc.semaphore(name))

        raw = sb("raw", [P, RING * UNIT + 256])
        w_hi = sb("w_hi", [P, RING, UNIT], F32R)
        w_lo = sb("w_lo", [P, RING, UNIT], F32R)
        xT_hi = sb("xT_hi", [P, KT * SEQ], F32R)
        xT_lo = sb("xT_lo", [P, KT * SEQ], F32R)
        hT_hi = sb("hT_hi", [P, TT, BLK], F32R)
        hT_lo = sb("hT_lo", [P, TT, BLK], F32R)
        xn_hi = sb("xn_hi", [P, TT, D], F32R)
        xn_lo = sb("xn_lo", [P, TT, D], F32R)
        pick = sb("pick", [P, TT, P], F32R)
        pickT = sb("pickT", [P, SEQ], F32R)
        gate_parts = sb("gate_parts", [P, MAX_ITEMS, TT, 2], F32R)
        router_hi = sb("router_hi", [P, KT * EXPERTS], F32R)
        router_lo = sb("router_lo", [P, KT * EXPERTS], F32R)
        h = sb("h", [P, TT, D])
        gated = sb("gated", [P, TT, BLK])
        act_tmp = sb("act_tmp", [P, TT, BLK])
        par = sb("par", [P, C_ALL])
        con = sb("con", [P, K_ALL])
        ones = sb("ones", [P, P])
        sums = sb("sums", [P, 8, TT])
        pos_item = sb("pos_item", [P, MAX_ITEMS, TT])
        gate_col = sb("gate_col", [P, 1])
        item_tab = sb("item_tab", [1, MAX_ITEMS + 4], I32)

        bank = [ctx.enter_context(nc.psum_tensor(f"bank{i}", [P, BLK], F32)) for i in range(8)]

        arena = raw[:, RAW_EARLY * UNIT:]
        u_sb = arena[:, 0:1024].rearrange("p (t d) -> p t d", t=TT)
        v_sb = arena[:, 1024:2048].rearrange("p (t d) -> p t d", t=TT)
        z_sb = arena[:, 2048:3072].rearrange("p (t d) -> p t d", t=TT)
        band_sb = arena[:, 3072:4608].rearrange("p (g s) -> p g s", g=GROUPS)
        wsp_sb = arena[:, 4608:5632].rearrange("p (h s) -> p h s", h=HEADS)
        wpool_sb = arena[:, 5632:6144].rearrange("p (g s) -> p g s", g=GROUPS)
        sig = arena[:, 0:1024].rearrange("p (c s) -> p c s", c=4)
        squares = arena[:, 0:2048].rearrange("p (c s) -> p c s", c=KT)
        diags = arena[:, 1024:1024 + DIAGS * P].rearrange("p (q c) -> p q c", q=DIAGS)
        xc = arena[:, 2048:2048 + KT * (SEQ + CONV_K - 1)].rearrange("p (c s) -> p c s", c=KT)
        yc = arena[:, 4336:4336 + KT * SEQ].rearrange("p (c s) -> p c s", c=KT)
        mean_sb = arena[:, 2048:2048 + SEQ]
        rstd_sb = arena[:, 2304:2304 + SEQ]
        mixedT = gated[:, :, :].rearrange("p t s -> p (t s)").rearrange("p (g s) -> p g s", g=GROUPS)
        act_flat = act_tmp[:, :, :].rearrange("p t s -> p (t s)")
        gv_sb = act_tmp[:, 0, :]
        route = act_tmp[:, 1, 0:128].rearrange("p (q t e) -> p q t e", q=8, t=TT)
        logits = act_tmp[:, 1, 128:144].rearrange("p (t e) -> p t e", t=TT)
        ahead = gated[:, 0, 0:256].rearrange("p (t e j) -> p t e j", t=TT, e=EXPERTS)
        taken = gated[:, 1, 0:24].rearrange("p (o e) -> p o e", o=OVERFLOWS)
        taken_no = gated[:, 1, 24:48].rearrange("p (o e) -> p o e", o=OVERFLOWS)
        taken_place = gated[:, 1, 48:96].rearrange("p (o t e) -> p o t e", o=OVERFLOWS, t=TT)
        taken_gate = gated[:, 1, 96:144].rearrange("p (o t e) -> p o t e", o=OVERFLOWS, t=TT)
        item_f = act_tmp[:, 1, 144:144 + MAX_ITEMS + 4]
        gate_item = act_tmp[:, 1, 160:160 + MAX_ITEMS * TT].rearrange("p (i t) -> p i t", t=TT)
        ident = con[:, K_IDENT:K_IDENT + P]
        before = con[:, K_BEFORE:K_BEFORE + P]
        slots = con[:, K_SLOTS:K_SLOTS + P]
        tie = con[:, K_TIE:K_TIE + 64].rearrange("p (e j) -> p e j", e=EXPERTS)
        expert_no = con[:, K_EXPERT:K_EXPERT + EXPERTS]
        xT_hi_k = xT_hi[:, :].rearrange("p (k s) -> p k s", k=KT)
        xT_lo_k = xT_lo[:, :].rearrange("p (k s) -> p k s", k=KT)
        xg_hi = xT_hi[:, 0:KT * P].rearrange("p (k s) -> p k s", k=KT)
        xg_lo = xT_lo[:, 0:KT * P].rearrange("p (k s) -> p k s", k=KT)
        y_hi = xT_hi[:, KT * P:]
        y_lo = xT_lo[:, KT * P:]

        x_in, par_in, con_in = [sem(f"x_in{t}") for t in range(TT)], sem("par_in"), sem("con_in")
        band_in, wsp_in, wpool_in, gv_in = sem("band_in"), sem("wsp_in"), sem("wpool_in"), sem("gv_in")
        b_pw2_in, g_final_in = sem("b_pw2_in"), sem("g_final_in")
        out_written = sem("out_written")
        landed = [sem(f"landed{s}") for s in range(RING)]
        hi_split, lo_split, w_used = sem("hi_split"), sem("lo_split"), sem("w_used")
        ones_set, masked = sem("ones_set"), sem("masked")
        norm_sq = [sem(f"norm_sq{s}") for s in range(5)]
        norm_ms = [sem(f"norm_ms{s}") for s in range(5)]
        norm_root = [sem(f"norm_root{s}") for s in range(5)]
        norm_rstd_set = [sem(f"norm_rstd_set{s}") for s in range(4)]
        turned = [sem(f"turned{s}") for s in range(4)]
        xT_hi_set = [sem(f"xT_hi_set{s}") for s in range(4)]
        xT_lo_set = [sem(f"xT_lo_set{s}") for s in range(4)]
        dve_step = sem("dve_step")
        gelu_done, v_sq, v_ms, v_root, v_normed = (sem(n) for n in ("gelu_done", "v_sq", "v_ms", "v_root", "v_normed"))
        z_copied, pooled, pool_copied, pool_mapped = (sem(n) for n in ("z_copied", "pooled", "pool_copied", "pool_mapped"))
        mixed, a_gated, a_turned = sem("mixed"), sem("a_gated"), sem("a_turned")
        cat_hi, cat_lo, h_mixed = sem("cat_hi"), sem("cat_lo"), sem("h_mixed")
        ffn_first = sem("ffn_first")
        ffn_silu = [sem("ffn_silu0"), sem("ffn_silu1")]
        ffn_gated = [sem("ffn_gated0"), sem("ffn_gated1")]
        ffn_turned = [sem("ffn_turned0"), sem("ffn_turned1")]
        ffn_hi = [sem("ffn_hi0"), sem("ffn_hi1")]
        ffn_lo = [sem("ffn_lo0"), sem("ffn_lo1")]
        ffn_down0 = sem("ffn_down0")
        h_ffn = sem("h_ffn")
        val_copied, gatec_copied, vg_turned = sem("val_copied"), sem("gatec_copied"), sem("vg_turned")
        sig_done, glu_done, conv_step = sem("sig_done"), sem("glu_done"), sem("conv_step")
        diag_set, diag_used, conv_merged = (sem(n) for n in ("diag_set", "diag_used", "conv_merged"))
        sum_done, centred, sq_done, var_set, var_root = (sem(n) for n in ("sum_done", "centred", "sq_done", "var_set", "var_root"))
        ln_scaled, swish_done, cv_hi, cv_lo, h_conv = (sem(n) for n in ("ln_scaled", "swish_done", "cv_hi", "cv_lo", "h_conv"))
        xn_hi_set, xn_lo_set, router_hi_set, router_lo_set = (sem(n) for n in ("xn_hi_set", "xn_lo_set", "router_hi_set", "router_lo_set"))
        logits_done, centred_logits, exp_done, chosen, counted = (sem(n) for n in ("logits_done", "centred_logits", "exp_done", "chosen", "counted"))
        gates_f, gates_hi, gates_lo, tab_ready = (sem(n) for n in ("gates_f", "gates_hi", "gates_lo", "tab_ready"))
        pick_ready, gathered, xg_hi_set, xg_lo_set = (sem(n) for n in ("pick_ready", "gathered", "xg_hi_set", "xg_lo_set"))
        silu_done, gated_done, ht_turned, ht_hi, ht_lo = (sem(n) for n in ("silu_done", "gated_done", "ht_turned", "ht_hi", "ht_lo"))
        slots_turned, pickT_set, gate_col_set = sem("slots_turned"), sem("pickT_set"), sem("gate_col_set")
        y_hi_set, y_lo_set, scattered, h_added = (sem(n) for n in ("y_hi_set", "y_lo_set", "scattered", "h_added"))
        out_ready = sem("out_ready")

        raw_slot = {u: u % RAW_EARLY for u in range(TRUNK_UNITS)}
        trunk_in_slot = [sum(1 for u in raw_slot if raw_slot[u] == s) for s in range(RING)]
        last_trunk_in_slot = [max(u for u in raw_slot if raw_slot[u] == s) for s in range(RAW_EARLY)]

        def raw_at(s):
            return raw[:, s * UNIT:(s + 1) * UNIT]

        def ring_slot(u):
            return u % RING

        def item_base(i):
            return i * ITEM_UNITS + TRUNK_UNITS

        def step_unit(n):
            return 4 + 6 * (n - 1)

        def wait(e, s, value):
            if not isinstance(value, int) or value > 0:
                e.wait_ge(s, value)

        block = ctx.enter_context(nc.Block())

        @block.sync
        def _(sp):
            for t in range(TT):
                sp.dma_start(h[:, t, :], x[t * P:(t + 1) * P, :]).then_inc(x_in[t], 16)
            sp.dma_start(con[:, :], consts).then_inc(con_in, 16)
            sp.dma_start(par[:, :], channel).then_inc(par_in, 16)
            for u in range(TRUNK_UNITS):
                wait(sp, lo_split, u - RAW_EARLY + 1)
                sp.dma_start(raw_at(raw_slot[u]), trunk[u, :, :]).then_inc(landed[raw_slot[u]], 16)
            for j in range(RING):
                if j < RAW_EARLY:
                    sp.wait_ge(lo_split, last_trunk_in_slot[j] + 1)
                if j == RAW_EARLY:
                    sp.wait_ge(cv_lo, 4)
                sp.dma_start(raw_at(j), experts[j, :, :]).then_inc(landed[j], 16)
            with sp.Fori(1, STEPS) as r:
                for j in range(RING):
                    sp.wait_ge(lo_split, r * RING + (TRUNK_UNITS + j - RING + 1))
                    sp.dma_start(raw_at(j), experts[r * RING + j, :, :]).then_inc(landed[j], 16)
            sp.wait_ge(tab_ready, 1)
            n_items = sp.value_load(item_tab[0:1, MAX_ITEMS:MAX_ITEMS + 1], min_val=EXPERTS, max_val=MAX_ITEMS - 1)
            with sp.Fori(1, n_items) as i:
                e = sp.value_load(item_tab[0:1, bass.ds(i, 1)], min_val=0, max_val=EXPERTS - 1)
                with sp.Fori(0, STEPS) as r:
                    for j in range(RING):
                        sp.wait_ge(lo_split, item_base(i) + r * RING + (j - RING + 1))
                        sp.dma_start(raw_at(j), experts[e * ITEM_UNITS + r * RING + j, :, :]).then_inc(landed[j], 16)
            sp.wait_ge(lo_split, item_base(n_items))
            sp.dma_start(raw_at(0)[:, 0:D], norm_final.partition_broadcast(P)).then_inc(g_final_in, 16)
            for t in range(TT):
                sp.wait_ge(out_ready, t + 1)
                sp.dma_start(out[t * P:(t + 1) * P, :], raw_at(1 + t)[:, 0:D]).then_inc(out_written, 16)
            sp.wait_ge(out_written, 16 * TT)

        @block.gpsimd
        def _(pool):
            pool.memset(ones[:, :], 1.0).then_inc(ones_set, 1)
            pool.wait_ge(wsp_in, 16)
            pool.affine_select(out=wsp_sb, in_=wsp_sb, compare_op=ALU.is_ge, fill=0.0, base=0,
                               pattern=[[0, HEADS], [1, P]], channel_multiplier=-1).then_inc(masked, 1)

        @block.scalar
        def _(act):
            done = [0]

            def split_unit(u):
                act.wait_ge(landed[raw_slot[u]], 16 * (u // RAW_EARLY + 1))
                wait(act, w_used, u - RING + 1)
                act.activation(w_hi[:, ring_slot(u), :], raw_at(raw_slot[u]), ACT.Copy).then_inc(hi_split, 1)

            def split_item(i, units):
                for m in units:
                    act.wait_ge(landed[m % RING], i * (16 * STEPS) + 16 * (trunk_in_slot[m % RING] + m // RING + 1))
                    act.wait_ge(w_used, item_base(i) + (m - RING + 1))
                    act.activation(w_hi[:, ring_slot(TRUNK_UNITS + m), :], raw_at(m % RING), ACT.Copy).then_inc(hi_split, 1)

            def splits(until):
                for u in range(done[0], until):
                    if u < TRUNK_UNITS:
                        split_unit(u)
                    else:
                        split_item(0, [u - TRUNK_UNITS])
                done[0] = max(done[0], until)

            def norm_sums(s):
                for t in range(TT):
                    act.activation(xn_hi[:, t, :], h[:, t, :], ACT.Square, accum_out=sums[:, 0, t:t + 1]).then_inc(norm_sq[s], 1)
                act.wait_ge(norm_ms[s], 1)
                act.activation(sums[:, 2, :], sums[:, 1, :], ACT.Sqrt).then_inc(norm_root[s], 1)

            def turned_x_hi(s, col, banks):
                for b in banks:
                    act.wait_ge(turned[s], b + 1)
                    for k in (2 * b, 2 * b + 1):
                        last = act.activation(xT_hi_k[:, k, :], bank[b][:, (k % 2) * SEQ:(k % 2 + 1) * SEQ], ACT.Copy,
                                              scale=par[:, col + k:col + k + 1])
                    last.then_inc(xT_hi_set[s], 1)

            def rstd(t):
                return sums[:, 6, t:t + 1]

            act.wait_ge(par_in, 16)
            turned_x_hi(0, C_NORM_MIX_E, range(2))
            splits(1)
            turned_x_hi(0, C_NORM_MIX_E, range(2, 4))
            splits(2)
            for t in range(TT):
                act.wait_ge(x_in[t], 16)
            norm_sums(0)
            act.dma_start(wsp_sb, w_spatial).then_inc(wsp_in, 16)
            act.dma_start(band_sb, bands).then_inc(band_in, 16)
            act.dma_start(wpool_sb, w_pool).then_inc(wpool_in, 16)
            act.dma_start(gv_sb, sgu_norm.partition_broadcast(P)).then_inc(gv_in, 16)
            splits(6)
            act.wait_ge(w_used, 2)
            act.wait_ge(norm_rstd_set[0], 1)
            for t in range(TT):
                act.activation(u_sb[:, t, :], bank[4 + t][:, :], ACT.Gelu_apprx_tanh, scale=rstd(t)).then_inc(gelu_done, 1)
            splits(8)
            act.wait_ge(w_used, 4)
            for t in range(TT):
                act.activation(v_sb[:, t, :], bank[6 + t][:, :], ACT.Gelu_apprx_tanh, scale=rstd(t)).then_inc(gelu_done, 1)
            for t in range(TT):
                act.wait_ge(gelu_done, 3 + t)
                act.activation(gated[:, t, :], v_sb[:, t, :], ACT.Square, accum_out=sums[:, 3, t:t + 1]).then_inc(v_sq, 1)
            act.wait_ge(v_ms, 1)
            act.activation(sums[:, 5, :], sums[:, 4, :], ACT.Sqrt).then_inc(v_root, 1)
            splits(10)
            act.wait_ge(w_used, 6)
            for t in range(TT):
                act.activation(z_sb[:, t, :], bank[t][:, :], ACT.Copy, scale=rstd(t)).then_inc(z_copied, 1)
            act.wait_ge(v_sq, 2)
            for b in range(2):
                act.wait_ge(pooled, b + 1)
                act.activation(mixedT[:, 2 * b:2 * b + 2, :], bank[4 + b][:, :].rearrange("p (g s) -> p g s", g=2),
                               ACT.Copy).then_inc(pool_copied, 1)
            for b in range(2):
                act.wait_ge(pool_mapped, b + 1)
                for g in (2 * b, 2 * b + 1):
                    last = act.activation(xT_hi_k[:, 4 + g, :], bank[6 + b][:, (g % 2) * SEQ:(g % 2 + 1) * SEQ], ACT.Copy,
                                          scale=par[:, C_POOL_SCALE + g:C_POOL_SCALE + g + 1])
                last.then_inc(cat_hi, 1)
            for b in range(2):
                act.wait_ge(a_turned, b + 1)
                act.activation(xT_hi[:, b * BLK:(b + 1) * BLK], bank[b][:, :], ACT.Copy).then_inc(cat_hi, 1)
            splits(14)
            turned_x_hi(1, C_NORM_FFN_E, range(4))
            act.wait_ge(h_mixed, 4)
            norm_sums(1)
            splits(16)
            act.wait_ge(norm_rstd_set[1], 1)
            for n in range(FFN_BLOCKS + 1):
                nf = BLK if n < FFN_BLOCKS - 1 else BLK // 2
                base = U_FFN + 6 * n
                if n < FFN_BLOCKS:
                    act.wait_ge(ffn_first, 2 * n + 1)
                    wait(act, ffn_gated[0], n)
                    act.activation(act_tmp[:, 0, 0:nf], bank[0][:, 0:nf], ACT.Silu, scale=rstd(0)).then_inc(ffn_silu[0], 1)
                if n >= 1:
                    pf = BLK if n - 1 < FFN_BLOCKS - 1 else BLK // 2
                    act.wait_ge(ffn_turned[1], n)
                    act.activation(hT_hi[:, 1, 0:pf], bank[1][:, 0:pf], ACT.Copy).then_inc(ffn_hi[1], 1)
                if n == FFN_BLOCKS:
                    break
                small = n == FFN_BLOCKS - 1
                splits(base + RING)
                g_end = base + (1 if small else 2)
                act.wait_ge(w_used, g_end)
                wait(act, ffn_gated[1], n)
                act.activation(act_tmp[:, 1, 0:nf], bank[1][:, 0:nf], ACT.Silu, scale=rstd(1)).then_inc(ffn_silu[1], 1)
                act.wait_ge(ffn_turned[0], n + 1)
                act.activation(hT_hi[:, 0, 0:nf], bank[0][:, 0:nf], ACT.Copy).then_inc(ffn_hi[0], 1)
                splits(g_end + RING)
                splits(base + (2 if small else 4) + RING)
            turned_x_hi(2, C_NORM_MIX_O, range(4))
            act.wait_ge(h_ffn, 4)
            norm_sums(2)
            splits(U_PW1 + RING)
            act.wait_ge(norm_rstd_set[2], 1)

            def diagonals(c):
                for k in range(PE_TAPS):
                    q = c * PE_TAPS + k
                    wait(act, diag_used, q - DIAGS + 1)
                    act.activation(diags[:, q % DIAGS, :], ident, ACT.Copy,
                                   scale=par[:, C_W_DW + c * CONV_K + k:C_W_DW + c * CONV_K + k + 1]).then_inc(diag_set, 1)

            for j in range(2):
                u0 = U_PW1 + 4 * j
                act.wait_ge(w_used, u0 + 2)
                wait(act, vg_turned, 4 * j)
                for t in range(TT):
                    act.activation(gated[:, t, :], bank[4 + t][:, :], ACT.Copy, scale=rstd(t)).then_inc(val_copied, 1)
                splits(u0 + 2 + RING)
                act.wait_ge(w_used, u0 + 4)
                for t in range(TT):
                    act.activation(act_tmp[:, t, :], bank[6 + t][:, :], ACT.Copy, scale=rstd(t)).then_inc(gatec_copied, 1)
                for c in range(4 * j, 4 * j + 4):
                    act.wait_ge(vg_turned, c + 1)
                    wait(act, glu_done, c - 3)
                    act.activation(sig[:, c % 4, :], bank[c % 4][:, SEQ:2 * SEQ], ACT.Sigmoid,
                                   bias=par[:, C_B_PW1 + 8 + c:C_B_PW1 + 9 + c]).then_inc(sig_done, 1)
                if j == 0:
                    splits(u0 + 4 + RING)
            for c in range(KT):
                diagonals(c)
            act.dma_start(act_tmp[0:1, :, :].rearrange("p t s -> p (t s)"), b_pw2).then_inc(b_pw2_in, 16)
            for q in range(2):
                act.wait_ge(centred, q + 1)
                act.activation(squares[:, 4 * q:4 * q + 4, :], yc[:, 4 * q:4 * q + 4, :], ACT.Square).then_inc(sq_done, 1)
            act.wait_ge(var_set, 1)
            act.activation(rstd_sb, rstd_sb, ACT.Sqrt).then_inc(var_root, 1)
            for q in range(2):
                act.wait_ge(ln_scaled, q + 1)
                for c in range(4 * q, 4 * q + 4):
                    act.activation(yc[:, c, :], yc[:, c, :], ACT.Silu, bias=par[:, C_LN_B + c:C_LN_B + c + 1],
                                   scale=par[:, C_LN_G + c:C_LN_G + c + 1]).then_inc(swish_done, 1)
                for c in range(4 * q, 4 * q + 4, 2):
                    act.wait_ge(swish_done, c + 2)
                    act.activation(xT_hi_k[:, c:c + 2, :], yc[:, c:c + 2, :], ACT.Copy).then_inc(cv_hi, 1)
            act.activation(router_hi[:, :], par[:, C_ROUTER:C_ROUTER + KT * EXPERTS], ACT.Copy).then_inc(router_hi_set, 1)
            splits(TRUNK_UNITS + 2)
            turned_x_hi(3, C_NORM_FFN_O, range(4))
            act.wait_ge(h_conv, 4)
            norm_sums(3)
            act.wait_ge(norm_rstd_set[3], 1)
            for t in range(TT):
                act.activation(xn_hi[:, t, :], h[:, t, :], ACT.Copy, scale=rstd(t)).then_inc(xn_hi_set, 1)
            splits(TRUNK_UNITS + RING)

            def turned_hi(i, n):
                act.wait_ge(ht_turned, i * STEPS + (n + 1))
                act.activation(hT_hi[:, 0, :], bank[2][:, :], ACT.Copy).then_inc(ht_hi, 1)

            def silu(i, n, unit_end):
                act.wait_ge(w_used, item_base(i) + unit_end)
                wait(act, gated_done, i * STEPS + n)
                act.activation(act_tmp[:, 0, :], bank[0][:, :], ACT.Silu).then_inc(silu_done, 1)

            def weighted_hi(i):
                act.wait_ge(w_used, item_base(i + 1))
                act.wait_ge(gate_col_set, i + 1)
                for c in range(2):
                    act.activation(y_hi[:, c * BLK:(c + 1) * BLK], bank[3 + c][:, :], ACT.Copy,
                                   scale=gate_col[:, 0:1]).then_inc(y_hi_set, 1)

            def item(i, first):
                if not first:
                    split_item(i, range(0, 2))
                    turned_hi(i - 1, STEPS - 1)
                    split_item(i, range(2, 4))
                for b in range(2):
                    act.wait_ge(gathered, 2 * i + (b + 1))
                    for k in range(4 * b, 4 * b + 4):
                        last = act.activation(xg_hi[:, k, :], bank[5 + b][:, (k % 4) * P:(k % 4 + 1) * P], ACT.Copy,
                                              scale=par[:, C_NORM_FFN_O + k:C_NORM_FFN_O + k + 1])
                    last.then_inc(xg_hi_set, 1)
                if not first:
                    weighted_hi(i - 1)
                    split_item(i, range(4, 6))
                else:
                    act.wait_ge(centred_logits, 1)
                    act.activation(route[:, 2, :, :], route[:, 1, :, :], ACT.Exp).then_inc(exp_done, 1)
                    act.wait_ge(gates_f, 1)
                    act.activation(gate_parts[:, :, :, 0], gate_item[:, :, :], ACT.Copy).then_inc(gates_hi, 1)
                silu(i, 0, 2)
                split_item(i, range(6, 10))
                silu(i, 1, step_unit(1) + 2)
                turned_hi(i, 0)
                split_item(i, range(10, 16))
                act.wait_ge(slots_turned, i + 1)
                act.activation(pickT[:, :], bank[5][:, P:P + SEQ], ACT.Copy).then_inc(pickT_set, 1)
                with act.Fori(2, STEPS - 1) as n:
                    act.wait_ge(w_used, item_base(i) + n * 6)
                    act.wait_ge(gated_done, i * STEPS + n)
                    act.activation(act_tmp[:, 0, :], bank[0][:, :], ACT.Silu).then_inc(silu_done, 1)
                    act.wait_ge(ht_turned, i * STEPS + n)
                    act.activation(hT_hi[:, 0, :], bank[2][:, :], ACT.Copy).then_inc(ht_hi, 1)
                    for j in range(RING):
                        m = 10 - 6 + j
                        s = m % RING
                        act.wait_ge(landed[s], i * (16 * STEPS) + n * 16 + 16 * (trunk_in_slot[s] + m // RING + 1))
                        act.wait_ge(w_used, item_base(i) + n * 6 + (m - RING + 1))
                        act.activation(w_hi[:, ring_slot(TRUNK_UNITS + m), :], raw_at(s), ACT.Copy).then_inc(hi_split, 1)
                silu(i, STEPS - 1, step_unit(STEPS - 1) + 2)
                turned_hi(i, STEPS - 2)
                split_item(i, range(ITEM_UNITS - 2, ITEM_UNITS))

            item(0, True)
            act.wait_ge(tab_ready, 1)
            n_items = act.value_load(item_tab[0:1, MAX_ITEMS:MAX_ITEMS + 1], min_val=EXPERTS, max_val=MAX_ITEMS - 1)
            last_item = act.value_load(item_tab[0:1, MAX_ITEMS + 1:MAX_ITEMS + 2], min_val=EXPERTS - 1, max_val=MAX_ITEMS - 2)
            with act.Fori(1, n_items) as i:
                item(i, False)
            turned_hi(last_item, STEPS - 1)
            weighted_hi(last_item)
            act.wait_ge(h_added, n_items * 4)
            for t in range(TT):
                act.activation(raw_at(1 + t)[:, 0:D], h[:, t, :], ACT.Square, accum_out=sums[:, 0, t:t + 1]).then_inc(norm_sq[4], 1)
            act.wait_ge(norm_ms[4], 1)
            act.activation(sums[:, 2, :], sums[:, 1, :], ACT.Sqrt).then_inc(norm_root[4], 1)

        @block.vector
        def _(dve):
            done = [0]
            steps = [0]

            def link(ins):
                steps[0] += 1
                ins.then_inc(dve_step, 1)
                dve.wait_ge(dve_step, steps[0])

            def split_unit(u):
                dve.wait_ge(hi_split, u + 1)
                s = ring_slot(u)
                dve.tensor_tensor(w_lo[:, s, :], raw_at(raw_slot[u]), w_hi[:, s, :].bitcast(F32), ALU.subtract).then_inc(lo_split, 1)

            def split_item(i, units):
                for m in units:
                    s = ring_slot(TRUNK_UNITS + m)
                    dve.wait_ge(hi_split, item_base(i) + (m + 1))
                    dve.tensor_tensor(w_lo[:, s, :], raw_at(m % RING), w_hi[:, s, :].bitcast(F32), ALU.subtract).then_inc(lo_split, 1)

            def splits(until):
                for u in range(done[0], until):
                    if u < TRUNK_UNITS:
                        split_unit(u)
                    else:
                        split_item(0, [u - TRUNK_UNITS])
                done[0] = max(done[0], until)

            def norm_rstd(s):
                dve.wait_ge(norm_sq[s], TT)
                dve.tensor_scalar(sums[:, 1, :], sums[:, 0, :], 1.0 / D, EPS, ALU.mult, ALU.add).then_inc(norm_ms[s], 1)
                dve.wait_ge(norm_root[s], 1)
                dve.reciprocal(sums[:, 6, :], sums[:, 2, :]).then_inc(norm_rstd_set[s], 1)

            def turned_x_lo(s, col, banks):
                for b in banks:
                    dve.wait_ge(xT_hi_set[s], b + 1)
                    for k in (2 * b, 2 * b + 1):
                        last = dve.scalar_tensor_tensor(out=xT_lo_k[:, k, :], in0=bank[b][:, (k % 2) * SEQ:(k % 2 + 1) * SEQ],
                                                        scalar=par[:, col + k:col + k + 1], in1=xT_hi_k[:, k, :].bitcast(F32),
                                                        op0=ALU.mult, op1=ALU.subtract)
                    last.then_inc(xT_lo_set[s], 1)

            dve.wait_ge(par_in, 16)
            turned_x_lo(0, C_NORM_MIX_E, range(2))
            splits(1)
            turned_x_lo(0, C_NORM_MIX_E, range(2, 4))
            splits(2)
            norm_rstd(0)
            splits(6)
            splits(8)
            dve.wait_ge(v_sq, TT)
            dve.tensor_scalar(sums[:, 4, :], sums[:, 3, :], 1.0 / BLK, EPS, ALU.mult, ALU.add).then_inc(v_ms, 1)
            dve.wait_ge(v_root, 1)
            link(dve.reciprocal(sums[:, 7, :], sums[:, 5, :]))
            dve.wait_ge(gv_in, 16)
            for t in range(TT):
                dve.scalar_tensor_tensor(out=v_sb[:, t, :], in0=v_sb[:, t, :], scalar=sums[:, 7, t:t + 1], in1=gv_sb,
                                         op0=ALU.mult, op1=ALU.mult).then_inc(v_normed, 1)
            splits(10)
            for t in range(TT):
                dve.wait_ge(mixed, t + 1)
                for hd in range(HEADS):
                    cols = slice(hd * HEAD_DIM, (hd + 1) * HEAD_DIM)
                    last = dve.scalar_tensor_tensor(out=u_sb[:, t, cols], in0=bank[2 + t][:, cols],
                                                    scalar=par[:, C_B_SPATIAL + hd:C_B_SPATIAL + hd + 1], in1=u_sb[:, t, cols],
                                                    op0=ALU.add, op1=ALU.mult)
                last.then_inc(a_gated, 1)
            for b in range(2):
                dve.wait_ge(cat_hi, b + 1)
                for g in (2 * b, 2 * b + 1):
                    last = dve.scalar_tensor_tensor(out=xT_lo_k[:, 4 + g, :], in0=bank[6 + b][:, (g % 2) * SEQ:(g % 2 + 1) * SEQ],
                                                    scalar=par[:, C_POOL_SCALE + g:C_POOL_SCALE + g + 1],
                                                    in1=xT_hi_k[:, 4 + g, :].bitcast(F32), op0=ALU.mult, op1=ALU.subtract)
                last.then_inc(cat_lo, 1)
            for b in range(2):
                dve.wait_ge(cat_hi, 2 + b + 1)
                dve.tensor_tensor(xT_lo[:, b * BLK:(b + 1) * BLK], bank[b][:, :], xT_hi[:, b * BLK:(b + 1) * BLK].bitcast(F32),
                                  ALU.subtract).then_inc(cat_lo, 1)
            splits(12)

            def add_to_h(c, t, b, s):
                dve.tensor_tensor(h[:, t, c * BLK:(c + 1) * BLK], bank[b][:, :], h[:, t, c * BLK:(c + 1) * BLK],
                                  ALU.add).then_inc(s, 1)

            for c in range(2):
                dve.wait_ge(w_used, U_OUT + 2 * c + 2)
                for t in range(TT):
                    add_to_h(c, t, 2 + 2 * c + t, h_mixed)
                if c == 0:
                    turned_x_lo(1, C_NORM_FFN_E, range(2))
                    splits(14)
            turned_x_lo(1, C_NORM_FFN_E, range(2, 4))
            norm_rstd(1)
            splits(16)
            for n in range(FFN_BLOCKS + 1):
                nf = BLK if n < FFN_BLOCKS - 1 else BLK // 2
                base = U_FFN + 6 * n
                if n >= 1:
                    pf = BLK if n - 1 < FFN_BLOCKS - 1 else BLK // 2
                    dve.wait_ge(ffn_hi[1], n)
                    dve.tensor_tensor(hT_lo[:, 1, 0:pf], bank[1][:, 0:pf], hT_hi[:, 1, 0:pf].bitcast(F32), ALU.subtract).then_inc(ffn_lo[1], 1)
                if n == FFN_BLOCKS:
                    break
                small = n == FFN_BLOCKS - 1
                dve.wait_ge(ffn_first, 2 * n + 2)
                dve.wait_ge(ffn_silu[0], n + 1)
                dve.scalar_tensor_tensor(out=gated[:, 0, 0:nf], in0=bank[2][:, 0:nf], scalar=sums[:, 6, 0:1], in1=act_tmp[:, 0, 0:nf],
                                         op0=ALU.mult, op1=ALU.mult).then_inc(ffn_gated[0], 1)
                splits(base + RING)
                dve.wait_ge(ffn_hi[0], n + 1)
                dve.tensor_tensor(hT_lo[:, 0, 0:nf], bank[0][:, 0:nf], hT_hi[:, 0, 0:nf].bitcast(F32), ALU.subtract).then_inc(ffn_lo[0], 1)
                splits(base + (1 if small else 2) + RING)
                u_end = base + (2 if small else 4)
                dve.wait_ge(w_used, u_end)
                dve.wait_ge(ffn_silu[1], n + 1)
                dve.scalar_tensor_tensor(out=gated[:, 1, 0:nf], in0=bank[3][:, 0:nf], scalar=sums[:, 6, 1:2], in1=act_tmp[:, 1, 0:nf],
                                         op0=ALU.mult, op1=ALU.mult).then_inc(ffn_gated[1], 1)
                splits(u_end + RING)
            for t in range(TT):
                if t == 0:
                    dve.wait_ge(ffn_down0, 1)
                else:
                    dve.wait_ge(w_used, U_PW1)
                for c in range(2):
                    add_to_h(c, t, 4 + 2 * t + c, h_ffn)
            turned_x_lo(2, C_NORM_MIX_O, range(4))
            norm_rstd(2)
            link(dve.memset(xc[:, :, 0:CONV_K - 1], 0.0))
            splits(U_PW1 + RING)
            taps = [0]

            def conv(c0):
                for k in range(PE_TAPS, CONV_K):
                    for c in range(c0, c0 + 4):
                        w = par[:, C_W_DW + c * CONV_K + k:C_W_DW + c * CONV_K + k + 1]
                        if k == PE_TAPS:
                            ins = dve.tensor_scalar(yc[:, c, :], xc[:, c, k:k + SEQ], w, par[:, C_B_DW + c:C_B_DW + c + 1],
                                                    ALU.mult, ALU.add)
                        else:
                            dve.wait_ge(conv_step, taps[0] - 3)
                            ins = dve.scalar_tensor_tensor(out=yc[:, c, :], in0=xc[:, c, k:k + SEQ], scalar=w,
                                                           in1=yc[:, c, :], op0=ALU.mult, op1=ALU.add)
                        ins.then_inc(conv_step, 1)
                        taps[0] += 1
                    if c0 > 0 and k == CONV_K - 3:
                        merge(range(4))

            def merge(tiles):
                for c in tiles:
                    dve.wait_ge(diag_used, (c + 1) * PE_TAPS)
                    dve.wait_ge(conv_step, 4 * (CONV_K - PE_TAPS) * (c // 4 + 1))
                    dve.tensor_tensor(yc[:, c, :], bank[(4 + c) % 8][:, 0:SEQ], yc[:, c, :], ALU.add).then_inc(conv_merged, 1)

            splits(U_PW1 + 2 + RING)
            for j in range(2):
                for c in range(4 * j, 4 * j + 4):
                    dve.wait_ge(sig_done, c + 1)
                    dve.scalar_tensor_tensor(out=xc[:, c, CONV_K - 1:CONV_K - 1 + SEQ], in0=bank[c % 4][:, 0:SEQ],
                                             scalar=par[:, C_B_PW1 + c:C_B_PW1 + c + 1], in1=sig[:, c % 4, :],
                                             op0=ALU.add, op1=ALU.mult).then_inc(glu_done, 1)
                if j == 0:
                    splits(U_PW1 + 4 + RING)
                dve.wait_ge(glu_done, 4 * j + 4)
                if j == 1:
                    splits(TRUNK_UNITS)
                conv(4 * j)
            merge(range(4, KT))
            dve.wait_ge(sum_done, 1)
            link(dve.tensor_scalar(mean_sb, bank[4][:, 0:SEQ], 1.0 / D, None, ALU.mult))
            dve.wait_ge(conv_merged, KT)
            for q in range(2):
                dve.tensor_tensor(yc[:, 4 * q:4 * q + 4, :], yc[:, 4 * q:4 * q + 4, :],
                                  mean_sb.unsqueeze(1).broadcast_to([P, 4, SEQ]), ALU.subtract).then_inc(centred, 1)
            dve.wait_ge(sum_done, 2)
            dve.tensor_scalar(rstd_sb, bank[5][:, 0:SEQ], 1.0 / D, EPS, ALU.mult, ALU.add).then_inc(var_set, 1)
            dve.wait_ge(var_root, 1)
            link(dve.reciprocal(mean_sb, rstd_sb))
            dve.wait_ge(centred, 2)
            for q in range(2):
                dve.tensor_tensor(yc[:, 4 * q:4 * q + 4, :], yc[:, 4 * q:4 * q + 4, :],
                                  mean_sb.unsqueeze(1).broadcast_to([P, 4, SEQ]), ALU.mult).then_inc(ln_scaled, 1)
            for c in range(0, KT, 2):
                dve.wait_ge(cv_hi, c // 2 + 1)
                dve.tensor_tensor(xT_lo_k[:, c:c + 2, :], yc[:, c:c + 2, :], xT_hi_k[:, c:c + 2, :].bitcast(F32),
                                  ALU.subtract).then_inc(cv_lo, 1)
            splits(TRUNK_UNITS + 2)
            dve.wait_ge(router_hi_set, 1)
            dve.tensor_tensor(router_lo[:, :], par[:, C_ROUTER:C_ROUTER + KT * EXPERTS], router_hi[:, :].bitcast(F32),
                              ALU.subtract).then_inc(router_lo_set, 1)
            dve.wait_ge(h_ffn, 4)
            for c in range(2):
                dve.wait_ge(w_used, U_PW2 + 2 * c + 2)
                for t in range(TT):
                    add_to_h(c, t, (6, 7, 2, 3)[2 * c + t], h_conv)
                turned_x_lo(3, C_NORM_FFN_O, range(2 * c, 2 * c + 2))
            norm_rstd(3)
            dve.wait_ge(norm_rstd_set[3], 1)
            for t in range(TT):
                dve.wait_ge(xn_hi_set, t + 1)
                dve.scalar_tensor_tensor(out=xn_lo[:, t, :], in0=h[:, t, :], scalar=sums[:, 6, t:t + 1], in1=xn_hi[:, t, :].bitcast(F32),
                                         op0=ALU.mult, op1=ALU.subtract).then_inc(xn_lo_set, 1)
            dve.wait_ge(logits_done, 1)
            for t in range(TT):
                last = dve.tensor_scalar(logits[:, t, :], bank[6 - 2 * t][:, t * EXPERTS:(t + 1) * EXPERTS], sums[:, 6, t:t + 1], None, ALU.mult)
            link(last)
            other = logits.unsqueeze(2).broadcast_to([P, TT, EXPERTS, EXPERTS])
            own = logits.unsqueeze(3).broadcast_to([P, TT, EXPERTS, EXPERTS])
            dve.tensor_tensor(ahead[:, :, :, 0:EXPERTS], other, own, ALU.is_gt)
            link(dve.tensor_tensor(ahead[:, :, :, EXPERTS:], other, own, ALU.is_equal))
            link(dve.tensor_tensor(ahead[:, :, :, EXPERTS:], ahead[:, :, :, EXPERTS:],
                                   tie.unsqueeze(1).broadcast_to([P, TT, EXPERTS, EXPERTS]), ALU.mult))
            link(dve.tensor_reduce(route[:, 0, :, :], ahead, AX.X, ALU.add))
            sel = route[:, 3, :, :]
            dve.tensor_scalar(sel, route[:, 0, :, :], 2.0, None, ALU.is_lt).then_inc(chosen, 1)
            splits(TRUNK_UNITS + 3)
            place = pos_item[:, 0:EXPERTS, :].rearrange("p e t -> p t e")
            over = route[:, 7, 0, :]
            dve.wait_ge(chosen, 1)
            dve.wait_ge(counted, 1)
            link(dve.scalar_tensor_tensor(out=place, in0=bank[5][:, 0:TT * EXPERTS].rearrange("p (t e) -> p t e", t=TT),
                                          scalar=float(SLOT_BASE), in1=sel, op0=ALU.add, op1=ALU.mult))
            link(dve.tensor_scalar(over, bank[5][:, TT * EXPERTS:(TT + 1) * EXPERTS], float(P), None, ALU.is_gt))

            def build_pick(i, where):
                for t in range(TT):
                    last = dve.tensor_scalar(pick[:, t, :], slots, where[:, t:t + 1], None, ALU.is_equal)
                last.then_inc(pick_ready, 1)

            build_pick(0, pos_item[:, 0, :])
            splits(TRUNK_UNITS + 5)

            def tables():
                link(dve.tensor_reduce(sums[:, 3, :], logits[:, :, :], AX.X, ALU.max))
                dve.tensor_tensor(route[:, 1, :, :], logits[:, :, :], sums[:, 3, :].unsqueeze(2).broadcast_to([P, TT, EXPERTS]),
                                  ALU.subtract).then_inc(centred_logits, 1)
                up_to, before_over = route[:, 0, 1, :], route[:, 7, 1, :]
                all_of_them = [P, OVERFLOWS, EXPERTS]
                link(dve.tensor_tensor_scan(up_to, ones[:, 0:EXPERTS], over, 0.0, ALU.mult, ALU.add))
                link(dve.tensor_tensor(before_over, up_to, over, ALU.subtract))
                link(dve.tensor_tensor(taken, before_over.unsqueeze(1).broadcast_to(all_of_them),
                                       expert_no[:, 0:OVERFLOWS].unsqueeze(2).broadcast_to(all_of_them), ALU.is_equal))
                link(dve.tensor_tensor(taken, taken, over.unsqueeze(1).broadcast_to(all_of_them), ALU.mult))
                dve.tensor_tensor(taken_no, taken, expert_no.unsqueeze(1).broadcast_to(all_of_them), ALU.mult)
                by_tile = [P, OVERFLOWS, TT, EXPERTS]
                dve.tensor_tensor(taken_place, taken.unsqueeze(2).broadcast_to(by_tile), place.unsqueeze(1).broadcast_to(by_tile), ALU.mult)
                dve.memset(pos_item[:, EXPERTS:, :], 0.0)
                dve.memset(gate_item[:, EXPERTS:, :], 0.0)
                dve.tensor_copy(item_f[:, 0:EXPERTS], expert_no)
                link(dve.memset(item_f[:, EXPERTS:], 0.0))
                for q in range(2):
                    dve.tensor_scalar(item_f[:, MAX_ITEMS + q:MAX_ITEMS + q + 1], up_to[:, EXPERTS - 1:EXPERTS],
                                      float(EXPERTS - q), None, ALU.add)
                dve.tensor_reduce(item_f[:, EXPERTS:EXPERTS + OVERFLOWS], taken_no, AX.X, ALU.add)
                link(dve.tensor_reduce(pos_item[:, EXPERTS:EXPERTS + OVERFLOWS, :], taken_place, AX.X, ALU.add))
                dve.tensor_copy(item_tab[:, :], item_f[0:1, :]).then_inc(tab_ready, 1)
                dve.tensor_scalar(pos_item[:, EXPERTS:, :], pos_item[:, EXPERTS:, :], -float(P), None, ALU.add)
                gates = gate_item[:, 0:EXPERTS, :].rearrange("p e t -> p t e")
                dve.wait_ge(exp_done, 1)
                link(dve.tensor_tensor(route[:, 4, :, :], route[:, 2, :, :], sel, ALU.mult))
                link(dve.tensor_reduce(sums[:, 4, :], route[:, 4, :, :], AX.X, ALU.add))
                link(dve.reciprocal(sums[:, 5, :], sums[:, 4, :]))
                link(dve.tensor_tensor(gates, route[:, 4, :, :], sums[:, 5, :].unsqueeze(2).broadcast_to([P, TT, EXPERTS]), ALU.mult))
                link(dve.tensor_tensor(taken_gate, taken.unsqueeze(2).broadcast_to(by_tile), gates.unsqueeze(1).broadcast_to(by_tile), ALU.mult))
                dve.tensor_reduce(gate_item[:, EXPERTS:EXPERTS + OVERFLOWS, :], taken_gate, AX.X, ALU.add).then_inc(gates_f, 1)
                dve.wait_ge(gates_hi, 1)
                dve.tensor_tensor(gate_parts[:, :, :, 1], gate_item[:, :, :], gate_parts[:, :, :, 0].bitcast(F32),
                                  ALU.subtract).then_inc(gates_lo, 1)

            def turned_lo(i, n):
                dve.wait_ge(ht_hi, i * STEPS + (n + 1))
                dve.tensor_tensor(hT_lo[:, 0, :], bank[2][:, :], hT_hi[:, 0, :].bitcast(F32), ALU.subtract).then_inc(ht_lo, 1)

            def gate_up(i, n, unit_end):
                dve.wait_ge(w_used, item_base(i) + unit_end)
                dve.wait_ge(silu_done, i * STEPS + (n + 1))
                dve.tensor_tensor(gated[:, 0, :], bank[1][:, :], act_tmp[:, 0, :], ALU.mult).then_inc(gated_done, 1)

            def weighted_lo(i):
                for c in range(2):
                    dve.wait_ge(y_hi_set, 2 * i + (c + 1))
                    dve.scalar_tensor_tensor(out=y_lo[:, c * BLK:(c + 1) * BLK], in0=bank[3 + c][:, :], scalar=gate_col[:, 0:1],
                                             in1=y_hi[:, c * BLK:(c + 1) * BLK].bitcast(F32), op0=ALU.mult, op1=ALU.subtract).then_inc(y_lo_set, 1)

            def add_item(i):
                wait(dve, h_added, 4 * i)
                for q in range(4):
                    dve.wait_ge(scattered, 4 * i + (q + 1))
                    add_to_h(q % 2, q // 2, (5, 6, 7, 2)[q], h_added)

            def item(i, first):
                if not first:
                    split_item(i, range(0, 2))
                    turned_lo(i - 1, STEPS - 1)
                    split_item(i, range(2, 4))
                for b in range(2):
                    dve.wait_ge(xg_hi_set, 2 * i + (b + 1))
                    for k in range(4 * b, 4 * b + 4):
                        last = dve.scalar_tensor_tensor(out=xg_lo[:, k, :], in0=bank[5 + b][:, (k % 4) * P:(k % 4 + 1) * P],
                                                        scalar=par[:, C_NORM_FFN_O + k:C_NORM_FFN_O + k + 1],
                                                        in1=xg_hi[:, k, :].bitcast(F32), op0=ALU.mult, op1=ALU.subtract)
                    last.then_inc(xg_lo_set, 1)
                if not first:
                    weighted_lo(i - 1)
                    split_item(i, range(4, 6))
                else:
                    splits(TRUNK_UNITS + RING)
                    tables()
                split_item(i, range(6, 8))
                if not first:
                    add_item(i - 1)
                gate_up(i, 0, 4)
                split_item(i, range(8, 10))
                turned_lo(i, 0)
                split_item(i, range(10, 12))
                gate_up(i, 1, step_unit(1) + 4)
                split_item(i, range(12, 16))
                dve.wait_ge(pickT_set, i + 1)
                dve.tensor_reduce(gate_col[:, :], bank[5][:, 0:2], AX.X, ALU.add).then_inc(gate_col_set, 1)
                build_pick(i + 1, pos_item[:, 1, :] if first else pos_item[:, bass.ds(i + 1, 1), :].rearrange("p o t -> p (o t)"))
                with dve.Fori(2, STEPS - 1) as n:
                    dve.wait_ge(ht_hi, i * STEPS + n)
                    dve.tensor_tensor(hT_lo[:, 0, :], bank[2][:, :], hT_hi[:, 0, :].bitcast(F32), ALU.subtract).then_inc(ht_lo, 1)
                    for j in range(RING):
                        if j == 2:
                            dve.wait_ge(w_used, item_base(i) + n * 6 + 2)
                            dve.wait_ge(silu_done, i * STEPS + n + 1)
                            dve.tensor_tensor(gated[:, 0, :], bank[1][:, :], act_tmp[:, 0, :], ALU.mult).then_inc(gated_done, 1)
                        m = 10 - 6 + j
                        s = ring_slot(TRUNK_UNITS + m)
                        dve.wait_ge(hi_split, item_base(i) + n * 6 + (m + 1))
                        dve.tensor_tensor(w_lo[:, s, :], raw_at(m % RING), w_hi[:, s, :].bitcast(F32), ALU.subtract).then_inc(lo_split, 1)
                turned_lo(i, STEPS - 2)
                split_item(i, range(ITEM_UNITS - 2, ITEM_UNITS))
                gate_up(i, STEPS - 1, step_unit(STEPS - 1) + 4)

            item(0, True)
            dve.wait_ge(tab_ready, 1)
            n_items = dve.value_load(item_tab[0:1, MAX_ITEMS:MAX_ITEMS + 1], min_val=EXPERTS, max_val=MAX_ITEMS - 1)
            last_item = dve.value_load(item_tab[0:1, MAX_ITEMS + 1:MAX_ITEMS + 2], min_val=EXPERTS - 1, max_val=MAX_ITEMS - 2)
            with dve.Fori(1, n_items) as i:
                item(i, False)
            turned_lo(last_item, STEPS - 1)
            weighted_lo(last_item)
            add_item(last_item)
            dve.wait_ge(norm_sq[4], TT)
            dve.tensor_scalar(sums[:, 1, :], sums[:, 0, :], 1.0 / D, EPS, ALU.mult, ALU.add).then_inc(norm_ms[4], 1)
            dve.wait_ge(norm_root[4], 1)
            link(dve.reciprocal(sums[:, 6, :], sums[:, 2, :]))
            dve.wait_ge(g_final_in, 16)
            for t in range(TT):
                dve.scalar_tensor_tensor(out=raw_at(1 + t)[:, 0:D], in0=h[:, t, :], scalar=sums[:, 6, t:t + 1], in1=raw_at(0)[:, 0:D],
                                         op0=ALU.mult, op1=ALU.mult).then_inc(out_ready, 1)

        @block.tensor
        def _(pe):
            def product(dst, a_hi, a_lo, b_hi, b_lo, first, last):
                pe.matmul(dst, a_hi, b_hi, start=first, stop=False)
                pe.matmul(dst, a_hi, b_lo, start=False, stop=False)
                return pe.matmul(dst, a_lo, b_hi, start=False, stop=last)

            def weights(slot, kts, cols):
                return (w_hi[:, slot, :].rearrange("p (k c) -> p k c", k=kts)[:, :, 0:cols],
                        w_lo[:, slot, :].rearrange("p (k c) -> p k c", k=kts)[:, :, 0:cols])

            def columns(units, t, dst, nf=BLK, between=None):
                per = KT // len(units)
                for q, u in enumerate(units):
                    if q == 1 and between:
                        between()
                    pe.wait_ge(lo_split, u + 1)
                    b_hi, b_lo = weights(ring_slot(u), per, nf)
                    for k in range(per):
                        kt = q * per + k
                        toks = slice(t * P, (t + 1) * P)
                        last = product(dst[:, 0:nf], xT_hi_k[:, kt, toks], xT_lo_k[:, kt, toks], b_hi[:, k, :], b_lo[:, k, :],
                                       kt == 0, kt == KT - 1)
                    if t == TT - 1:
                        last.then_inc(w_used, 1)
                return last

            def pair(units, dsts, nf=BLK, between=None, biased=False):
                per = KT // len(units)
                for q, u in enumerate(units):
                    if q == 1 and between:
                        between()
                    pe.wait_ge(lo_split, u + 1)
                    b_hi, b_lo = weights(ring_slot(u), per, nf)
                    for t in range(TT):
                        toks = slice(t * P, (t + 1) * P)
                        for k in range(per):
                            kt = q * per + k
                            last = product(dsts[t][:, 0:nf], xT_hi_k[:, kt, toks], xT_lo_k[:, kt, toks], b_hi[:, k, :],
                                           b_lo[:, k, :], kt == 0 and not biased, kt == KT - 1)
                    last.then_inc(w_used, 1)

            def turn_h(s, kts, toks=range(TT)):
                for k in kts:
                    for t in toks:
                        last = pe.transpose(bank[k // 2][:, (k % 2) * SEQ + t * P:(k % 2) * SEQ + (t + 1) * P],
                                            h[:, t, k * P:(k + 1) * P], ident)
                    if k % 2 == 1 and TT - 1 in toks:
                        last.then_inc(turned[s], 1)

            def turn_rest(s, h_ready):
                pe.wait_ge(h_ready, 4)
                turn_h(s, range(4, 8))
                pe.wait_ge(xT_lo_set[s], 4)

            pe.wait_ge(con_in, 16)
            pe.wait_ge(x_in[0], 16)
            turn_h(0, range(KT), [0])
            pe.wait_ge(x_in[1], 16)
            turn_h(0, range(KT), [1])
            pe.wait_ge(xT_lo_set[0], 2)
            pair([0, 1], bank[4:6], between=lambda: pe.wait_ge(xT_lo_set[0], 4))
            pair([2, 3], bank[6:8])
            pair([4, 5], bank[0:2])
            pe.wait_ge(z_copied, 2)
            pe.wait_ge(gelu_done, 4)
            pe.wait_ge(band_in, 16)
            for g in range(GROUPS):
                chans = slice(g * P, (g + 1) * P)
                o = bank[4 + g // 2][:, (g % 2) * SEQ:(g % 2 + 1) * SEQ]
                pe.matmul(o[:, 0:P], z_sb[:, 0, chans], band_sb[:, g, 0:P], start=True, stop=True)
                pe.matmul(o[:, P:SEQ], z_sb[:, 0, chans], band_sb[:, g, P:2 * P], start=True, stop=False)
                last = pe.matmul(o[:, P:SEQ], z_sb[:, 1, chans], band_sb[:, g, 2 * P:3 * P], start=False, stop=True)
                if g % 2 == 1:
                    last.then_inc(pooled, 1)
            pe.wait_ge(masked, 1)
            for t in range(TT):
                pe.wait_ge(v_normed, t + 1)
                for hd in range(HEADS):
                    cols = slice(hd * HEAD_DIM, (hd + 1) * HEAD_DIM)
                    last = pe.matmul(bank[2 + t][:, cols], wsp_sb[:, hd, :], v_sb[:, t, cols], start=True, stop=True)
                last.then_inc(mixed, 1)
            pe.wait_ge(wpool_in, 16)
            for g in range(GROUPS):
                pe.wait_ge(pool_copied, g // 2 + 1)
                last = pe.matmul(bank[6 + g // 2][:, (g % 2) * SEQ:(g % 2 + 1) * SEQ], wpool_sb[:, g, :], mixedT[:, g, :],
                                 start=True, stop=True)
                if g % 2 == 1:
                    last.then_inc(pool_mapped, 1)
            pe.wait_ge(a_gated, 2)
            for b in range(4):
                for t in range(TT):
                    last = pe.transpose(bank[b // 2][:, (b % 2) * SEQ + t * P:(b % 2) * SEQ + (t + 1) * P],
                                        u_sb[:, t, b * P:(b + 1) * P], ident)
                if b % 2 == 1:
                    last.then_inc(a_turned, 1)
            pe.wait_ge(cat_lo, 4)
            pair([6, 7], bank[2:4])

            def turn_first(s, h_ready):
                pe.wait_ge(h_ready, 2)
                turn_h(s, range(4))

            pair([8, 9], bank[4:6], between=lambda: turn_first(1, h_mixed))
            pe.wait_ge(xT_lo_set[1], 2)

            def turn_hidden(n, t, nf):
                pe.wait_ge(ffn_gated[t], n + 1)
                for f in range(nf // P):
                    last = pe.transpose(bank[t][:, f * P:(f + 1) * P], gated[:, t, f * P:(f + 1) * P], ident)
                last.then_inc(ffn_turned[t], 1)

            def down(n, t, units):
                pe.wait_ge(ffn_lo[t], n + 1)
                for q, u in enumerate(units):
                    pe.wait_ge(lo_split, u + 1)
                    b_hi, b_lo = weights(ring_slot(u), 2, D)
                    for f in range(2):
                        ft = slice((2 * q + f) * P, (2 * q + f + 1) * P)
                        for c in range(2):
                            cols = slice(c * BLK, (c + 1) * BLK)
                            last = product(bank[4 + 2 * t + c][:, :], hT_hi[:, t, ft], hT_lo[:, t, ft], b_hi[:, f, cols], b_lo[:, f, cols],
                                           n == 0 and q == 0 and f == 0, n == FFN_BLOCKS - 1 and f == 1)
                    if t == TT - 1:
                        last.then_inc(w_used, 1)
                if t == 0 and n == FFN_BLOCKS - 1:
                    last.then_inc(ffn_down0, 1)

            def ffn_units(n):
                base = U_FFN + 6 * n
                if n < FFN_BLOCKS - 1:
                    return BLK, [base, base + 1], [base + 2, base + 3], [base + 4, base + 5]
                return BLK // 2, [base], [base + 1], [base + 2]

            for n in range(FFN_BLOCKS):
                nf, gate_u, up_u, down_u = ffn_units(n)
                columns(gate_u, 0, bank[0], nf, between=(lambda: turn_rest(1, h_mixed)) if n == 0 else None).then_inc(ffn_first, 1)
                if n >= 1:
                    pf, _, _, last_down = ffn_units(n - 1)
                    turn_hidden(n - 1, 1, pf)
                columns(up_u, 0, bank[2], nf).then_inc(ffn_first, 1)
                if n >= 1:
                    down(n - 1, 1, last_down)
                columns(gate_u, 1, bank[1], nf)
                turn_hidden(n, 0, nf)
                columns(up_u, 1, bank[3], nf)
                down(n, 0, down_u)
            nf, _, _, down_u = ffn_units(FFN_BLOCKS - 1)
            turn_hidden(FFN_BLOCKS - 1, 1, nf)
            down(FFN_BLOCKS - 1, 1, down_u)
            pe.wait_ge(h_ffn, 2)
            turn_h(2, range(KT), [0])
            for k in range(0, KT, 4):
                pe.wait_ge(h_ffn, 3 + k // 4)
                turn_h(2, range(k, k + 4), [1])
            pe.wait_ge(xT_lo_set[2], 2)
            for j in range(2):
                u0 = U_PW1 + 4 * j
                wait(pe, val_copied, 2 * j)
                pair([u0, u0 + 1], bank[4:6], between=lambda: pe.wait_ge(xT_lo_set[2], 4))
                wait(pe, gatec_copied, 2 * j)
                pair([u0 + 2, u0 + 3], bank[6:8])
                pe.wait_ge(val_copied, 2 * j + 2)
                pe.wait_ge(gatec_copied, 2 * j + 2)
                for c in range(4 * j, 4 * j + 4):
                    wait(pe, glu_done, c - 3)
                    for t in range(TT):
                        pe.transpose(bank[c % 4][:, t * P:(t + 1) * P], gated[:, t, (c % 4) * P:(c % 4 + 1) * P], ident)
                        last = pe.transpose(bank[c % 4][:, SEQ + t * P:SEQ + (t + 1) * P], act_tmp[:, t, (c % 4) * P:(c % 4 + 1) * P], ident)
                    last.then_inc(vg_turned, 1)
            for c in range(KT):
                pe.wait_ge(glu_done, c + 1 if c < 4 else KT)
                for k in range(PE_TAPS):
                    q = c * PE_TAPS + k
                    pe.wait_ge(diag_set, q + 1)
                    pe.matmul(bank[(4 + c) % 8][:, 0:SEQ], diags[:, q % DIAGS, :], xc[:, c, k:k + SEQ],
                              start=k == 0, stop=k == PE_TAPS - 1).then_inc(diag_used, 1)
            pe.wait_ge(ones_set, 1)
            for c in range(KT):
                pe.wait_ge(conv_merged, c + 1)
                last = pe.matmul(bank[4][:, 0:SEQ], ones[:, :], yc[:, c, :], start=c == 0, stop=c == KT - 1)
            last.then_inc(sum_done, 1)
            for c in range(KT):
                pe.wait_ge(sq_done, c // 4 + 1)
                last = pe.matmul(bank[5][:, 0:SEQ], ones[:, :], squares[:, c, :], start=c == 0, stop=c == KT - 1)
            last.then_inc(sum_done, 1)
            pe.wait_ge(b_pw2_in, 16)
            for c in range(2):
                for t in range(TT):
                    pe.matmul(bank[(6, 7, 2, 3)[2 * c + t]][:, :], ones[0:1, :], act_flat[0:1, c * BLK:(c + 1) * BLK],
                              start=True, stop=False)
            pe.wait_ge(cv_lo, 2)
            pair([U_PW2, U_PW2 + 1], bank[6:8], biased=True, between=lambda: pe.wait_ge(cv_lo, 4))
            pair([U_PW2 + 2, U_PW2 + 3], bank[2:4], biased=True, between=lambda: turn_first(3, h_conv))
            pe.wait_ge(router_lo_set, 1)

            def router(k):
                r = slice(k * EXPERTS, (k + 1) * EXPERTS)
                for t in range(TT):
                    toks = slice(t * P, (t + 1) * P)
                    last = product(bank[6 - 2 * t][:, t * EXPERTS:(t + 1) * EXPERTS], xT_hi_k[:, k, toks], xT_lo_k[:, k, toks],
                                   router_hi[:, r], router_lo[:, r], k == 0, k == KT - 1)
                return last

            pe.wait_ge(xT_lo_set[3], 2)
            for k in range(4):
                router(k)
            turn_rest(3, h_conv)
            for k in range(4, KT):
                last = router(k)
            last.then_inc(logits_done, 1)
            pe.wait_ge(chosen, 1)
            sel = route[:, 3, :, :]
            places = bank[5]
            pe.matmul(places[:, 0:EXPERTS], before, sel[:, 0, :], start=True, stop=True)
            pe.matmul(places[:, EXPERTS:2 * EXPERTS], ones[:, :], sel[:, 0, :], start=True, stop=False)
            pe.matmul(places[:, EXPERTS:2 * EXPERTS], before, sel[:, 1, :], start=False, stop=True)
            pe.matmul(places[:, 2 * EXPERTS:3 * EXPERTS], ones[:, :], sel[:, 0, :], start=True, stop=False)
            pe.matmul(places[:, 2 * EXPERTS:3 * EXPERTS], ones[:, :], sel[:, 1, :], start=False, stop=True).then_inc(counted, 1)

            def item_columns(i, m0, dst):
                for q in range(2):
                    pe.wait_ge(lo_split, item_base(i) + (m0 + q + 1))
                    b_hi, b_lo = weights(ring_slot(TRUNK_UNITS + m0 + q), 4, BLK)
                    for k in range(4):
                        kt = q * 4 + k
                        last = product(dst[:, :], xg_hi[:, kt, :], xg_lo[:, kt, :], b_hi[:, k, :], b_lo[:, k, :], kt == 0, kt == KT - 1)
                    last.then_inc(w_used, 1)

            def item_down(i, m0, first, last_step):
                for q in range(2):
                    pe.wait_ge(lo_split, item_base(i) + (m0 + q + 1))
                    b_hi, b_lo = weights(ring_slot(TRUNK_UNITS + m0 + q), 2, D)
                    for f in range(2):
                        ft = slice((2 * q + f) * P, (2 * q + f + 1) * P)
                        for c in range(2):
                            cols = slice(c * BLK, (c + 1) * BLK)
                            last = product(bank[3 + c][:, :], hT_hi[:, 0, ft], hT_lo[:, 0, ft], b_hi[:, f, cols], b_lo[:, f, cols],
                                           first and q == 0 and f == 0, last_step and q == 1 and f == 1)
                    last.then_inc(w_used, 1)

            def item_turn():
                for f in range(BLK // P):
                    last = pe.transpose(bank[2][:, f * P:(f + 1) * P], gated[:, 0, f * P:(f + 1) * P], ident)
                last.then_inc(ht_turned, 1)

            def scatter(i):
                pe.wait_ge(y_lo_set, 2 * i + 2)
                pe.wait_ge(pickT_set, i + 1)
                for q in range(4):
                    t, c = q // 2, q % 2
                    dst = bank[(5, 6, 7, 2)[q]][:, :]
                    cols = slice(c * BLK, (c + 1) * BLK)
                    pe.matmul(dst, pickT[:, t * P:(t + 1) * P], y_hi[:, cols], start=True, stop=False)
                    pe.matmul(dst, pickT[:, t * P:(t + 1) * P], y_lo[:, cols], start=False, stop=True).then_inc(scattered, 1)

            def item(i, first):
                if not first:
                    pe.wait_ge(gated_done, i * STEPS)
                    item_turn()
                else:
                    pe.wait_ge(xn_lo_set, TT)
                pe.wait_ge(pick_ready, i + 1)
                wait(pe, gate_col_set, i)
                for b in range(2):
                    for k in range(4):
                        o = bank[5 + b][:, k * P:(k + 1) * P]
                        chans = slice((4 * b + k) * P, (4 * b + k + 1) * P)
                        for t in range(TT):
                            pe.matmul(o, xn_hi[:, t, chans], pick[:, t, :], start=t == 0, stop=False)
                            last = pe.matmul(o, xn_lo[:, t, chans], pick[:, t, :], start=False, stop=t == TT - 1)
                    last.then_inc(gathered, 1)
                if not first:
                    pe.wait_ge(ht_lo, i * STEPS)
                    item_down(i - 1, ITEM_UNITS - 2, False, True)
                pe.wait_ge(xg_lo_set, 2 * i + 2)
                wait(pe, silu_done, i * STEPS)
                item_columns(i, 0, bank[0])
                if not first:
                    scatter(i - 1)
                wait(pe, gated_done, i * STEPS)
                item_columns(i, 2, bank[1])
                pe.wait_ge(silu_done, i * STEPS + 1)
                item_columns(i, 4, bank[0])
                pe.wait_ge(gated_done, i * STEPS + 1)
                wait(pe, h_added, 4 * i)
                item_turn()
                item_columns(i, 6, bank[1])
                pe.wait_ge(ht_lo, i * STEPS + 1)
                item_down(i, 8, True, False)
                pe.wait_ge(gates_lo, 1)
                for t in range(TT):
                    parts = gate_parts[:, 0, t, :] if first else gate_parts[:, bass.ds(i, 1), t, :].rearrange("p o w -> p (o w)")
                    pe.matmul(bank[5][:, 0:2], pick[:, t, :], parts, start=t == 0, stop=t == TT - 1)
                for t in range(TT):
                    last = pe.transpose(bank[5][:, P + t * P:P + (t + 1) * P], pick[:, t, :].bitcast(F32), ident)
                last.then_inc(slots_turned, 1)
                with pe.Fori(2, STEPS) as n:
                    pe.wait_ge(silu_done, i * STEPS + n)
                    b = item_base(i) + n * 6
                    for q in range(2):
                        pe.wait_ge(lo_split, b + (q - 1))
                        b_hi, b_lo = weights(ring_slot(TRUNK_UNITS + 4 + q), 4, BLK)
                        for k in range(4):
                            kt = q * 4 + k
                            last = product(bank[0][:, :], xg_hi[:, kt, :], xg_lo[:, kt, :], b_hi[:, k, :], b_lo[:, k, :], kt == 0, kt == KT - 1)
                        last.then_inc(w_used, 1)
                    pe.wait_ge(gated_done, i * STEPS + n)
                    item_turn()
                    for q in range(2):
                        pe.wait_ge(lo_split, b + (q + 1))
                        b_hi, b_lo = weights(ring_slot(TRUNK_UNITS + 6 + q), 4, BLK)
                        for k in range(4):
                            kt = q * 4 + k
                            last = product(bank[1][:, :], xg_hi[:, kt, :], xg_lo[:, kt, :], b_hi[:, k, :], b_lo[:, k, :], kt == 0, kt == KT - 1)
                        last.then_inc(w_used, 1)
                    pe.wait_ge(ht_lo, i * STEPS + n)
                    for q in range(2):
                        pe.wait_ge(lo_split, b + (q + 3))
                        b_hi, b_lo = weights(ring_slot(TRUNK_UNITS + 8 + q), 2, D)
                        for f in range(2):
                            ft = slice((2 * q + f) * P, (2 * q + f + 1) * P)
                            for c in range(2):
                                cols = slice(c * BLK, (c + 1) * BLK)
                                last = product(bank[3 + c][:, :], hT_hi[:, 0, ft], hT_lo[:, 0, ft], b_hi[:, f, cols], b_lo[:, f, cols], False, False)
                        last.then_inc(w_used, 1)

            item(0, True)
            pe.wait_ge(tab_ready, 1)
            n_items = pe.value_load(item_tab[0:1, MAX_ITEMS:MAX_ITEMS + 1], min_val=EXPERTS, max_val=MAX_ITEMS - 1)
            last_item = pe.value_load(item_tab[0:1, MAX_ITEMS + 1:MAX_ITEMS + 2], min_val=EXPERTS - 1, max_val=MAX_ITEMS - 2)
            with pe.Fori(1, n_items) as i:
                item(i, False)
            pe.wait_ge(gated_done, n_items * STEPS)
            item_turn()
            pe.wait_ge(ht_lo, n_items * STEPS)
            item_down(last_item, ITEM_UNITS - 2, False, True)
            scatter(last_item)


def col_units(w, nf, halves):
    f = w.shape[1]
    per = KT // halves
    return (w.reshape(halves, per, P, f // nf, nf).transpose(3, 0, 2, 1, 4).reshape(f // nf, halves, P, UNIT))


def row_units(w):
    return w.reshape(-1, 2, P, D).transpose(0, 2, 1, 3).reshape(-1, P, UNIT)


def constants():
    con = np.zeros((P, K_ALL), np.float32)
    con[:, K_IDENT:K_IDENT + P] = np.eye(P)
    s = np.arange(P)
    con[:, K_BEFORE:K_BEFORE + P] = s[:, None] < s[None, :]
    con[:, K_SLOTS:K_SLOTS + P] = SLOT_BASE + s[None, :]
    e = np.arange(EXPERTS)
    con[:, K_TIE:K_TIE + 64] = (e[None, :] < e[:, None]).reshape(1, 64)
    con[:, K_EXPERT:K_EXPERT + EXPERTS] = e[None, :]
    band = np.zeros((P, GROUPS, 3 * P), np.float32)
    t = np.arange(SEQ)
    for g, win in enumerate(WINDOWS):
        lag = t[None, :] - t[:, None]
        b = np.where((lag >= 0) & (lag < win), np.float32(1) / np.minimum(t + 1, win).astype(np.float32)[None, :], np.float32(0))
        b = b - np.eye(SEQ, dtype=np.float32)
        band[:, g, 0:SEQ] = b[0:P, :]
        band[:, g, SEQ:] = b[P:, P:]
    return con, band


def kernel(**inputs):
    import concourse.bacc as _bacc
    from concourse.bass_utils import run_bass_kernel_spmd as _run

    a = {k: np.asarray(v) for k, v in inputs.items()}
    f32 = np.float32

    trunk = np.empty((TRUNK_UNITS, P, UNIT), f32)
    trunk[U_IN:U_OUT] = col_units(a["w_in_e"][0], BLK, 2).reshape(-1, P, UNIT)
    trunk[U_OUT:U_FFN] = col_units(a["w_out_e"][0], BLK, 2).reshape(-1, P, UNIT)
    whole = (FFN_BLOCKS - 1) * BLK
    ffn = trunk[U_FFN:U_FFN + 30].reshape(FFN_BLOCKS - 1, 3, 2, P, UNIT)
    ffn[:, 0] = col_units(a["w_gate_d"][0][:, :whole], BLK, 2)
    ffn[:, 1] = col_units(a["w_up_d"][0][:, :whole], BLK, 2)
    ffn[:, 2] = row_units(a["w_down_d"][0][:whole]).reshape(-1, 2, P, UNIT)
    trunk[U_FFN + 30] = col_units(a["w_gate_d"][0][:, whole:], BLK // 2, 1)[0, 0]
    trunk[U_FFN + 31] = col_units(a["w_up_d"][0][:, whole:], BLK // 2, 1)[0, 0]
    trunk[U_FFN + 32] = row_units(a["w_down_d"][0][whole:])[0]
    pw1 = col_units(a["w_pw1"][0], BLK, 2)
    trunk[U_PW1:U_PW2] = pw1[[0, 2, 1, 3]].reshape(-1, P, UNIT)
    trunk[U_PW2:] = col_units(a["w_pw2"][0], BLK, 2).reshape(-1, P, UNIT)

    experts = np.empty((EXPERTS, ITEM_UNITS, P, UNIT), f32)
    for e in range(EXPERTS):
        g = col_units(a["w_gate_x"][0, e], BLK, 2)
        u = col_units(a["w_up_x"][0, e], BLK, 2)
        d = row_units(a["w_down_x"][0, e]).reshape(STEPS, 2, P, UNIT)
        experts[e, 0:2], experts[e, 2:4] = g[0], u[0]
        for n in range(1, STEPS):
            m = 4 + 6 * (n - 1)
            experts[e, m:m + 2], experts[e, m + 2:m + 4], experts[e, m + 4:m + 6] = g[n], u[n], d[n - 1]
        experts[e, ITEM_UNITS - 2:] = d[STEPS - 1]

    def by_channel(v):
        return v.reshape(-1, P).T

    w_dw = a["w_dw"][0].reshape(CONV_K, KT, P).transpose(2, 1, 0).reshape(P, -1)
    router = a["w_router"][0].reshape(KT, P, EXPERTS).transpose(1, 0, 2).reshape(P, -1)
    channel = np.concatenate([by_channel(a["norm_mix_e"][0]), by_channel(a["norm_ffn_e"][0]), by_channel(a["norm_mix_o"][0]),
                              by_channel(a["pool_scale"][0]), by_channel(a["b_dw"][0]), by_channel(a["ln_g"][0]),
                              by_channel(a["ln_b"][0]), by_channel(a["b_pw1"][0]), a["b_spatial"][0].T, w_dw, router,
                              by_channel(a["norm_ffn_o"][0])], axis=1)
    con, band = constants()
    arrays = {
        "x_in_dram": a["x"][0], "trunk_dram": trunk, "experts_dram": experts.reshape(-1, P, UNIT),
        "channel_dram": channel, "consts_dram": con, "bands_dram": band,
        "w_spatial_dram": a["w_spatial"][0].transpose(2, 0, 1), "w_pool_dram": a["w_pool"][0].transpose(1, 0, 2),
        "sgu_norm_dram": a["sgu_norm"][0], "b_pw2_dram": a["b_pw2"],
        "norm_final_dram": a["norm_final"],
    }
    arrays = {k: np.ascontiguousarray(v) for k, v in arrays.items()}
    nc = _bacc.Bacc("TRN2", target_bir_lowering=False, num_devices=1)
    args = [nc.dram_tensor(k, v.shape, F32, kind="ExternalInput").ap() for k, v in arrays.items()]
    args.append(nc.dram_tensor("out_dram", (SEQ, D), F32, kind="ExternalOutput").ap())
    build(nc, *args)
    r = _run(nc, [arrays], core_ids=[0])
    return r.results[0]["out_dram"].reshape(1, SEQ, D)
```

```python
from contextlib import ExitStack

import numpy as np

import concourse.bass as bass
from concourse import mybir

ALU = mybir.AluOpType
ACT = mybir.ActivationFunctionType
AX = mybir.AxisListType
F32 = mybir.dt.float32
F32R = mybir.dt.float32r
I32 = mybir.dt.int32

P = 128
SEQ = 256
D = 1024
TT = SEQ // P
KT = D // P
HEADS = 8
HEAD_DIM = 64
WINDOWS = (2, 4, 8, 16)
GROUPS = len(WINDOWS)
CONV_K = 31
F_DENSE = 2816
F_EXPERT = 3584
EXPERTS = 8
EPS = 1e-6

UNIT = 2048
BLK = 512
RING = 6
RAW_EARLY = 3

U_IN = 0
U_OUT = U_IN + 6
U_FFN = U_OUT + 4
FFN_BLOCKS = 6
U_PW1 = U_FFN + 33
U_PW2 = U_PW1 + 8
TRUNK_UNITS = U_PW2 + 4
STEPS = F_EXPERT // BLK
ITEM_UNITS = 6 * STEPS
OVERFLOWS = 3
SLOT_BASE = 1000
MAX_ITEMS = 12

PE_TAPS = 13
DIAGS = 8

C_NORM_MIX_E, C_NORM_FFN_E, C_NORM_MIX_O = 0, 8, 16
C_POOL_SCALE, C_B_DW, C_LN_G, C_LN_B = 24, 28, 36, 44
C_B_PW1, C_B_SPATIAL, C_W_DW, C_ROUTER = 52, 68, 76, 76 + 8 * CONV_K
C_ALL = C_ROUTER + KT * EXPERTS
C_NORM_FFN_O = C_ALL
C_ALL += 8
K_IDENT, K_BEFORE, K_SLOTS, K_TIE, K_EXPERT = 0, 128, 256, 384, 448
K_ALL = 456


def build(nc, x, trunk, experts, channel, consts, bands, w_spatial, w_pool, sgu_norm, b_pw2,
          norm_final, out):
    ctx = ExitStack()
    with ctx:
        def sb(name, shape, dt=F32):
            return ctx.enter_context(nc.sbuf_tensor(name, shape, dt))

        def sem(name):
            return ctx.enter_context(nc.semaphore(name))

        raw = sb("raw", [P, RING * UNIT + 256])
        w_hi = sb("w_hi", [P, RING, UNIT], F32R)
        w_lo = sb("w_lo", [P, RING, UNIT], F32R)
        xT_hi = sb("xT_hi", [P, KT * SEQ], F32R)
        xT_lo = sb("xT_lo", [P, KT * SEQ], F32R)
        hT_hi = sb("hT_hi", [P, TT, BLK], F32R)
        hT_lo = sb("hT_lo", [P, TT, BLK], F32R)
        xn_hi = sb("xn_hi", [P, TT, D], F32R)
        xn_lo = sb("xn_lo", [P, TT, D], F32R)
        pick = sb("pick", [P, TT, P], F32R)
        pickT = sb("pickT", [P, SEQ], F32R)
        gate_parts = sb("gate_parts", [P, MAX_ITEMS, TT, 2], F32R)
        router_hi = sb("router_hi", [P, KT * EXPERTS], F32R)
        router_lo = sb("router_lo", [P, KT * EXPERTS], F32R)
        h = sb("h", [P, TT, D])
        gated = sb("gated", [P, TT, BLK])
        act_tmp = sb("act_tmp", [P, TT, BLK])
        par = sb("par", [P, C_ALL])
        con = sb("con", [P, K_ALL])
        ones = sb("ones", [P, P])
        eps = sb("eps", [P, 1])
        sums = sb("sums", [P, 8, TT])
        pos_item = sb("pos_item", [P, MAX_ITEMS, TT])
        gate_col = sb("gate_col", [P, 1])
        item_tab = sb("item_tab", [1, MAX_ITEMS + 4], I32)

        bank = [ctx.enter_context(nc.psum_tensor(f"bank{i}", [P, BLK], F32)) for i in range(8)]

        arena = raw[:, RAW_EARLY * UNIT:]
        u_sb = arena[:, 0:1024].rearrange("p (t d) -> p t d", t=TT)
        v_sb = arena[:, 1024:2048].rearrange("p (t d) -> p t d", t=TT)
        z_sb = arena[:, 2048:3072].rearrange("p (t d) -> p t d", t=TT)
        band_sb = arena[:, 3072:4608].rearrange("p (g s) -> p g s", g=GROUPS)
        wsp_sb = arena[:, 4608:5632].rearrange("p (h s) -> p h s", h=HEADS)
        wpool_sb = arena[:, 5632:6144].rearrange("p (g s) -> p g s", g=GROUPS)
        sig = arena[:, 0:1024].rearrange("p (c s) -> p c s", c=4)
        squares = arena[:, 0:2048].rearrange("p (c s) -> p c s", c=KT)
        diags = arena[:, 1024:1024 + DIAGS * P].rearrange("p (q c) -> p q c", q=DIAGS)
        xc = arena[:, 2048:2048 + KT * (SEQ + CONV_K - 1)].rearrange("p (c s) -> p c s", c=KT)
        yc = arena[:, 4336:4336 + KT * SEQ].rearrange("p (c s) -> p c s", c=KT)
        mean_sb = arena[:, 2048:2048 + SEQ]
        std_sb = arena[:, 2304:2304 + SEQ]
        mixedT = gated[:, :, :].rearrange("p t s -> p (t s)").rearrange("p (g s) -> p g s", g=GROUPS)
        act_flat = act_tmp[:, :, :].rearrange("p t s -> p (t s)")
        gv_sb = act_tmp[:, 0, :]
        tail = raw[:, RING * UNIT:]
        route = tail[:, 0:128].rearrange("p (q t e) -> p q t e", q=8, t=TT)
        logits = tail[:, 128:144].rearrange("p (t e) -> p t e", t=TT)
        ahead = gated[:, 0, 0:256].rearrange("p (t e j) -> p t e j", t=TT, e=EXPERTS)
        taken = gated[:, 0, 256:280].rearrange("p (o e) -> p o e", o=OVERFLOWS)
        taken_no = gated[:, 0, 280:304].rearrange("p (o e) -> p o e", o=OVERFLOWS)
        taken_place = gated[:, 0, 304:352].rearrange("p (o t e) -> p o t e", o=OVERFLOWS, t=TT)
        taken_gate = gated[:, 0, 352:400].rearrange("p (o t e) -> p o t e", o=OVERFLOWS, t=TT)
        item_f = tail[:, 144:144 + MAX_ITEMS + 4]
        gate_item = tail[:, 160:160 + MAX_ITEMS * TT].rearrange("p (i t) -> p i t", t=TT)
        ident = con[:, K_IDENT:K_IDENT + P]
        before = con[:, K_BEFORE:K_BEFORE + P]
        slots = con[:, K_SLOTS:K_SLOTS + P]
        tie = con[:, K_TIE:K_TIE + 64].rearrange("p (e j) -> p e j", e=EXPERTS)
        expert_no = con[:, K_EXPERT:K_EXPERT + EXPERTS]
        xT_hi_k = xT_hi[:, :].rearrange("p (k s) -> p k s", k=KT)
        xT_lo_k = xT_lo[:, :].rearrange("p (k s) -> p k s", k=KT)
        xg_hi = xT_hi[:, 0:KT * P].rearrange("p (k s) -> p k s", k=KT)
        xg_lo = xT_lo[:, 0:KT * P].rearrange("p (k s) -> p k s", k=KT)
        xg_tok = [gated[:, 1, :], act_tmp[:, 1, :]]
        sel_r = pickT[:, 0:TT * EXPERTS].rearrange("p (t e) -> p t e", t=TT)
        before_r, ones_r = pick[:, 0, :], pick[:, 1, :]
        y_hi = xT_hi[:, KT * P:]
        y_lo = xT_lo[:, KT * P:]

        x_in, par_in, con_in = [sem(f"x_in{t}") for t in range(TT)], sem("par_in"), sem("con_in")
        band_in, wsp_in, wpool_in, gv_in = sem("band_in"), sem("wsp_in"), sem("wpool_in"), sem("gv_in")
        b_pw2_in, g_final_in = sem("b_pw2_in"), sem("g_final_in")
        out_written = sem("out_written")
        landed = [sem(f"landed{s}") for s in range(RING)]
        hi_split, lo_split, w_used = sem("hi_split"), sem("lo_split"), sem("w_used")
        eps_set, ones_set, masked = sem("eps_set"), sem("ones_set"), sem("masked")
        norm_sq = [sem(f"norm_sq{s}") for s in range(5)]
        norm_root = [sem(f"norm_root{s}") for s in range(5)]
        norm_rstd_set = [sem(f"norm_rstd_set{s}") for s in range(4)]
        turned = [sem(f"turned{s}") for s in range(4)]
        xT_hi_set = [sem(f"xT_hi_set{s}") for s in range(4)]
        xT_lo_set = [sem(f"xT_lo_set{s}") for s in range(4)]
        dve_step = sem("dve_step")
        gelu_done, v_sq, v_root, v_normed = (sem(n) for n in ("gelu_done", "v_sq", "v_root", "v_normed"))
        z_copied, pooled, pool_copied, pool_mapped = (sem(n) for n in ("z_copied", "pooled", "pool_copied", "pool_mapped"))
        mixed, a_gated, a_turned = sem("mixed"), sem("a_gated"), sem("a_turned")
        cat_hi, cat_lo, h_mixed = sem("cat_hi"), sem("cat_lo"), sem("h_mixed")
        ffn_first = sem("ffn_first")
        ffn_silu = [sem("ffn_silu0"), sem("ffn_silu1")]
        ffn_gated = [sem("ffn_gated0"), sem("ffn_gated1")]
        ffn_turned = [sem("ffn_turned0"), sem("ffn_turned1")]
        ffn_hi = [sem("ffn_hi0"), sem("ffn_hi1")]
        ffn_lo = [sem("ffn_lo0"), sem("ffn_lo1")]
        ffn_down0 = sem("ffn_down0")
        h_ffn = sem("h_ffn")
        val_copied, gatec_copied, vg_turned = sem("val_copied"), sem("gatec_copied"), sem("vg_turned")
        sig_done, glu_done, conv_step = sem("sig_done"), sem("glu_done"), sem("conv_step")
        diag_set, diag_used, conv_merged = (sem(n) for n in ("diag_set", "diag_used", "conv_merged"))
        sum_done, centred, sq_done, sq_added, var_root = (sem(n) for n in ("sum_done", "centred", "sq_done", "sq_added", "var_root"))
        ln_scaled, swish_done, cv_hi, cv_lo, h_conv = (sem(n) for n in ("ln_scaled", "swish_done", "cv_hi", "cv_lo", "h_conv"))
        xn_hi_set, xn_lo_set, router_hi_set, router_lo_set = (sem(n) for n in ("xn_hi_set", "xn_lo_set", "router_hi_set", "router_lo_set"))
        logits_done, centred_logits, exp_done, chosen, counted = (sem(n) for n in ("logits_done", "centred_logits", "exp_done", "chosen", "counted"))
        gates_f, gates_hi, gates_lo, tab_ready = (sem(n) for n in ("gates_f", "gates_hi", "gates_lo", "tab_ready"))
        pick_ready, gathered, xg_copied, xg_turned = (sem(n) for n in ("pick_ready", "gathered", "xg_copied", "xg_turned"))
        xg_hi_set, xg_lo_set = sem("xg_hi_set"), sem("xg_lo_set")
        silu_done, gated_done, ht_turned, ht_hi, ht_lo = (sem(n) for n in ("silu_done", "gated_done", "ht_turned", "ht_hi", "ht_lo"))
        slots_turned, pickT_set, gate_col_set = sem("slots_turned"), sem("pickT_set"), sem("gate_col_set")
        y_hi_set, y_lo_set, scattered, h_added = (sem(n) for n in ("y_hi_set", "y_lo_set", "scattered", "h_added"))
        counters_set, out_ready, down_lower = sem("counters_set"), sem("out_ready"), sem("down_lower")

        raw_slot = {u: u % RAW_EARLY for u in range(TRUNK_UNITS)}
        trunk_in_slot = [sum(1 for u in raw_slot if raw_slot[u] == s) for s in range(RING)]
        last_trunk_in_slot = [max(u for u in raw_slot if raw_slot[u] == s) for s in range(RAW_EARLY)]

        def raw_at(s):
            return raw[:, s * UNIT:(s + 1) * UNIT]

        def ring_slot(u):
            return u % RING

        def item_base(i):
            return i * ITEM_UNITS + TRUNK_UNITS

        def step_unit(n):
            return 4 + 6 * (n - 1)

        def wait(e, s, value):
            if not isinstance(value, int) or value > 0:
                e.wait_ge(s, value)

        block = ctx.enter_context(nc.Block())

        @block.sync
        def _(sp):
            sp.dma_start(con[:, :], consts).then_inc(con_in, 16)
            for t in range(TT):
                sp.dma_start(h[:, t, :], x[t * P:(t + 1) * P, :]).then_inc(x_in[t], 16)
            sp.dma_start(par[:, :], channel).then_inc(par_in, 16)
            for u in range(TRUNK_UNITS):
                wait(sp, lo_split, u - RAW_EARLY + 1)
                sp.dma_start(raw_at(raw_slot[u]), trunk[u, :, :]).then_inc(landed[raw_slot[u]], 16)
            for j in (1, 2, 3, 0, 4, 5):
                if j < RAW_EARLY:
                    sp.wait_ge(lo_split, last_trunk_in_slot[j] + 1)
                if j == RAW_EARLY:
                    sp.wait_ge(cv_lo, 4)
                sp.dma_start(raw_at(j), experts[j, :, :]).then_inc(landed[j], 16)
            with sp.Fori(1, STEPS) as r:
                for j in range(RING):
                    sp.wait_ge(lo_split, r * RING + (TRUNK_UNITS + j - RING + 1))
                    sp.dma_start(raw_at(j), experts[r * RING + j, :, :]).then_inc(landed[j], 16)
            sp.wait_ge(tab_ready, 1)
            n_items = sp.value_load(item_tab[0:1, MAX_ITEMS:MAX_ITEMS + 1], min_val=EXPERTS, max_val=MAX_ITEMS - 1)
            with sp.Fori(1, n_items) as i:
                e = sp.value_load(item_tab[0:1, bass.ds(i, 1)], min_val=0, max_val=EXPERTS - 1)
                with sp.Fori(0, STEPS) as r:
                    for j in range(RING):
                        sp.wait_ge(lo_split, item_base(i) + r * RING + (j - RING + 1))
                        sp.dma_start(raw_at(j), experts[e * ITEM_UNITS + r * RING + j, :, :]).then_inc(landed[j], 16)
            sp.wait_ge(lo_split, item_base(n_items))
            sp.dma_start(raw_at(0)[:, 0:D], norm_final.partition_broadcast(P)).then_inc(g_final_in, 16)
            for t in range(TT):
                for c in range(2):
                    cols = slice(c * BLK, (c + 1) * BLK)
                    sp.wait_ge(out_ready, 2 * t + c + 1)
                    sp.dma_start(out[t * P:(t + 1) * P, cols], raw_at(1 + t)[:, cols]).then_inc(out_written, 16)
            sp.wait_ge(out_written, 16 * TT * 2)

        @block.gpsimd
        def _(pool):
            pool.memset(eps[:, :], EPS).then_inc(eps_set, 1)
            pool.memset(ones[:, :], 1.0).then_inc(ones_set, 1)
            pool.wait_ge(wsp_in, 16)
            pool.affine_select(out=wsp_sb, in_=wsp_sb, compare_op=ALU.is_ge, fill=0.0, base=0,
                               pattern=[[0, HEADS], [1, P]], channel_multiplier=-1).then_inc(masked, 1)

        @block.scalar
        def _(act):
            done = [0]

            def split_unit(u):
                act.wait_ge(landed[raw_slot[u]], 16 * (u // RAW_EARLY + 1))
                wait(act, w_used, u - RING + 1)
                act.activation(w_hi[:, ring_slot(u), :], raw_at(raw_slot[u]), ACT.Copy).then_inc(hi_split, 1)

            def split_item(i, units):
                for m in units:
                    act.wait_ge(landed[m % RING], i * (16 * STEPS) + 16 * (trunk_in_slot[m % RING] + m // RING + 1))
                    act.wait_ge(w_used, item_base(i) + (m - RING + 1))
                    act.activation(w_hi[:, ring_slot(TRUNK_UNITS + m), :], raw_at(m % RING), ACT.Copy).then_inc(hi_split, 1)

            def splits(until):
                for u in range(done[0], until):
                    if u < TRUNK_UNITS:
                        split_unit(u)
                    else:
                        split_item(0, [u - TRUNK_UNITS])
                done[0] = max(done[0], until)

            def root(dst, sums_of_squares, count, summed, rooted):
                act.wait_ge(summed, TT)
                act.activation(dst, sums_of_squares, ACT.Sqrt, scale=1.0 / count, bias=eps[:, 0:1]).then_inc(rooted, 1)

            def norm_sums(s):
                for t in range(TT):
                    act.activation(xn_hi[:, t, :], h[:, t, :], ACT.Square, accum_out=sums[:, 0, t:t + 1]).then_inc(norm_sq[s], 1)
                root(sums[:, 2, :], sums[:, 0, :], D, norm_sq[s], norm_root[s])

            def turned_x_hi(s, col, banks):
                for b in banks:
                    act.wait_ge(turned[s], b + 1)
                    for k in (2 * b, 2 * b + 1):
                        last = act.activation(xT_hi_k[:, k, :], bank[b][:, (k % 2) * SEQ:(k % 2 + 1) * SEQ], ACT.Copy,
                                              scale=par[:, col + k:col + k + 1])
                    last.then_inc(xT_hi_set[s], 1)

            def rstd(t):
                return sums[:, 6, t:t + 1]

            act.wait_ge(eps_set, 1)
            act.wait_ge(par_in, 16)
            turned_x_hi(0, C_NORM_MIX_E, range(2))
            splits(1)
            turned_x_hi(0, C_NORM_MIX_E, range(2, 4))
            splits(2)
            for t in range(TT):
                act.wait_ge(x_in[t], 16)
            norm_sums(0)
            act.dma_start(wsp_sb, w_spatial).then_inc(wsp_in, 16)
            act.dma_start(band_sb, bands).then_inc(band_in, 16)
            act.dma_start(wpool_sb, w_pool).then_inc(wpool_in, 16)
            act.dma_start(gv_sb, sgu_norm.partition_broadcast(P)).then_inc(gv_in, 16)
            splits(6)
            act.wait_ge(w_used, 2)
            act.wait_ge(norm_rstd_set[0], 1)
            for t in range(TT):
                act.activation(u_sb[:, t, :], bank[4 + t][:, :], ACT.Gelu_apprx_tanh, scale=rstd(t)).then_inc(gelu_done, 1)
            splits(8)
            act.wait_ge(w_used, 4)
            for t in range(TT):
                act.activation(v_sb[:, t, :], bank[6 + t][:, :], ACT.Gelu_apprx_tanh, scale=rstd(t)).then_inc(gelu_done, 1)
            for t in range(TT):
                act.wait_ge(gelu_done, 3 + t)
                act.activation(gated[:, t, :], v_sb[:, t, :], ACT.Square, accum_out=sums[:, 3, t:t + 1]).then_inc(v_sq, 1)
            root(sums[:, 5, :], sums[:, 3, :], BLK, v_sq, v_root)
            splits(10)
            act.wait_ge(w_used, 6)
            for t in range(TT):
                act.activation(z_sb[:, t, :], bank[t][:, :], ACT.Copy, scale=rstd(t)).then_inc(z_copied, 1)
            act.wait_ge(v_sq, 2)
            for b in range(2):
                act.wait_ge(pooled, b + 1)
                act.activation(mixedT[:, 2 * b:2 * b + 2, :], bank[4 + b][:, :].rearrange("p (g s) -> p g s", g=2),
                               ACT.Copy).then_inc(pool_copied, 1)
            for b in range(2):
                act.wait_ge(pool_mapped, b + 1)
                for g in (2 * b, 2 * b + 1):
                    last = act.activation(xT_hi_k[:, 4 + g, :], bank[6 + b][:, (g % 2) * SEQ:(g % 2 + 1) * SEQ], ACT.Copy,
                                          scale=par[:, C_POOL_SCALE + g:C_POOL_SCALE + g + 1])
                last.then_inc(cat_hi, 1)
            for b in range(2):
                act.wait_ge(a_turned, b + 1)
                act.activation(xT_hi[:, b * BLK:(b + 1) * BLK], bank[b][:, :], ACT.Copy).then_inc(cat_hi, 1)
            splits(14)
            turned_x_hi(1, C_NORM_FFN_E, range(4))
            act.wait_ge(h_mixed, 4)
            norm_sums(1)
            splits(16)
            act.wait_ge(norm_rstd_set[1], 1)
            for n in range(FFN_BLOCKS + 1):
                nf = BLK if n < FFN_BLOCKS - 1 else BLK // 2
                base = U_FFN + 6 * n
                if n < FFN_BLOCKS:
                    act.wait_ge(ffn_first, 2 * n + 1)
                    wait(act, ffn_gated[0], n)
                    act.activation(act_tmp[:, 0, 0:nf], bank[0][:, 0:nf], ACT.Silu, scale=rstd(0)).then_inc(ffn_silu[0], 1)
                if n >= 1:
                    pf = BLK if n - 1 < FFN_BLOCKS - 1 else BLK // 2
                    act.wait_ge(ffn_turned[1], n)
                    act.activation(hT_hi[:, 1, 0:pf], bank[1][:, 0:pf], ACT.Copy).then_inc(ffn_hi[1], 1)
                if n == FFN_BLOCKS:
                    break
                small = n == FFN_BLOCKS - 1
                splits(base + RING)
                g_end = base + (1 if small else 2)
                act.wait_ge(w_used, g_end)
                wait(act, ffn_gated[1], n)
                act.activation(act_tmp[:, 1, 0:nf], bank[1][:, 0:nf], ACT.Silu, scale=rstd(1)).then_inc(ffn_silu[1], 1)
                act.wait_ge(ffn_turned[0], n + 1)
                act.activation(hT_hi[:, 0, 0:nf], bank[0][:, 0:nf], ACT.Copy).then_inc(ffn_hi[0], 1)
                if not small:
                    splits(g_end + RING)
                    splits(base + 4 + RING)
            turned_x_hi(2, C_NORM_MIX_O, range(4))
            act.wait_ge(h_ffn, 4)
            norm_sums(2)
            splits(U_PW1 + RING)
            act.wait_ge(norm_rstd_set[2], 1)

            def diagonals(numbers):
                for q in numbers:
                    c, k = q // PE_TAPS, q % PE_TAPS
                    wait(act, diag_used, q - DIAGS + 1)
                    act.activation(diags[:, q % DIAGS, :], ident, ACT.Copy,
                                   scale=par[:, C_W_DW + c * CONV_K + k:C_W_DW + c * CONV_K + k + 1]).then_inc(diag_set, 1)

            for j in range(2):
                u0 = U_PW1 + 4 * j
                act.wait_ge(w_used, u0 + 2)
                wait(act, vg_turned, 4 * j)
                for t in range(TT):
                    act.activation(gated[:, t, :], bank[4 + t][:, :], ACT.Copy, scale=rstd(t)).then_inc(val_copied, 1)
                splits(u0 + 2 + RING)
                if j == 1:
                    diagonals(range(DIAGS))
                act.wait_ge(w_used, u0 + 4)
                for t in range(TT):
                    act.activation(act_tmp[:, t, :], bank[6 + t][:, :], ACT.Copy, scale=rstd(t)).then_inc(gatec_copied, 1)
                for c in range(4 * j, 4 * j + 4):
                    act.wait_ge(vg_turned, c + 1)
                    wait(act, glu_done, c - 3)
                    act.activation(sig[:, c % 4, :], bank[c % 4][:, SEQ:2 * SEQ], ACT.Sigmoid,
                                   bias=par[:, C_B_PW1 + 8 + c:C_B_PW1 + 9 + c]).then_inc(sig_done, 1)
                if j == 0:
                    splits(u0 + 4 + RING)
            diagonals(range(DIAGS, KT * PE_TAPS))
            act.dma_start(act_tmp[0:1, :, :].rearrange("p t s -> p (t s)"), b_pw2).then_inc(b_pw2_in, 16)
            for q in range(2):
                act.wait_ge(centred, q + 1)
                act.activation(squares[:, 4 * q:4 * q + 4, :], yc[:, 4 * q:4 * q + 4, :], ACT.Square).then_inc(sq_done, 1)
            act.wait_ge(sum_done, 2)
            act.activation(std_sb, bank[5][:, 0:SEQ], ACT.Sqrt, scale=1.0 / D, bias=eps[:, 0:1]).then_inc(var_root, 1)
            for q in range(0, KT, 2):
                act.wait_ge(ln_scaled, q // 2 + 1)
                for c in range(q, q + 2):
                    act.activation(yc[:, c, :], yc[:, c, :], ACT.Silu, bias=par[:, C_LN_B + c:C_LN_B + c + 1],
                                   scale=par[:, C_LN_G + c:C_LN_G + c + 1]).then_inc(swish_done, 1)
                act.wait_ge(swish_done, q + 2)
                act.activation(xT_hi_k[:, q:q + 2, :], yc[:, q:q + 2, :], ACT.Copy).then_inc(cv_hi, 1)
            act.activation(router_hi[:, :], par[:, C_ROUTER:C_ROUTER + KT * EXPERTS], ACT.Copy).then_inc(router_hi_set, 1)
            act.activation(before_r, before, ACT.Copy)
            act.activation(ones_r, ones[:, :], ACT.Copy).then_inc(counters_set, 1)
            splits(TRUNK_UNITS + 2)
            turned_x_hi(3, C_NORM_FFN_O, range(2))
            splits(TRUNK_UNITS + 5)
            turned_x_hi(3, C_NORM_FFN_O, range(2, 4))
            act.wait_ge(h_conv, 4)
            norm_sums(3)
            act.wait_ge(norm_rstd_set[3], 1)
            for t in range(TT):
                act.activation(xn_hi[:, t, :], h[:, t, :], ACT.Copy, scale=rstd(t)).then_inc(xn_hi_set, 1)
            splits(TRUNK_UNITS + RING)
            act.wait_ge(centred_logits, 1)
            act.activation(route[:, 2, :, :], route[:, 1, :, :], ACT.Exp).then_inc(exp_done, 1)

            def turned_hi(i, n):
                act.wait_ge(ht_turned, i * STEPS + (n + 1))
                act.activation(hT_hi[:, 0, :], bank[2][:, :], ACT.Copy).then_inc(ht_hi, 1)

            def silu(i, n, unit_end):
                act.wait_ge(w_used, item_base(i) + unit_end)
                wait(act, gated_done, i * STEPS + n)
                act.activation(act_tmp[:, 0, :], bank[0][:, :], ACT.Silu).then_inc(silu_done, 1)

            def weighted_hi(i, tail=False):
                act.wait_ge(gate_col_set, i + 1)
                for c in range(2):
                    if tail and c == 0:
                        act.wait_ge(down_lower, 1)
                    else:
                        act.wait_ge(w_used, item_base(i + 1))
                    act.activation(y_hi[:, c * BLK:(c + 1) * BLK], bank[3 + c][:, :], ACT.Copy,
                                   scale=gate_col[:, 0:1]).then_inc(y_hi_set, 1)

            def item(i, first):
                if not first:
                    split_item(i, range(0, 1))
                    turned_hi(i - 1, STEPS - 1)
                for c in range(2):
                    act.wait_ge(gathered, 2 * i + (c + 1))
                    act.activation(xg_tok[c], bank[5 + c][:, :], ACT.Copy).then_inc(xg_copied, 1)
                if not first:
                    split_item(i, range(1, 3))
                for b in range(2):
                    act.wait_ge(xg_turned, 2 * i + (b + 1))
                    for k in range(4 * b, 4 * b + 4):
                        last = act.activation(xg_hi[:, k, :], bank[5 + b][:, (k % 4) * P:(k % 4 + 1) * P], ACT.Copy,
                                              scale=par[:, C_NORM_FFN_O + k:C_NORM_FFN_O + k + 1])
                    last.then_inc(xg_hi_set, 1)
                if not first:
                    split_item(i, range(3, 4))
                    weighted_hi(i - 1)
                    split_item(i, range(4, 6))
                else:
                    act.wait_ge(gates_f, 1)
                    act.activation(gate_parts[:, :, :, 0], gate_item[:, :, :], ACT.Copy).then_inc(gates_hi, 1)
                    split_item(i, range(6, 7))
                silu(i, 0, 2)
                split_item(i, range(7 if first else 6, 10))
                silu(i, 1, step_unit(1) + 2)
                turned_hi(i, 0)
                split_item(i, range(10, 15))
                act.wait_ge(slots_turned, i + 1)
                act.activation(pickT[:, :], bank[5][:, P:P + SEQ], ACT.Copy).then_inc(pickT_set, 1)
                with act.Fori(2, STEPS - 1) as n:
                    act.wait_ge(w_used, item_base(i) + n * 6)
                    act.wait_ge(gated_done, i * STEPS + n)
                    act.activation(act_tmp[:, 0, :], bank[0][:, :], ACT.Silu).then_inc(silu_done, 1)
                    act.wait_ge(ht_turned, i * STEPS + n)
                    act.activation(hT_hi[:, 0, :], bank[2][:, :], ACT.Copy).then_inc(ht_hi, 1)
                    for j in range(RING):
                        m = 3 + j
                        s = m % RING
                        act.wait_ge(landed[s], i * (16 * STEPS) + n * 16 + 16 * (trunk_in_slot[s] + m // RING + 1))
                        act.wait_ge(w_used, item_base(i) + n * 6 + (m - RING + 1))
                        act.activation(w_hi[:, ring_slot(TRUNK_UNITS + m), :], raw_at(s), ACT.Copy).then_inc(hi_split, 1)
                silu(i, STEPS - 1, step_unit(STEPS - 1) + 2)
                turned_hi(i, STEPS - 2)
                split_item(i, range(ITEM_UNITS - 3, ITEM_UNITS))

            item(0, True)
            act.wait_ge(tab_ready, 1)
            n_items = act.value_load(item_tab[0:1, MAX_ITEMS:MAX_ITEMS + 1], min_val=EXPERTS, max_val=MAX_ITEMS - 1)
            last_item = act.value_load(item_tab[0:1, MAX_ITEMS + 1:MAX_ITEMS + 2], min_val=EXPERTS - 1, max_val=MAX_ITEMS - 2)
            with act.Fori(1, n_items) as i:
                item(i, False)
            turned_hi(last_item, STEPS - 1)
            weighted_hi(last_item, tail=True)
            for t in range(TT):
                act.wait_ge(h_added, last_item * 4 + (3 + t))
                act.activation(raw_at(1 + t)[:, 0:D], h[:, t, :], ACT.Square, accum_out=sums[:, 0, t:t + 1]).then_inc(norm_sq[4], 1)
                act.wait_ge(norm_sq[4], t + 1)
                act.activation(sums[:, 2, t:t + 1], sums[:, 0, t:t + 1], ACT.Sqrt, scale=1.0 / D, bias=eps[:, 0:1]).then_inc(norm_root[4], 1)

        @block.vector
        def _(dve):
            done = [0]
            steps = [0]

            def link(ins):
                steps[0] += 1
                ins.then_inc(dve_step, 1)
                dve.wait_ge(dve_step, steps[0])

            def split_unit(u):
                dve.wait_ge(hi_split, u + 1)
                s = ring_slot(u)
                dve.tensor_tensor(w_lo[:, s, :], raw_at(raw_slot[u]), w_hi[:, s, :].bitcast(F32), ALU.subtract).then_inc(lo_split, 1)

            def split_item(i, units):
                for m in units:
                    s = ring_slot(TRUNK_UNITS + m)
                    dve.wait_ge(hi_split, item_base(i) + (m + 1))
                    dve.tensor_tensor(w_lo[:, s, :], raw_at(m % RING), w_hi[:, s, :].bitcast(F32), ALU.subtract).then_inc(lo_split, 1)

            def splits(until):
                for u in range(done[0], until):
                    if u < TRUNK_UNITS:
                        split_unit(u)
                    else:
                        split_item(0, [u - TRUNK_UNITS])
                done[0] = max(done[0], until)

            def norm_rstd(s):
                dve.wait_ge(norm_root[s], 1)
                dve.reciprocal(sums[:, 6, :], sums[:, 2, :]).then_inc(norm_rstd_set[s], 1)

            def turned_x_lo(s, col, banks):
                for b in banks:
                    dve.wait_ge(xT_hi_set[s], b + 1)
                    for k in (2 * b, 2 * b + 1):
                        last = dve.scalar_tensor_tensor(out=xT_lo_k[:, k, :], in0=bank[b][:, (k % 2) * SEQ:(k % 2 + 1) * SEQ],
                                                        scalar=par[:, col + k:col + k + 1], in1=xT_hi_k[:, k, :].bitcast(F32),
                                                        op0=ALU.mult, op1=ALU.subtract)
                    last.then_inc(xT_lo_set[s], 1)

            dve.wait_ge(par_in, 16)
            turned_x_lo(0, C_NORM_MIX_E, range(2))
            splits(1)
            turned_x_lo(0, C_NORM_MIX_E, range(2, 4))
            splits(2)
            norm_rstd(0)
            splits(6)
            splits(8)
            dve.wait_ge(v_root, 1)
            link(dve.reciprocal(sums[:, 7, :], sums[:, 5, :]))
            dve.wait_ge(gv_in, 16)
            for t in range(TT):
                dve.scalar_tensor_tensor(out=v_sb[:, t, :], in0=v_sb[:, t, :], scalar=sums[:, 7, t:t + 1], in1=gv_sb,
                                         op0=ALU.mult, op1=ALU.mult).then_inc(v_normed, 1)
            splits(10)
            def spatial_gate(t):
                dve.wait_ge(mixed, t + 1)
                for hd in range(HEADS):
                    cols = slice(hd * HEAD_DIM, (hd + 1) * HEAD_DIM)
                    last = dve.scalar_tensor_tensor(out=u_sb[:, t, cols], in0=bank[2 + t][:, cols],
                                                    scalar=par[:, C_B_SPATIAL + hd:C_B_SPATIAL + hd + 1], in1=u_sb[:, t, cols],
                                                    op0=ALU.add, op1=ALU.mult)
                last.then_inc(a_gated, 1)

            spatial_gate(0)
            for b in range(2):
                dve.wait_ge(cat_hi, b + 1)
                for g in (2 * b, 2 * b + 1):
                    last = dve.scalar_tensor_tensor(out=xT_lo_k[:, 4 + g, :], in0=bank[6 + b][:, (g % 2) * SEQ:(g % 2 + 1) * SEQ],
                                                    scalar=par[:, C_POOL_SCALE + g:C_POOL_SCALE + g + 1],
                                                    in1=xT_hi_k[:, 4 + g, :].bitcast(F32), op0=ALU.mult, op1=ALU.subtract)
                last.then_inc(cat_lo, 1)
            spatial_gate(1)
            for b in range(2):
                dve.wait_ge(cat_hi, 2 + b + 1)
                dve.tensor_tensor(xT_lo[:, b * BLK:(b + 1) * BLK], bank[b][:, :], xT_hi[:, b * BLK:(b + 1) * BLK].bitcast(F32),
                                  ALU.subtract).then_inc(cat_lo, 1)
            splits(12)

            def add_to_h(c, t, b, s):
                dve.tensor_tensor(h[:, t, c * BLK:(c + 1) * BLK], bank[b][:, :], h[:, t, c * BLK:(c + 1) * BLK],
                                  ALU.add).then_inc(s, 1)

            for c in range(2):
                dve.wait_ge(w_used, U_OUT + 2 * c + 2)
                for t in range(TT):
                    add_to_h(c, t, 4 - 2 * c + t, h_mixed)
                if c == 0:
                    turned_x_lo(1, C_NORM_FFN_E, range(2))
                    splits(14)
            turned_x_lo(1, C_NORM_FFN_E, range(2, 4))
            norm_rstd(1)
            splits(16)
            for n in range(FFN_BLOCKS + 1):
                nf = BLK if n < FFN_BLOCKS - 1 else BLK // 2
                base = U_FFN + 6 * n
                if n >= 1:
                    pf = BLK if n - 1 < FFN_BLOCKS - 1 else BLK // 2
                    dve.wait_ge(ffn_hi[1], n)
                    dve.tensor_tensor(hT_lo[:, 1, 0:pf], bank[1][:, 0:pf], hT_hi[:, 1, 0:pf].bitcast(F32), ALU.subtract).then_inc(ffn_lo[1], 1)
                if n == FFN_BLOCKS:
                    break
                small = n == FFN_BLOCKS - 1
                dve.wait_ge(ffn_first, 2 * n + 2)
                dve.wait_ge(ffn_silu[0], n + 1)
                dve.scalar_tensor_tensor(out=gated[:, 0, 0:nf], in0=bank[2][:, 0:nf], scalar=sums[:, 6, 0:1], in1=act_tmp[:, 0, 0:nf],
                                         op0=ALU.mult, op1=ALU.mult).then_inc(ffn_gated[0], 1)
                splits(base + RING)
                dve.wait_ge(ffn_hi[0], n + 1)
                dve.tensor_tensor(hT_lo[:, 0, 0:nf], bank[0][:, 0:nf], hT_hi[:, 0, 0:nf].bitcast(F32), ALU.subtract).then_inc(ffn_lo[0], 1)
                if not small:
                    splits(base + 2 + RING)
                u_end = base + (2 if small else 4)
                dve.wait_ge(w_used, u_end)
                dve.wait_ge(ffn_silu[1], n + 1)
                dve.scalar_tensor_tensor(out=gated[:, 1, 0:nf], in0=bank[3][:, 0:nf], scalar=sums[:, 6, 1:2], in1=act_tmp[:, 1, 0:nf],
                                         op0=ALU.mult, op1=ALU.mult).then_inc(ffn_gated[1], 1)
                if not small:
                    splits(u_end + RING)
            dve.wait_ge(ffn_down0, 1)
            for c in range(2):
                add_to_h(c, 0, 4 + c, h_ffn)
            dve.wait_ge(w_used, U_PW1)
            for c in range(2):
                add_to_h(c, 1, 6 + c, h_ffn)
            turned_x_lo(2, C_NORM_MIX_O, range(4))
            norm_rstd(2)
            link(dve.memset(xc[:, :, 0:CONV_K - 1], 0.0))
            splits(U_PW1 + RING)
            taps = [0]

            def conv(c0):
                for k in range(PE_TAPS, CONV_K):
                    for c in range(c0, c0 + 4):
                        w = par[:, C_W_DW + c * CONV_K + k:C_W_DW + c * CONV_K + k + 1]
                        if k == PE_TAPS:
                            ins = dve.tensor_scalar(yc[:, c, :], xc[:, c, k:k + SEQ], w, par[:, C_B_DW + c:C_B_DW + c + 1],
                                                    ALU.mult, ALU.add)
                        else:
                            dve.wait_ge(conv_step, taps[0] - 3)
                            ins = dve.scalar_tensor_tensor(out=yc[:, c, :], in0=xc[:, c, k:k + SEQ], scalar=w,
                                                           in1=yc[:, c, :], op0=ALU.mult, op1=ALU.add)
                        ins.then_inc(conv_step, 1)
                        taps[0] += 1
                    if c0 > 0 and k == CONV_K - 3:
                        merge(range(4))

            def merge(tiles):
                for c in tiles:
                    dve.wait_ge(diag_used, (c + 1) * PE_TAPS)
                    dve.wait_ge(conv_step, 4 * (CONV_K - PE_TAPS) * (c // 4 + 1))
                    dve.tensor_tensor(yc[:, c, :], bank[(4 + c) % 8][:, 0:SEQ], yc[:, c, :], ALU.add).then_inc(conv_merged, 1)

            splits(U_PW1 + 2 + RING)
            for j in range(2):
                for c in range(4 * j, 4 * j + 4):
                    dve.wait_ge(sig_done, c + 1)
                    dve.scalar_tensor_tensor(out=xc[:, c, CONV_K - 1:CONV_K - 1 + SEQ], in0=bank[c % 4][:, 0:SEQ],
                                             scalar=par[:, C_B_PW1 + c:C_B_PW1 + c + 1], in1=sig[:, c % 4, :],
                                             op0=ALU.add, op1=ALU.mult).then_inc(glu_done, 1)
                if j == 0:
                    splits(U_PW1 + 4 + RING)
                dve.wait_ge(glu_done, 4 * j + 4)
                conv(4 * j)
            merge(range(4, KT))
            dve.wait_ge(sum_done, 1)
            link(dve.tensor_scalar(mean_sb, bank[4][:, 0:SEQ], 1.0 / D, None, ALU.mult))
            dve.wait_ge(conv_merged, KT)
            for q in range(2):
                dve.tensor_tensor(yc[:, 4 * q:4 * q + 4, :], yc[:, 4 * q:4 * q + 4, :],
                                  mean_sb.unsqueeze(1).broadcast_to([P, 4, SEQ]), ALU.subtract).then_inc(centred, 1)
            for q in range(2):
                dve.wait_ge(sq_done, q + 1)
                dve.tensor_tensor(squares[:, 4 * q:4 * q + 2, :], squares[:, 4 * q:4 * q + 2, :], squares[:, 4 * q + 2:4 * q + 4, :],
                                  ALU.add).then_inc(sq_added, 1)
            splits(TRUNK_UNITS - 1)
            dve.wait_ge(var_root, 1)
            link(dve.reciprocal(mean_sb, std_sb))
            for c in range(0, KT, 2):
                dve.tensor_tensor(yc[:, c:c + 2, :], yc[:, c:c + 2, :], mean_sb.unsqueeze(1).broadcast_to([P, 2, SEQ]),
                                  ALU.mult).then_inc(ln_scaled, 1)
            for c in range(0, KT, 2):
                dve.wait_ge(cv_hi, c // 2 + 1)
                dve.tensor_tensor(xT_lo_k[:, c:c + 2, :], yc[:, c:c + 2, :], xT_hi_k[:, c:c + 2, :].bitcast(F32),
                                  ALU.subtract).then_inc(cv_lo, 1)
            splits(TRUNK_UNITS)
            dve.wait_ge(router_hi_set, 1)
            dve.tensor_tensor(router_lo[:, :], par[:, C_ROUTER:C_ROUTER + KT * EXPERTS], router_hi[:, :].bitcast(F32),
                              ALU.subtract).then_inc(router_lo_set, 1)
            dve.wait_ge(h_ffn, 4)
            for c in range(2):
                dve.wait_ge(w_used, U_PW2 + 2 * c + 2)
                for t in range(TT):
                    add_to_h(c, t, (6, 7, 2, 3)[2 * c + t], h_conv)
                splits(TRUNK_UNITS + 2 * (c + 1))
                turned_x_lo(3, C_NORM_FFN_O, range(2 * c, 2 * c + 2))
                if c == 0:
                    splits(TRUNK_UNITS + 3)
            norm_rstd(3)
            dve.wait_ge(norm_rstd_set[3], 1)
            splits(TRUNK_UNITS + 5)

            def xn_rest(t):
                dve.wait_ge(xn_hi_set, t + 1)
                dve.scalar_tensor_tensor(out=xn_lo[:, t, :], in0=h[:, t, :], scalar=sums[:, 6, t:t + 1], in1=xn_hi[:, t, :].bitcast(F32),
                                         op0=ALU.mult, op1=ALU.subtract).then_inc(xn_lo_set, 1)

            dve.wait_ge(logits_done, 1)
            for t in range(TT):
                last = dve.tensor_scalar(logits[:, t, :], bank[6 - 2 * t][:, t * EXPERTS:(t + 1) * EXPERTS], sums[:, 6, t:t + 1], None, ALU.mult)
            link(last)
            other = logits.unsqueeze(2).broadcast_to([P, TT, EXPERTS, EXPERTS])
            own = logits.unsqueeze(3).broadcast_to([P, TT, EXPERTS, EXPERTS])
            dve.tensor_tensor(ahead[:, :, :, 0:EXPERTS], other, own, ALU.is_gt)
            link(dve.tensor_tensor(ahead[:, :, :, EXPERTS:], other, own, ALU.is_equal))
            link(dve.tensor_tensor(ahead[:, :, :, EXPERTS:], ahead[:, :, :, EXPERTS:],
                                   tie.unsqueeze(1).broadcast_to([P, TT, EXPERTS, EXPERTS]), ALU.mult))
            dve.tensor_reduce(sums[:, 3, :], logits[:, :, :], AX.X, ALU.max)
            link(dve.tensor_reduce(route[:, 0, :, :], ahead, AX.X, ALU.add))
            sel = sel_r.bitcast(F32)
            dve.tensor_scalar(sel_r, route[:, 0, :, :], 2.0, None, ALU.is_lt).then_inc(chosen, 1)
            dve.tensor_tensor(route[:, 1, :, :], logits[:, :, :], sums[:, 3, :].unsqueeze(2).broadcast_to([P, TT, EXPERTS]),
                              ALU.subtract).then_inc(centred_logits, 1)
            xn_rest(0)
            place = pos_item[:, 0:EXPERTS, :].rearrange("p e t -> p t e")
            over = route[:, 7, 0, :]
            dve.wait_ge(chosen, 1)
            dve.wait_ge(counted, 1)
            dve.tensor_scalar(over, bank[5][:, TT * EXPERTS:(TT + 1) * EXPERTS], float(P), None, ALU.is_gt)
            link(dve.scalar_tensor_tensor(out=place, in0=bank[5][:, 0:TT * EXPERTS].rearrange("p (t e) -> p t e", t=TT),
                                          scalar=float(SLOT_BASE), in1=sel, op0=ALU.add, op1=ALU.mult))

            def build_pick(i, where):
                for t in range(TT):
                    last = dve.tensor_scalar(pick[:, t, :], slots, where[:, t:t + 1], None, ALU.is_equal)
                last.then_inc(pick_ready, 1)

            build_pick(0, pos_item[:, 0, :])
            xn_rest(1)

            def tables():
                up_to, before_over = route[:, 0, 1, :], route[:, 7, 1, :]
                all_of_them = [P, OVERFLOWS, EXPERTS]
                link(dve.tensor_tensor_scan(up_to, ones[:, 0:EXPERTS], over, 0.0, ALU.mult, ALU.add))
                link(dve.tensor_tensor(before_over, up_to, over, ALU.subtract))
                link(dve.tensor_tensor(taken, before_over.unsqueeze(1).broadcast_to(all_of_them),
                                       expert_no[:, 0:OVERFLOWS].unsqueeze(2).broadcast_to(all_of_them), ALU.is_equal))
                link(dve.tensor_tensor(taken, taken, over.unsqueeze(1).broadcast_to(all_of_them), ALU.mult))
                dve.tensor_tensor(taken_no, taken, expert_no.unsqueeze(1).broadcast_to(all_of_them), ALU.mult)
                by_tile = [P, OVERFLOWS, TT, EXPERTS]
                dve.tensor_tensor(taken_place, taken.unsqueeze(2).broadcast_to(by_tile), place.unsqueeze(1).broadcast_to(by_tile), ALU.mult)
                dve.memset(pos_item[:, EXPERTS:, :], 0.0)
                dve.memset(gate_item[:, EXPERTS:, :], 0.0)
                dve.tensor_copy(item_f[:, 0:EXPERTS], expert_no)
                link(dve.memset(item_f[:, EXPERTS:], 0.0))
                for q in range(2):
                    dve.tensor_scalar(item_f[:, MAX_ITEMS + q:MAX_ITEMS + q + 1], up_to[:, EXPERTS - 1:EXPERTS],
                                      float(EXPERTS - q), None, ALU.add)
                dve.tensor_reduce(item_f[:, EXPERTS:EXPERTS + OVERFLOWS], taken_no, AX.X, ALU.add)
                link(dve.tensor_reduce(pos_item[:, EXPERTS:EXPERTS + OVERFLOWS, :], taken_place, AX.X, ALU.add))
                dve.tensor_copy(item_tab[:, :], item_f[0:1, :]).then_inc(tab_ready, 1)
                link(dve.tensor_scalar(pos_item[:, EXPERTS:, :], pos_item[:, EXPERTS:, :], -float(P), None, ALU.add))

            def token_gates():
                by_tile = [P, OVERFLOWS, TT, EXPERTS]
                gates = gate_item[:, 0:EXPERTS, :].rearrange("p e t -> p t e")
                dve.wait_ge(exp_done, 1)
                link(dve.tensor_tensor(route[:, 4, :, :], route[:, 2, :, :], sel, ALU.mult))
                link(dve.tensor_reduce(sums[:, 4, :], route[:, 4, :, :], AX.X, ALU.add))
                link(dve.reciprocal(sums[:, 5, :], sums[:, 4, :]))
                link(dve.tensor_tensor(gates, route[:, 4, :, :], sums[:, 5, :].unsqueeze(2).broadcast_to([P, TT, EXPERTS]), ALU.mult))
                link(dve.tensor_tensor(taken_gate, taken.unsqueeze(2).broadcast_to(by_tile), gates.unsqueeze(1).broadcast_to(by_tile), ALU.mult))
                dve.tensor_reduce(gate_item[:, EXPERTS:EXPERTS + OVERFLOWS, :], taken_gate, AX.X, ALU.add).then_inc(gates_f, 1)

            splits(TRUNK_UNITS + RING)
            tables()

            def turned_lo(i, n):
                dve.wait_ge(ht_hi, i * STEPS + (n + 1))
                dve.tensor_tensor(hT_lo[:, 0, :], bank[2][:, :], hT_hi[:, 0, :].bitcast(F32), ALU.subtract).then_inc(ht_lo, 1)

            def gate_up(i, n, unit_end):
                dve.wait_ge(w_used, item_base(i) + unit_end)
                dve.wait_ge(silu_done, i * STEPS + (n + 1))
                dve.tensor_tensor(gated[:, 0, :], bank[1][:, :], act_tmp[:, 0, :], ALU.mult).then_inc(gated_done, 1)

            def weighted_lo(i):
                for c in range(2):
                    dve.wait_ge(y_hi_set, 2 * i + (c + 1))
                    dve.scalar_tensor_tensor(out=y_lo[:, c * BLK:(c + 1) * BLK], in0=bank[3 + c][:, :], scalar=gate_col[:, 0:1],
                                             in1=y_hi[:, c * BLK:(c + 1) * BLK].bitcast(F32), op0=ALU.mult, op1=ALU.subtract).then_inc(y_lo_set, 1)

            def add_item(i):
                wait(dve, h_added, 4 * i)
                for q in range(4):
                    dve.wait_ge(scattered, 4 * i + (q + 1))
                    add_to_h(q // 2, q % 2, (5, 6, 7, 2)[q], h_added)

            def item(i, first):
                if not first:
                    split_item(i, range(0, 1))
                    turned_lo(i - 1, STEPS - 1)
                    split_item(i, range(1, 3))
                for b in range(2):
                    dve.wait_ge(xg_hi_set, 2 * i + (b + 1))
                    for k in range(4 * b, 4 * b + 4):
                        last = dve.scalar_tensor_tensor(out=xg_lo[:, k, :], in0=bank[5 + b][:, (k % 4) * P:(k % 4 + 1) * P],
                                                        scalar=par[:, C_NORM_FFN_O + k:C_NORM_FFN_O + k + 1],
                                                        in1=xg_hi[:, k, :].bitcast(F32), op0=ALU.mult, op1=ALU.subtract)
                    last.then_inc(xg_lo_set, 1)
                if not first:
                    split_item(i, range(3, 4))
                    weighted_lo(i - 1)
                    split_item(i, range(4, 6))
                else:
                    token_gates()
                split_item(i, range(6, 8))
                if not first:
                    add_item(i - 1)
                gate_up(i, 0, 4)
                split_item(i, range(8, 10))
                if first:
                    dve.wait_ge(gates_hi, 1)
                    dve.tensor_tensor(gate_parts[:, :, :, 1], gate_item[:, :, :], gate_parts[:, :, :, 0].bitcast(F32),
                                      ALU.subtract).then_inc(gates_lo, 1)
                turned_lo(i, 0)
                split_item(i, range(10, 12))
                gate_up(i, 1, step_unit(1) + 4)
                split_item(i, range(12, 15))
                dve.wait_ge(pickT_set, i + 1)
                dve.tensor_reduce(gate_col[:, :], bank[5][:, 0:2], AX.X, ALU.add).then_inc(gate_col_set, 1)
                build_pick(i + 1, pos_item[:, 1, :] if first else pos_item[:, bass.ds(i + 1, 1), :].rearrange("p o t -> p (o t)"))
                with dve.Fori(2, STEPS - 1) as n:
                    dve.wait_ge(ht_hi, i * STEPS + n)
                    dve.tensor_tensor(hT_lo[:, 0, :], bank[2][:, :], hT_hi[:, 0, :].bitcast(F32), ALU.subtract).then_inc(ht_lo, 1)
                    for j in range(RING):
                        if j == 3:
                            dve.wait_ge(w_used, item_base(i) + n * 6 + 2)
                            dve.wait_ge(silu_done, i * STEPS + n + 1)
                            dve.tensor_tensor(gated[:, 0, :], bank[1][:, :], act_tmp[:, 0, :], ALU.mult).then_inc(gated_done, 1)
                        m = 3 + j
                        s = ring_slot(TRUNK_UNITS + m)
                        dve.wait_ge(hi_split, item_base(i) + n * 6 + (m + 1))
                        dve.tensor_tensor(w_lo[:, s, :], raw_at(m % RING), w_hi[:, s, :].bitcast(F32), ALU.subtract).then_inc(lo_split, 1)
                turned_lo(i, STEPS - 2)
                split_item(i, range(ITEM_UNITS - 3, ITEM_UNITS - 1))
                gate_up(i, STEPS - 1, step_unit(STEPS - 1) + 4)
                split_item(i, range(ITEM_UNITS - 1, ITEM_UNITS))

            item(0, True)
            dve.wait_ge(tab_ready, 1)
            n_items = dve.value_load(item_tab[0:1, MAX_ITEMS:MAX_ITEMS + 1], min_val=EXPERTS, max_val=MAX_ITEMS - 1)
            last_item = dve.value_load(item_tab[0:1, MAX_ITEMS + 1:MAX_ITEMS + 2], min_val=EXPERTS - 1, max_val=MAX_ITEMS - 2)
            with dve.Fori(1, n_items) as i:
                item(i, False)
            turned_lo(last_item, STEPS - 1)
            weighted_lo(last_item)
            add_item(last_item)
            dve.wait_ge(g_final_in, 16)
            for t in range(TT):
                dve.wait_ge(norm_root[4], t + 1)
                link(dve.reciprocal(sums[:, 6, t:t + 1], sums[:, 2, t:t + 1]))
                for c in range(2):
                    cols = slice(c * BLK, (c + 1) * BLK)
                    dve.scalar_tensor_tensor(out=raw_at(1 + t)[:, cols], in0=h[:, t, cols], scalar=sums[:, 6, t:t + 1],
                                             in1=raw_at(0)[:, cols], op0=ALU.mult, op1=ALU.mult).then_inc(out_ready, 1)

        @block.tensor
        def _(pe):
            def product(dst, a_hi, a_lo, b_hi, b_lo, first, last):
                pe.matmul(dst, a_hi, b_hi, start=first, stop=False)
                pe.matmul(dst, a_hi, b_lo, start=False, stop=False)
                return pe.matmul(dst, a_lo, b_hi, start=False, stop=last)

            def weights(slot, kts, cols):
                return (w_hi[:, slot, :].rearrange("p (k c) -> p k c", k=kts)[:, :, 0:cols],
                        w_lo[:, slot, :].rearrange("p (k c) -> p k c", k=kts)[:, :, 0:cols])

            def by_parts(kt0, tiles, dsts, b_hi, b_lo, start, stop, ready):
                for j, (kind, ks, wait_for) in enumerate(ready):
                    wait_for()
                    for t, dst in zip(tiles, dsts):
                        toks = slice(t * P, (t + 1) * P)
                        for k in ks:
                            a = xT_lo_k if kind == "rest * upper" else xT_hi_k
                            b = b_lo if kind == "upper * rest" else b_hi
                            last = pe.matmul(dst[:, 0:b.shape[2]], a[:, kt0 + k, toks], b[:, k, :], start=start and j == 0 and k == ks[0],
                                             stop=stop and j == len(ready) - 1 and k == ks[-1])
                return last

            def columns(units, t, dst, nf=BLK, between=None, second=None):
                per = KT // len(units)
                for q, u in enumerate(units):
                    if q == 1 and between:
                        between()
                    pe.wait_ge(lo_split, u + 1)
                    b_hi, b_lo = weights(ring_slot(u), per, nf)
                    if q == 1 and second:
                        last = by_parts(q * per, [t], [dst[:, 0:nf]], b_hi, b_lo, False, True, second)
                        continue
                    for k in range(per):
                        kt = q * per + k
                        toks = slice(t * P, (t + 1) * P)
                        last = product(dst[:, 0:nf], xT_hi_k[:, kt, toks], xT_lo_k[:, kt, toks], b_hi[:, k, :], b_lo[:, k, :],
                                       kt == 0, kt == KT - 1)
                    if t == TT - 1:
                        last.then_inc(w_used, 1)
                return last

            def pair(units, dsts, nf=BLK, between=None, biased=False, first=None):
                per = KT // len(units)
                for q, u in enumerate(units):
                    if q == 1 and between:
                        between()
                    b_hi, b_lo = weights(ring_slot(u), per, nf)
                    if q == 0 and first:
                        by_parts(0, range(TT), [d[:, 0:nf] for d in dsts], b_hi, b_lo, not biased, False, first).then_inc(w_used, 1)
                        continue
                    pe.wait_ge(lo_split, u + 1)
                    for t in range(TT):
                        toks = slice(t * P, (t + 1) * P)
                        for k in range(per):
                            kt = q * per + k
                            last = product(dsts[t][:, 0:nf], xT_hi_k[:, kt, toks], xT_lo_k[:, kt, toks], b_hi[:, k, :],
                                           b_lo[:, k, :], kt == 0 and not biased, kt == KT - 1)
                    last.then_inc(w_used, 1)

            def turn_h(s, kts, toks=range(TT)):
                for k in kts:
                    for t in toks:
                        last = pe.transpose(bank[k // 2][:, (k % 2) * SEQ + t * P:(k % 2) * SEQ + (t + 1) * P],
                                            h[:, t, k * P:(k + 1) * P], ident)
                    if k % 2 == 1 and TT - 1 in toks:
                        last.then_inc(turned[s], 1)

            def turn_rest(s, h_ready):
                pe.wait_ge(h_ready, 4)
                turn_h(s, range(4, 8))

            def waits(*pairs):
                def run():
                    for semaphore, value in pairs:
                        pe.wait_ge(semaphore, value)
                return run

            pe.wait_ge(con_in, 16)
            pe.wait_ge(x_in[0], 16)
            turn_h(0, range(KT), [0])
            pe.wait_ge(x_in[1], 16)
            turn_h(0, range(KT), [1])
            pair([0, 1], bank[4:6], between=waits((xT_lo_set[0], 4)),
                 first=[("upper * upper", range(4), waits((xT_hi_set[0], 2), (hi_split, 1))), ("rest * upper", range(4), waits((xT_lo_set[0], 2))),
                        ("upper * rest", range(4), waits((lo_split, 1)))])
            pair([2, 3], bank[6:8])
            pair([4, 5], bank[0:2])
            def spatial(t):
                pe.wait_ge(v_normed, t + 1)
                for hd in range(HEADS):
                    cols = slice(hd * HEAD_DIM, (hd + 1) * HEAD_DIM)
                    last = pe.matmul(bank[2 + t][:, cols], wsp_sb[:, hd, :], v_sb[:, t, cols], start=True, stop=True)
                last.then_inc(mixed, 1)

            pe.wait_ge(masked, 1)
            spatial(0)
            pe.wait_ge(z_copied, 2)
            pe.wait_ge(gelu_done, 4)
            pe.wait_ge(band_in, 16)
            for g in range(GROUPS):
                chans = slice(g * P, (g + 1) * P)
                o = bank[4 + g // 2][:, (g % 2) * SEQ:(g % 2 + 1) * SEQ]
                pe.matmul(o[:, 0:P], z_sb[:, 0, chans], band_sb[:, g, 0:P], start=True, stop=True)
                pe.matmul(o[:, P:SEQ], z_sb[:, 0, chans], band_sb[:, g, P:2 * P], start=True, stop=False)
                last = pe.matmul(o[:, P:SEQ], z_sb[:, 1, chans], band_sb[:, g, 2 * P:3 * P], start=False, stop=True)
                if g % 2 == 1:
                    last.then_inc(pooled, 1)
            spatial(1)
            pe.wait_ge(wpool_in, 16)
            for g in range(GROUPS):
                pe.wait_ge(pool_copied, g // 2 + 1)
                last = pe.matmul(bank[6 + g // 2][:, (g % 2) * SEQ:(g % 2 + 1) * SEQ], wpool_sb[:, g, :], mixedT[:, g, :],
                                 start=True, stop=True)
                if g % 2 == 1:
                    last.then_inc(pool_mapped, 1)
            def turn_gated():
                pe.wait_ge(a_gated, 2)
                for b in range(4):
                    for t in range(TT):
                        last = pe.transpose(bank[b // 2][:, (b % 2) * SEQ + t * P:(b % 2) * SEQ + (t + 1) * P],
                                            u_sb[:, t, b * P:(b + 1) * P], ident)
                    if b % 2 == 1:
                        last.then_inc(a_turned, 1)

            b_hi, b_lo = weights(ring_slot(U_OUT), 4, BLK)
            by_parts(4, [0], bank[4:5], b_hi, b_lo, True, False,
                     [("upper * upper", range(4), waits((cat_hi, 2), (lo_split, U_OUT + 1))), ("upper * rest", range(4), waits()),
                      ("rest * upper", range(4), waits((cat_lo, 2)))])
            turn_gated()
            by_parts(4, [1], bank[5:6], b_hi, b_lo, True, False,
                     [("upper * upper", range(4), waits()), ("upper * rest", range(4), waits()),
                      ("rest * upper", range(4), waits())]).then_inc(w_used, 1)
            b_hi, b_lo = weights(ring_slot(U_OUT + 1), 4, BLK)
            by_parts(0, range(TT), bank[4:6], b_hi, b_lo, False, True,
                     [("upper * upper", range(4), waits((cat_hi, 4), (lo_split, U_OUT + 2))), ("upper * rest", range(4), waits()),
                      ("rest * upper", range(4), waits((cat_lo, 4)))]).then_inc(w_used, 1)

            def turn_first(s, h_ready):
                pe.wait_ge(h_ready, 2)
                turn_h(s, range(4))

            pair([8, 9], bank[2:4], between=lambda: turn_first(1, h_mixed))
            pe.wait_ge(xT_lo_set[1], 2)

            def turn_hidden(n, t, nf):
                pe.wait_ge(ffn_gated[t], n + 1)
                for f in range(nf // P):
                    last = pe.transpose(bank[t][:, f * P:(f + 1) * P], gated[:, t, f * P:(f + 1) * P], ident)
                last.then_inc(ffn_turned[t], 1)

            def down(n, t, units):
                pe.wait_ge(ffn_lo[t], n + 1)
                for q, u in enumerate(units):
                    pe.wait_ge(lo_split, u + 1)
                    b_hi, b_lo = weights(ring_slot(u), 2, D)
                    for f in range(2):
                        ft = slice((2 * q + f) * P, (2 * q + f + 1) * P)
                        for c in range(2):
                            cols = slice(c * BLK, (c + 1) * BLK)
                            last = product(bank[4 + 2 * t + c][:, :], hT_hi[:, t, ft], hT_lo[:, t, ft], b_hi[:, f, cols], b_lo[:, f, cols],
                                           n == 0 and q == 0 and f == 0, n == FFN_BLOCKS - 1 and f == 1)
                    if t == TT - 1:
                        last.then_inc(w_used, 1)
                if t == 0 and n == FFN_BLOCKS - 1:
                    last.then_inc(ffn_down0, 1)

            def ffn_units(n):
                base = U_FFN + 6 * n
                if n < FFN_BLOCKS - 1:
                    return BLK, [base, base + 1], [base + 2, base + 3], [base + 4, base + 5]
                return BLK // 2, [base], [base + 1], [base + 2]

            for n in range(FFN_BLOCKS):
                nf, gate_u, up_u, down_u = ffn_units(n)
                columns(gate_u, 0, bank[0], nf, between=(lambda: turn_rest(1, h_mixed)) if n == 0 else None,
                        second=[("upper * upper", range(2), waits((xT_hi_set[1], 3))), ("upper * rest", range(2), waits()),
                                ("upper * upper", range(2, 4), waits((xT_hi_set[1], 4))), ("upper * rest", range(2, 4), waits()),
                                ("rest * upper", range(4), waits((xT_lo_set[1], 4)))] if n == 0 else None).then_inc(ffn_first, 1)
                if n >= 1:
                    pf, _, _, last_down = ffn_units(n - 1)
                    turn_hidden(n - 1, 1, pf)
                columns(up_u, 0, bank[2], nf).then_inc(ffn_first, 1)
                if n >= 1:
                    down(n - 1, 1, last_down)
                columns(gate_u, 1, bank[1], nf)
                turn_hidden(n, 0, nf)
                columns(up_u, 1, bank[3], nf)
                down(n, 0, down_u)
            nf, _, _, down_u = ffn_units(FFN_BLOCKS - 1)
            turn_hidden(FFN_BLOCKS - 1, 1, nf)
            b_hi, b_lo = weights(ring_slot(down_u[0]), 2, D)
            pe.wait_ge(ffn_hi[1], FFN_BLOCKS)
            for a, bs in ((hT_hi, (b_hi, b_lo)), (hT_lo, (b_hi,))):
                if a is hT_lo:
                    pe.wait_ge(ffn_lo[1], FFN_BLOCKS)
                for f in range(2):
                    for c in range(2):
                        for b in bs:
                            last = pe.matmul(bank[6 + c][:, :], a[:, 1, f * P:(f + 1) * P], b[:, f, c * BLK:(c + 1) * BLK],
                                             start=False, stop=a is hT_lo and f == 1)
            last.then_inc(w_used, 1)
            pe.wait_ge(h_ffn, 2)
            turn_h(2, range(KT), [0])
            for k in range(0, KT, 4):
                pe.wait_ge(h_ffn, 3 + k // 4)
                turn_h(2, range(k, k + 4), [1])
            for j in range(2):
                u0 = U_PW1 + 4 * j
                wait(pe, val_copied, 2 * j)
                pair([u0, u0 + 1], bank[4:6], between=waits((xT_lo_set[2], 4)),
                     first=[("upper * upper", range(2), waits((xT_hi_set[2], 1), (lo_split, u0 + 1))), ("upper * rest", range(2), waits()),
                            ("upper * upper", range(2, 4), waits((xT_hi_set[2], 2))), ("upper * rest", range(2, 4), waits()),
                            ("rest * upper", range(4), waits((xT_lo_set[2], 2)))])
                wait(pe, gatec_copied, 2 * j)
                pair([u0 + 2, u0 + 3], bank[6:8])
                pe.wait_ge(val_copied, 2 * j + 2)
                for c in range(4 * j, 4 * j + 4):
                    wait(pe, glu_done, c - 3)
                    for t in range(TT):
                        pe.transpose(bank[c % 4][:, t * P:(t + 1) * P], gated[:, t, (c % 4) * P:(c % 4 + 1) * P], ident)
                pe.wait_ge(gatec_copied, 2 * j + 2)
                for c in range(4 * j, 4 * j + 4):
                    for t in range(TT):
                        last = pe.transpose(bank[c % 4][:, SEQ + t * P:SEQ + (t + 1) * P], act_tmp[:, t, (c % 4) * P:(c % 4 + 1) * P], ident)
                    last.then_inc(vg_turned, 1)
            for c in range(KT):
                pe.wait_ge(glu_done, c + 1 if c < 4 else KT)
                for k in range(PE_TAPS):
                    q = c * PE_TAPS + k
                    pe.wait_ge(diag_set, q + 1)
                    pe.matmul(bank[(4 + c) % 8][:, 0:SEQ], diags[:, q % DIAGS, :], xc[:, c, k:k + SEQ],
                              start=k == 0, stop=k == PE_TAPS - 1).then_inc(diag_used, 1)
            pe.wait_ge(ones_set, 1)
            pe.wait_ge(b_pw2_in, 16)

            def pw2_bias(c):
                for t in range(TT):
                    pe.matmul(bank[(6, 7, 2, 3)[2 * c + t]][:, :], ones[0:1, :], act_flat[0:1, c * BLK:(c + 1) * BLK],
                              start=True, stop=False)

            for c in range(KT):
                pe.wait_ge(conv_merged, c + 1)
                last = pe.matmul(bank[4][:, 0:SEQ], ones[:, :], yc[:, c, :], start=c == 0, stop=c == KT - 1)
            last.then_inc(sum_done, 1)
            pw2_bias(0)
            pw2_bias(1)
            for c in (0, 1, 4, 5):
                pe.wait_ge(sq_added, c // 4 + 1)
                last = pe.matmul(bank[5][:, 0:SEQ], ones[:, :], squares[:, c, :], start=c == 0, stop=c == 5)
            last.then_inc(sum_done, 1)
            pair([U_PW2, U_PW2 + 1], bank[6:8], biased=True, between=waits((cv_lo, 4)),
                 first=[("upper * upper", range(2), waits((cv_hi, 1), (lo_split, U_PW2 + 1))), ("upper * rest", range(2), waits()),
                        ("upper * upper", range(2, 4), waits((cv_hi, 2))), ("upper * rest", range(2, 4), waits()),
                        ("rest * upper", range(4), waits((cv_lo, 2)))])
            pair([U_PW2 + 2, U_PW2 + 3], bank[2:4], biased=True, between=lambda: turn_first(3, h_conv))
            pe.wait_ge(router_lo_set, 1)

            def router(tiles, first, stop):
                for kind in range(3):
                    for k in tiles:
                        if kind == 0:
                            pe.wait_ge(xT_hi_set[3], k // 2 + 1)
                        if kind == 2:
                            pe.wait_ge(xT_lo_set[3], k // 2 + 1)
                        for t in range(TT):
                            a = (xT_lo_k if kind == 2 else xT_hi_k)[:, k, t * P:(t + 1) * P]
                            b = (router_lo if kind == 1 else router_hi)[:, k * EXPERTS:(k + 1) * EXPERTS]
                            last = pe.matmul(bank[6 - 2 * t][:, t * EXPERTS:(t + 1) * EXPERTS], a, b,
                                             start=first and kind == 0 and k == tiles[0], stop=stop and kind == 2 and k == tiles[-1])
                return last

            router(range(4), True, False)
            turn_rest(3, h_conv)
            last = router(range(4, KT), False, True)
            last.then_inc(logits_done, 1)
            pe.wait_ge(chosen, 1)
            pe.wait_ge(counters_set, 1)
            places = bank[5]
            pe.matmul(places[:, 0:EXPERTS], before_r, sel_r[:, 0, :], start=True, stop=True)
            pe.matmul(places[:, EXPERTS:2 * EXPERTS], ones_r, sel_r[:, 0, :], start=True, stop=False)
            pe.matmul(places[:, EXPERTS:2 * EXPERTS], before_r, sel_r[:, 1, :], start=False, stop=True)
            pe.matmul(places[:, 2 * EXPERTS:3 * EXPERTS], ones_r, sel_r[:, 0, :], start=True, stop=False)
            pe.matmul(places[:, 2 * EXPERTS:3 * EXPERTS], ones_r, sel_r[:, 1, :], start=False, stop=True).then_inc(counted, 1)

            def first_gate(i):
                for q in range(2):
                    pe.wait_ge(xg_hi_set, 2 * i + (q + 1))
                    pe.wait_ge(lo_split, item_base(i) + (q + 1))
                    b_hi, b_lo = weights(ring_slot(TRUNK_UNITS + q), 4, BLK)
                    for k in range(4):
                        pe.matmul(bank[0][:, :], xg_hi[:, q * 4 + k, :], b_hi[:, k, :], start=q == 0 and k == 0, stop=False)
                        pe.matmul(bank[0][:, :], xg_hi[:, q * 4 + k, :], b_lo[:, k, :], start=False, stop=False)
                    pe.wait_ge(xg_lo_set, 2 * i + (q + 1))
                    for k in range(4):
                        last = pe.matmul(bank[0][:, :], xg_lo[:, q * 4 + k, :], b_hi[:, k, :], start=False, stop=q == 1 and k == 3)
                    last.then_inc(w_used, 1)

            def item_columns(i, m0, dst):
                for q in range(2):
                    pe.wait_ge(lo_split, item_base(i) + (m0 + q + 1))
                    b_hi, b_lo = weights(ring_slot(TRUNK_UNITS + m0 + q), 4, BLK)
                    for k in range(4):
                        kt = q * 4 + k
                        last = product(dst[:, :], xg_hi[:, kt, :], xg_lo[:, kt, :], b_hi[:, k, :], b_lo[:, k, :], kt == 0, kt == KT - 1)
                    last.then_inc(w_used, 1)

            def item_down(i, m0, first, last_step, between=None):
                for q in range(2):
                    if q == 1 and between:
                        between()
                    pe.wait_ge(lo_split, item_base(i) + (m0 + q + 1))
                    b_hi, b_lo = weights(ring_slot(TRUNK_UNITS + m0 + q), 2, D)
                    for f in range(2):
                        ft = slice((2 * q + f) * P, (2 * q + f + 1) * P)
                        for c in range(2):
                            cols = slice(c * BLK, (c + 1) * BLK)
                            last = product(bank[3 + c][:, :], hT_hi[:, 0, ft], hT_lo[:, 0, ft], b_hi[:, f, cols], b_lo[:, f, cols],
                                           first and q == 0 and f == 0, last_step and q == 1 and f == 1)
                    last.then_inc(w_used, 1)

            def item_turn():
                for f in range(BLK // P):
                    last = pe.transpose(bank[2][:, f * P:(f + 1) * P], gated[:, 0, f * P:(f + 1) * P], ident)
                last.then_inc(ht_turned, 1)

            def scatter(i, tail=False):
                pe.wait_ge(pickT_set, i + 1)
                for q in range(4):
                    c, t = q // 2, q % 2
                    dst = bank[(5, 6, 7, 2)[q]][:, :]
                    cols = slice(c * BLK, (c + 1) * BLK)
                    if tail:
                        pe.wait_ge(y_hi_set, 2 * i + (c + 1))
                    else:
                        pe.wait_ge(y_lo_set, 2 * i + 2)
                    pe.matmul(dst, pickT[:, t * P:(t + 1) * P], y_hi[:, cols], start=True, stop=False)
                    if tail:
                        pe.wait_ge(y_lo_set, 2 * i + (c + 1))
                    pe.matmul(dst, pickT[:, t * P:(t + 1) * P], y_lo[:, cols], start=False, stop=True).then_inc(scattered, 1)

            def gather(i, first=False):
                pe.wait_ge(pick_ready, i + 1)
                for c in range(2):
                    for t in range(TT):
                        if first and c == 0:
                            pe.wait_ge(xn_hi_set, t + 1)
                        pe.matmul(bank[5 + c][:, :], pick[:, t, :], xn_hi[:, t, c * BLK:(c + 1) * BLK], start=t == 0, stop=False)
                        if first and c == 0:
                            pe.wait_ge(xn_lo_set, t + 1)
                        last = pe.matmul(bank[5 + c][:, :], pick[:, t, :], xn_lo[:, t, c * BLK:(c + 1) * BLK], start=False, stop=t == TT - 1)
                    last.then_inc(gathered, 1)

            def turn_gathered(i):
                for c in range(2):
                    pe.wait_ge(xg_copied, 2 * i + (c + 1))
                    for k in range(4):
                        last = pe.transpose(bank[5 + c][:, k * P:(k + 1) * P], xg_tok[c][:, k * P:(k + 1) * P], ident)
                    last.then_inc(xg_turned, 1)

            def item(i, first):
                if first:
                    gather(i, first)
                    turn_gathered(i)
                else:
                    pe.wait_ge(gated_done, i * STEPS)
                    item_turn()
                    gather(i)
                    pe.wait_ge(ht_lo, i * STEPS)
                    item_down(i - 1, ITEM_UNITS - 2, False, True, between=lambda: turn_gathered(i))
                wait(pe, silu_done, i * STEPS)
                first_gate(i)
                if not first:
                    scatter(i - 1)
                wait(pe, gated_done, i * STEPS)
                item_columns(i, 2, bank[1])
                pe.wait_ge(silu_done, i * STEPS + 1)
                item_columns(i, 4, bank[0])
                pe.wait_ge(gated_done, i * STEPS + 1)
                wait(pe, h_added, 4 * i)
                item_turn()
                item_columns(i, 6, bank[1])
                pe.wait_ge(ht_lo, i * STEPS + 1)
                item_down(i, 8, True, False)
                pe.wait_ge(gates_lo, 1)
                for t in range(TT):
                    parts = gate_parts[:, 0, t, :] if first else gate_parts[:, bass.ds(i, 1), t, :].rearrange("p o w -> p (o w)")
                    pe.matmul(bank[5][:, 0:2], pick[:, t, :], parts, start=t == 0, stop=t == TT - 1)
                for t in range(TT):
                    last = pe.transpose(bank[5][:, P + t * P:P + (t + 1) * P], pick[:, t, :].bitcast(F32), ident)
                last.then_inc(slots_turned, 1)
                with pe.Fori(2, STEPS) as n:
                    pe.wait_ge(silu_done, i * STEPS + n)
                    b = item_base(i) + n * 6
                    for q in range(2):
                        pe.wait_ge(lo_split, b + (q - 1))
                        b_hi, b_lo = weights(ring_slot(TRUNK_UNITS + 4 + q), 4, BLK)
                        for k in range(4):
                            kt = q * 4 + k
                            last = product(bank[0][:, :], xg_hi[:, kt, :], xg_lo[:, kt, :], b_hi[:, k, :], b_lo[:, k, :], kt == 0, kt == KT - 1)
                        last.then_inc(w_used, 1)
                    pe.wait_ge(gated_done, i * STEPS + n)
                    item_turn()
                    for q in range(2):
                        pe.wait_ge(lo_split, b + (q + 1))
                        b_hi, b_lo = weights(ring_slot(TRUNK_UNITS + 6 + q), 4, BLK)
                        for k in range(4):
                            kt = q * 4 + k
                            last = product(bank[1][:, :], xg_hi[:, kt, :], xg_lo[:, kt, :], b_hi[:, k, :], b_lo[:, k, :], kt == 0, kt == KT - 1)
                        last.then_inc(w_used, 1)
                    pe.wait_ge(ht_lo, i * STEPS + n)
                    for q in range(2):
                        pe.wait_ge(lo_split, b + (q + 3))
                        b_hi, b_lo = weights(ring_slot(TRUNK_UNITS + 8 + q), 2, D)
                        for f in range(2):
                            ft = slice((2 * q + f) * P, (2 * q + f + 1) * P)
                            for c in range(2):
                                cols = slice(c * BLK, (c + 1) * BLK)
                                last = product(bank[3 + c][:, :], hT_hi[:, 0, ft], hT_lo[:, 0, ft], b_hi[:, f, cols], b_lo[:, f, cols], False, False)
                        last.then_inc(w_used, 1)

            item(0, True)
            pe.wait_ge(tab_ready, 1)
            n_items = pe.value_load(item_tab[0:1, MAX_ITEMS:MAX_ITEMS + 1], min_val=EXPERTS, max_val=MAX_ITEMS - 1)
            last_item = pe.value_load(item_tab[0:1, MAX_ITEMS + 1:MAX_ITEMS + 2], min_val=EXPERTS - 1, max_val=MAX_ITEMS - 2)
            with pe.Fori(1, n_items) as i:
                item(i, False)
            pe.wait_ge(gated_done, n_items * STEPS)
            item_turn()
            pe.wait_ge(ht_hi, n_items * STEPS)
            pe.wait_ge(lo_split, item_base(last_item) + (ITEM_UNITS - 1))
            b_hi, b_lo = weights(ring_slot(TRUNK_UNITS + ITEM_UNITS - 2), 2, D)
            for a, bs in ((hT_hi, (b_hi, b_lo)), (hT_lo, (b_hi,))):
                if a is hT_lo:
                    pe.wait_ge(ht_lo, n_items * STEPS)
                for f in range(2):
                    for c in range(2):
                        for b in bs:
                            last = pe.matmul(bank[3 + c][:, :], a[:, 0, f * P:(f + 1) * P], b[:, f, c * BLK:(c + 1) * BLK],
                                             start=False, stop=False)
            last.then_inc(w_used, 1)
            pe.wait_ge(lo_split, item_base(last_item) + ITEM_UNITS)
            b_hi, b_lo = weights(ring_slot(TRUNK_UNITS + ITEM_UNITS - 1), 2, D)
            for c in range(2):
                for f in range(2):
                    ft = slice((2 + f) * P, (3 + f) * P)
                    cols = slice(c * BLK, (c + 1) * BLK)
                    last = product(bank[3 + c][:, :], hT_hi[:, 0, ft], hT_lo[:, 0, ft], b_hi[:, f, cols], b_lo[:, f, cols], False, f == 1)
                last.then_inc(down_lower if c == 0 else w_used, 1)
            scatter(last_item, tail=True)


def col_units(w, nf, halves):
    f = w.shape[1]
    per = KT // halves
    return (w.reshape(halves, per, P, f // nf, nf).transpose(3, 0, 2, 1, 4).reshape(f // nf, halves, P, UNIT))


def row_units(w):
    return w.reshape(-1, 2, P, D).transpose(0, 2, 1, 3).reshape(-1, P, UNIT)


def constants():
    con = np.zeros((P, K_ALL), np.float32)
    con[:, K_IDENT:K_IDENT + P] = np.eye(P)
    s = np.arange(P)
    con[:, K_BEFORE:K_BEFORE + P] = s[:, None] < s[None, :]
    con[:, K_SLOTS:K_SLOTS + P] = SLOT_BASE + s[None, :]
    e = np.arange(EXPERTS)
    con[:, K_TIE:K_TIE + 64] = (e[None, :] < e[:, None]).reshape(1, 64)
    con[:, K_EXPERT:K_EXPERT + EXPERTS] = e[None, :]
    band = np.zeros((P, GROUPS, 3 * P), np.float32)
    t = np.arange(SEQ)
    for g, win in enumerate(WINDOWS):
        lag = t[None, :] - t[:, None]
        b = np.where((lag >= 0) & (lag < win), np.float32(1) / np.minimum(t + 1, win).astype(np.float32)[None, :], np.float32(0))
        b = b - np.eye(SEQ, dtype=np.float32)
        band[:, g, 0:SEQ] = b[0:P, :]
        band[:, g, SEQ:] = b[P:, P:]
    return con, band


def kernel(**inputs):
    import concourse.bacc as _bacc
    from concourse.bass_utils import run_bass_kernel_spmd as _run

    a = {k: np.asarray(v) for k, v in inputs.items()}
    f32 = np.float32

    trunk = np.empty((TRUNK_UNITS, P, UNIT), f32)
    trunk[U_IN:U_OUT] = col_units(a["w_in_e"][0], BLK, 2).reshape(-1, P, UNIT)
    w_out = col_units(a["w_out_e"][0], BLK, 2)
    trunk[U_OUT:U_FFN] = w_out[0, 1], w_out[0, 0], w_out[1, 0], w_out[1, 1]
    whole = (FFN_BLOCKS - 1) * BLK
    ffn = trunk[U_FFN:U_FFN + 30].reshape(FFN_BLOCKS - 1, 3, 2, P, UNIT)
    ffn[:, 0] = col_units(a["w_gate_d"][0][:, :whole], BLK, 2)
    ffn[:, 1] = col_units(a["w_up_d"][0][:, :whole], BLK, 2)
    ffn[:, 2] = row_units(a["w_down_d"][0][:whole]).reshape(-1, 2, P, UNIT)
    trunk[U_FFN + 30] = col_units(a["w_gate_d"][0][:, whole:], BLK // 2, 1)[0, 0]
    trunk[U_FFN + 31] = col_units(a["w_up_d"][0][:, whole:], BLK // 2, 1)[0, 0]
    trunk[U_FFN + 32] = row_units(a["w_down_d"][0][whole:])[0]
    pw1 = col_units(a["w_pw1"][0], BLK, 2)
    trunk[U_PW1:U_PW2] = pw1[[0, 2, 1, 3]].reshape(-1, P, UNIT)
    trunk[U_PW2:] = col_units(a["w_pw2"][0], BLK, 2).reshape(-1, P, UNIT)

    experts = np.empty((EXPERTS, ITEM_UNITS, P, UNIT), f32)
    for e in range(EXPERTS):
        g = col_units(a["w_gate_x"][0, e], BLK, 2)
        u = col_units(a["w_up_x"][0, e], BLK, 2)
        d = row_units(a["w_down_x"][0, e]).reshape(STEPS, 2, P, UNIT)
        experts[e, 0:2], experts[e, 2:4] = g[0], u[0]
        for n in range(1, STEPS):
            m = 4 + 6 * (n - 1)
            experts[e, m:m + 2], experts[e, m + 2:m + 4], experts[e, m + 4:m + 6] = g[n], u[n], d[n - 1]
        experts[e, ITEM_UNITS - 2:] = d[STEPS - 1]

    def by_channel(v):
        return v.reshape(-1, P).T

    w_dw = a["w_dw"][0].reshape(CONV_K, KT, P).transpose(2, 1, 0).reshape(P, -1)
    router = a["w_router"][0].reshape(KT, P, EXPERTS).transpose(1, 0, 2).reshape(P, -1)
    channel = np.concatenate([by_channel(a["norm_mix_e"][0]), by_channel(a["norm_ffn_e"][0]), by_channel(a["norm_mix_o"][0]),
                              by_channel(a["pool_scale"][0]), by_channel(a["b_dw"][0]), by_channel(a["ln_g"][0]),
                              by_channel(a["ln_b"][0]), by_channel(a["b_pw1"][0]), a["b_spatial"][0].T, w_dw, router,
                              by_channel(a["norm_ffn_o"][0])], axis=1)
    con, band = constants()
    arrays = {
        "x_in_dram": a["x"][0], "trunk_dram": trunk, "experts_dram": experts.reshape(-1, P, UNIT),
        "channel_dram": channel, "consts_dram": con, "bands_dram": band,
        "w_spatial_dram": a["w_spatial"][0].transpose(2, 0, 1), "w_pool_dram": a["w_pool"][0].transpose(1, 0, 2),
        "sgu_norm_dram": a["sgu_norm"][0], "b_pw2_dram": a["b_pw2"],
        "norm_final_dram": a["norm_final"],
    }
    arrays = {k: np.ascontiguousarray(v) for k, v in arrays.items()}
    nc = _bacc.Bacc("TRN2", target_bir_lowering=False, num_devices=1)
    args = [nc.dram_tensor(k, v.shape, F32, kind="ExternalInput").ap() for k, v in arrays.items()]
    args.append(nc.dram_tensor("out_dram", (SEQ, D), F32, kind="ExternalOutput").ap())
    build(nc, *args)
    r = _run(nc, [arrays], core_ids=[0])
    return r.results[0]["out_dram"].reshape(1, SEQ, D)
```
